# Optimizing a Trainium2 kernel written in Bass

```python
import math
import jax
import jax.numpy as jnp
from jax import lax
import numpy as np

D_MODEL = 1024
BATCH = 1
SEQ = 512
DEPTH = 2

GRID_W = 64
CTX_LEN = 256
N_DIRS = 2
NORM_EPS = 1e-6
D_MIX = D_MODEL

DA_HEADS = 4
DA_QK_DIM = 64
DA_V_DIM = 2 * DA_QK_DIM
DA_WIDTH = DA_HEADS * DA_V_DIM
DA_Q_BLOCK = 128
ROPE_BASE = 10000.0
ROPE_FREQS = DA_QK_DIM // 4

GDN_HEADS = 4
GDN_HEAD_DIM = 64
GDN_WIDTH = GDN_HEADS * GDN_HEAD_DIM
GDN_CONV = 5
GDN_CHUNK = 64

RWKV_HEADS = 4
RWKV_HEAD_DIM = 64
RWKV_WIDTH = RWKV_HEADS * RWKV_HEAD_DIM
RWKV_W_LORA = 32
RWKV_A_LORA = 32
RWKV_G_LORA = 64
RWKV_DECAY_SCALE = 0.6065306597126334
RWKV_GN_EPS = 64e-5

N_EXPERTS = 16
EC_CAPACITY_FACTOR = 2
D_EXPERT = 1024

IN_SIZES = (DA_HEADS * 2 * DA_QK_DIM, DA_HEADS * 2 * DA_QK_DIM, DA_WIDTH,
            3 * GDN_WIDTH, GDN_WIDTH, N_DIRS * GDN_HEADS, N_DIRS * GDN_HEADS,
            3 * RWKV_WIDTH, RWKV_W_LORA, RWKV_A_LORA, RWKV_G_LORA)
D_IN = sum(IN_SIZES)

kernel_name = 'hybrid_parallel_heads_diffusion_trunk'

def _rmsnorm(x, g):
    xf = x.astype(jnp.float32)
    y = xf * lax.rsqrt(jnp.mean(xf * xf, axis=-1, keepdims=True) + NORM_EPS)
    return (y * g.astype(jnp.float32)).astype(x.dtype)

def _l2norm(x):
    return x * lax.rsqrt(jnp.sum(x * x, axis=-1, keepdims=True) + 1e-12)

def _flip(t):
    return jnp.flip(t, axis=1)

def _ident(t):
    return t

def _modulation(cond, w, b, dtype):
    m = jnp.dot(cond, w.astype(jnp.float32)) + b.astype(jnp.float32)
    return [t.astype(dtype) for t in jnp.split(m[:, None, :], 6, axis=-1)]

def _modulate(h, shift, scale):
    return h * (1 + scale) + shift

def _split_cols(p):
    out, off = [], 0
    for n in IN_SIZES:
        out.append(p[..., off:off + n])
        off += n
    return out

def _axial_rope_tables(rows):
    row = jnp.repeat(jnp.arange(rows, dtype=jnp.float32), GRID_W)
    col = jnp.tile(jnp.arange(GRID_W, dtype=jnp.float32), rows)
    freqs = ROPE_BASE ** (-jnp.arange(ROPE_FREQS, dtype=jnp.float32) / ROPE_FREQS)
    ang = jnp.stack([row[:, None] * freqs, col[:, None] * freqs], axis=1)
    return jnp.cos(ang), jnp.sin(ang)

def _rope_2d(x, cos, sin):
    shp = x.shape
    xs = x.astype(jnp.float32).reshape(shp[:-1] + (2, 2, ROPE_FREQS))
    x1, x2 = xs[..., 0, :], xs[..., 1, :]
    cb, sb = cos[None, :, None, None], sin[None, :, None, None]
    y = jnp.stack([x1 * cb - x2 * sb, x2 * cb + x1 * sb], axis=-2)
    return y.reshape(shp).astype(x.dtype)

def _da_heads(p):
    B, T, _ = p[0].shape
    q = p[0].reshape(B, T, DA_HEADS, 2, DA_QK_DIM)
    k = p[1].reshape(B, T, DA_HEADS, 2, DA_QK_DIM)
    v = p[2].reshape(B, T, DA_HEADS, DA_V_DIM)
    return q, k, v

def _diff_lambda(lv, lam_init):
    lv = lv.astype(jnp.float32)
    return jnp.exp(jnp.sum(lv[0] * lv[1])) - jnp.exp(jnp.sum(lv[2] * lv[3])) + lam_init

def _diff_attention(q_c, k_c, v_c, q_l, k_l, v_l, cos, sin, lam, lam_init, norm_g, need_ctx):
    dtype = v_l.dtype
    scale = DA_QK_DIM ** -0.5
    q_l = _rope_2d(q_l, cos, sin)
    k_l = _rope_2d(k_l, cos, sin)
    k_all = jnp.concatenate([k_c, k_l], axis=1)
    v_all = jnp.concatenate([v_c, v_l], axis=1).astype(jnp.float32)

    def attend(q, k, v):
        s = jnp.einsum('bqhmd,bkhmd->bhmqk', q, k, preferred_element_type=jnp.float32) * scale
        p = jax.nn.softmax(s, axis=-1)
        w = p[:, :, 0] - lam * p[:, :, 1]
        return jnp.einsum('bhqk,bkhd->bqhd', w, v)

    def finish(o):
        B, T = o.shape[:2]
        return (_rmsnorm(o, norm_g) * (1.0 - lam_init)).reshape(B, T, DA_WIDTH).astype(dtype)

    B, T = q_l.shape[:2]
    n_blk = T // DA_Q_BLOCK
    q_blocks = jnp.swapaxes(q_l.reshape((B, n_blk, DA_Q_BLOCK) + q_l.shape[2:]), 0, 1)
    o_l = lax.map(lambda qb: attend(qb, k_all, v_all), q_blocks)
    o_l = jnp.swapaxes(o_l, 0, 1).reshape(B, T, DA_HEADS, DA_V_DIM)
    o_c = finish(attend(q_c, k_c, v_c.astype(jnp.float32))) if need_ctx else None
    return o_c, finish(o_l)

def _short_conv(x, w):
    pad = GDN_CONV // 2
    y = lax.conv_general_dilated(x, w[:, None, :].astype(x.dtype), window_strides=(1,), padding=[(pad, pad)],
                                 dimension_numbers=('NWC', 'WIO', 'NWC'), feature_group_count=x.shape[-1])
    return jax.nn.silu(y)

def _gdn_prepare(qkv, a_in, b_in, conv_w, a_log, dt_bias):
    B, T, _ = qkv.shape
    qkv = _short_conv(qkv, conv_w).astype(jnp.float32).reshape(B, T, 3, GDN_HEADS, GDN_HEAD_DIM)
    q = _l2norm(qkv[:, :, 0]) * GDN_HEAD_DIM ** -0.5
    k = _l2norm(qkv[:, :, 1])
    v = qkv[:, :, 2]
    a = a_in.astype(jnp.float32).reshape(B, T, N_DIRS, GDN_HEADS)
    g = -jnp.exp(a_log.astype(jnp.float32)) * jax.nn.softplus(a + dt_bias.astype(jnp.float32))
    beta = jax.nn.sigmoid(b_in.astype(jnp.float32).reshape(B, T, N_DIRS, GDN_HEADS))
    return q, k, v, g, beta

def _gdn_chunked(q, k, v, g, beta, s0):
    B, T, H, _ = q.shape
    C = GDN_CHUNK
    n = T // C

    def chunks(t):
        t = t.reshape((B, n, C, H) + t.shape[3:])
        return jnp.moveaxis(t, (1, 3), (0, 2))

    qc, kc, vc, gch, bch = (chunks(t) for t in (q, k, v, g, beta))
    gcum = jnp.cumsum(gch, axis=-1)
    incl = jnp.tril(jnp.ones((C, C), dtype=bool))
    strict = jnp.tril(jnp.ones((C, C), dtype=bool), -1)
    decay = jnp.exp(jnp.where(incl, gcum[..., :, None] - gcum[..., None, :], -jnp.inf))
    kb = kc * bch[..., None]
    a_mat = jnp.where(strict, jnp.einsum('nbhid,nbhjd->nbhij', kb, kc) * decay, 0.0)
    eye = jnp.eye(C, dtype=jnp.float32)
    t_inv = lax.linalg.triangular_solve(eye + a_mat, jnp.broadcast_to(eye, a_mat.shape),
                                        left_side=True, lower=True, unit_diagonal=True)
    u = jnp.einsum('nbhij,nbhjd->nbhid', t_inv, vc * bch[..., None])
    w = jnp.einsum('nbhij,nbhjd->nbhid', t_inv, kb * jnp.exp(gcum)[..., None])
    qk = jnp.einsum('nbhid,nbhjd->nbhij', qc, kc) * decay
    q_dec = qc * jnp.exp(gcum)[..., None]
    k_dec = kc * jnp.exp(gcum[..., -1:] - gcum)[..., None]
    g_tot = jnp.exp(gcum[..., -1])

    def step(s, xs):
        u_i, w_i, qk_i, qd_i, kd_i, gt_i = xs
        v_new = u_i - jnp.einsum('bhid,bhdv->bhiv', w_i, s)
        o_i = jnp.einsum('bhid,bhdv->bhiv', qd_i, s) + jnp.einsum('bhij,bhjv->bhiv', qk_i, v_new)
        s = s * gt_i[..., None, None] + jnp.einsum('bhid,bhiv->bhdv', kd_i, v_new)
        return s, o_i

    s_fin, o = lax.scan(step, s0, (u, w, qk, q_dec, k_dec, g_tot))
    o = jnp.moveaxis(o, (0, 2), (1, 3)).reshape(B, T, H, v.shape[-1])
    return s_fin, o

def _gdn_out(o, gate, norm_g, dtype):
    B, T = o.shape[:2]
    y = _rmsnorm(o, norm_g) * jax.nn.silu(gate.astype(jnp.float32).reshape(B, T, GDN_HEADS, GDN_HEAD_DIM))
    return y.reshape(B, T, GDN_WIDTH).astype(dtype)

def _gdn_mixer(p_c, p_l, conv_w, a_log, dt_bias, norm_g):
    dtype = p_l[3].dtype
    qc, kc, vc, gc, bc = _gdn_prepare(p_c[3], p_c[5], p_c[6], conv_w, a_log, dt_bias)
    ql, kl, vl, gl, bl = _gdn_prepare(p_l[3], p_l[5], p_l[6], conv_w, a_log, dt_bias)
    s0 = jnp.zeros((ql.shape[0], GDN_HEADS, GDN_HEAD_DIM, GDN_HEAD_DIM), jnp.float32)
    o_c, o_l = [], []
    for d in range(N_DIRS):
        f = _flip if d == 1 else _ident
        s_c, oc = _gdn_chunked(f(qc), f(kc), f(vc), f(gc[:, :, d]), f(bc[:, :, d]), s0)
        _, ol = _gdn_chunked(f(ql), f(kl), f(vl), f(gl[:, :, d]), f(bl[:, :, d]), s_c)
        o_c.append(f(oc))
        o_l.append(f(ol))
    return (_gdn_out(o_c[0] + o_c[1], p_c[4], norm_g, dtype),
            _gdn_out(o_l[0] + o_l[1], p_l[4], norm_g, dtype))

def _rwkv_prepare(rkv, xw, xa, xg, w0, w_up, a0, a_up, g_up, k_k, k_a):
    rkv, xw, xa, xg = (t.astype(jnp.float32) for t in (rkv, xw, xa, xg))
    B, T, _ = rkv.shape

    def heads(t):
        return t.reshape(B, T, RWKV_HEADS, RWKV_HEAD_DIM)

    r, k, v = rkv[..., :RWKV_WIDTH], rkv[..., RWKV_WIDTH:2 * RWKV_WIDTH], rkv[..., 2 * RWKV_WIDTH:]
    kk = _l2norm(heads(k * k_k))
    g = jnp.dot(jax.nn.sigmoid(xg), g_up.astype(jnp.float32))
    decay, a, kd = [], [], []
    for d in range(N_DIRS):
        logw = -RWKV_DECAY_SCALE * jax.nn.sigmoid(w0[d] + jnp.dot(jnp.tanh(xw), w_up[d].astype(jnp.float32)))
        a_d = jax.nn.sigmoid(a0[d] + jnp.dot(xa, a_up[d].astype(jnp.float32)))
        decay.append(heads(jnp.exp(logw)))
        a.append(heads(a_d))
        kd.append(heads(k * (1.0 + (a_d - 1.0) * k_a)))
    return heads(r), heads(v), kk, g, decay, a, kd

def _rwkv_scan(r, w, k, v, kk, a, s0):
    def step(s, xs):
        r_t, w_t, k_t, v_t, kk_t, a_t = xs
        read = jnp.einsum('bhk,bhkv->bhv', -kk_t, s)
        s = w_t[..., :, None] * s + (kk_t * a_t)[..., :, None] * read[..., None, :] + k_t[..., :, None] * v_t[..., None, :]
        return s, jnp.einsum('bhk,bhkv->bhv', r_t, s)

    xs = tuple(jnp.moveaxis(t, 1, 0) for t in (r, w, k, v, kk, a))
    s_fin, y = lax.scan(step, s0, xs)
    return s_fin, jnp.moveaxis(y, 0, 1)

def _rwkv_out(y, prep, r_k, gn_w, gn_b, dtype):
    r, v, _, g, _, _, kd = prep
    B, T = y.shape[:2]
    mu = jnp.mean(y, axis=-1, keepdims=True)
    var = jnp.mean(jnp.square(y - mu), axis=-1, keepdims=True)
    yn = ((y - mu) * lax.rsqrt(var + RWKV_GN_EPS)).reshape(B, T, RWKV_WIDTH) * gn_w + gn_b
    bonus = (jnp.sum(r * (kd[0] + kd[1]) * r_k, axis=-1, keepdims=True) * v).reshape(B, T, RWKV_WIDTH)
    return ((yn + bonus) * g).astype(dtype)

def _rwkv_mixer(p_c, p_l, w0, w_up, a0, a_up, g_up, k_k, k_a, r_k, gn_w, gn_b):
    dtype = p_l[7].dtype
    prm = (w0, w_up, a0, a_up, g_up, k_k, k_a)
    c_in = _rwkv_prepare(p_c[7], p_c[8], p_c[9], p_c[10], *prm)
    l_in = _rwkv_prepare(p_l[7], p_l[8], p_l[9], p_l[10], *prm)
    rc, vc, kkc, _, wc, ac, kc = c_in
    rl, vl, kkl, _, wl, al, kl = l_in
    s0 = jnp.zeros((rl.shape[0], RWKV_HEADS, RWKV_HEAD_DIM, RWKV_HEAD_DIM), jnp.float32)
    y_c, y_l = [], []
    for d in range(N_DIRS):
        f = _flip if d == 1 else _ident
        s_c, yc = _rwkv_scan(f(rc), f(wc[d]), f(kc[d]), f(vc), f(kkc), f(ac[d]), s0)
        _, yl = _rwkv_scan(f(rl), f(wl[d]), f(kl[d]), f(vl), f(kkl), f(al[d]), s_c)
        y_c.append(f(yc))
        y_l.append(f(yl))
    return (_rwkv_out(y_c[0] + y_c[1], c_in, r_k, gn_w, gn_b, dtype),
            _rwkv_out(y_l[0] + y_l[1], l_in, r_k, gn_w, gn_b, dtype))

def _expert_choice_moe(h, router, w_gate, w_up, w_down):
    B, T, _ = h.shape
    cap = EC_CAPACITY_FACTOR * T // N_EXPERTS
    logits = jnp.einsum('btd,de->bte', h, router, preferred_element_type=jnp.float32)
    aff = jax.nn.softmax(logits, axis=-1)
    top_aff, top_idx = lax.top_k(jnp.swapaxes(aff, 1, 2), cap)
    b_idx = jnp.arange(B)[:, None, None]
    xe = h[b_idx, top_idx]
    hid = jax.nn.silu(jnp.einsum('becd,edf->becf', xe, w_gate)) * jnp.einsum('becd,edf->becf', xe, w_up)
    ye = jnp.einsum('becf,efd->becd', hid, w_down) * top_aff[..., None].astype(h.dtype)
    return jnp.zeros_like(h).at[b_idx, top_idx].add(ye.astype(h.dtype))

def setup_inputs(seed: int = 0) -> dict:
    key = jax.random.key(seed)
    ks = jax.random.split(key, 32)
    f32 = jnp.float32
    D = D_MODEL

    def nrm(i, shape, s):
        return jax.random.normal(ks[i], shape, f32) * s

    dt = jnp.exp(jax.random.uniform(ks[14], (DEPTH, N_DIRS, GDN_HEADS), f32, math.log(1e-3), math.log(1e-1)))
    return {
        'x': nrm(0, (BATCH, SEQ, D), 1.0),
        'c': nrm(1, (BATCH, D), 1.0),
        'ctx': nrm(2, (BATCH, CTX_LEN, D), 1.0),
        'c_ctx': nrm(3, (D,), 1.0),
        'w_mod': nrm(4, (DEPTH, D, 6 * D), 0.5 * D ** -0.5),
        'b_mod': nrm(5, (DEPTH, 6 * D), 0.02),
        'norm_pre': 1.0 + nrm(6, (DEPTH, 2, D), 0.02),
        'norm_post': 1.0 + nrm(7, (DEPTH, 2, D), 0.02),
        'w_in': nrm(8, (DEPTH, D, D_IN), D ** -0.5),
        'w_out': nrm(9, (DEPTH, D_MIX, D), D_MIX ** -0.5),
        'da_lambda': nrm(10, (DEPTH, 4, DA_QK_DIM), 0.1),
        'da_norm': 1.0 + nrm(11, (DEPTH, DA_V_DIM), 0.02),
        'gdn_conv': nrm(12, (DEPTH, GDN_CONV, 3 * GDN_WIDTH), GDN_CONV ** -0.5),
        'gdn_a_log': jnp.log(jax.random.uniform(ks[13], (DEPTH, N_DIRS, GDN_HEADS), f32, 1.0, 16.0)),
        'gdn_dt_bias': dt + jnp.log(-jnp.expm1(-dt)),
        'gdn_norm': 1.0 + nrm(15, (DEPTH, GDN_HEAD_DIM), 0.02),
        'rwkv_w0': nrm(16, (DEPTH, N_DIRS, RWKV_WIDTH), 1.0),
        'rwkv_w_up': nrm(17, (DEPTH, N_DIRS, RWKV_W_LORA, RWKV_WIDTH), 0.1),
        'rwkv_a0': nrm(18, (DEPTH, N_DIRS, RWKV_WIDTH), 0.5),
        'rwkv_a_up': nrm(19, (DEPTH, N_DIRS, RWKV_A_LORA, RWKV_WIDTH), 0.1),
        'rwkv_g_up': nrm(20, (DEPTH, RWKV_G_LORA, RWKV_WIDTH), RWKV_G_LORA ** -0.5),
        'rwkv_k_k': 0.85 + nrm(21, (DEPTH, RWKV_WIDTH), 0.02),
        'rwkv_k_a': 1.0 + nrm(22, (DEPTH, RWKV_WIDTH), 0.02),
        'rwkv_r_k': nrm(23, (DEPTH, RWKV_HEADS, RWKV_HEAD_DIM), 0.1),
        'rwkv_gn_w': 1.0 + nrm(24, (DEPTH, RWKV_WIDTH), 0.02),
        'rwkv_gn_b': nrm(25, (DEPTH, RWKV_WIDTH), 0.02),
        'moe_router': nrm(26, (DEPTH, D, N_EXPERTS), D ** -0.5),
        'moe_w_gate': nrm(27, (DEPTH, N_EXPERTS, D, D_EXPERT), D ** -0.5),
        'moe_w_up': nrm(28, (DEPTH, N_EXPERTS, D, D_EXPERT), D ** -0.5),
        'moe_w_down': nrm(29, (DEPTH, N_EXPERTS, D_EXPERT, D), D_EXPERT ** -0.5),
    }

def reference(x, c, ctx, c_ctx, w_mod, b_mod, norm_pre, norm_post, w_in, w_out,
              da_lambda, da_norm, gdn_conv, gdn_a_log, gdn_dt_bias, gdn_norm,
              rwkv_w0, rwkv_w_up, rwkv_a0, rwkv_a_up, rwkv_g_up, rwkv_k_k, rwkv_k_a,
              rwkv_r_k, rwkv_gn_w, rwkv_gn_b, moe_router, moe_w_gate, moe_w_up, moe_w_down):
    dtype = x.dtype
    T = x.shape[1]
    ROWS = T // GRID_W
    cos, sin = _axial_rope_tables(ROWS)
    cond_lat = jax.nn.silu(c.astype(jnp.float32))
    cond_ctx = jax.nn.silu(c_ctx.astype(jnp.float32))[None, :]
    x_lat, x_ctx = x, ctx.astype(dtype)
    for i in range(DEPTH):
        last = i == DEPTH - 1
        sh1_l, sc1_l, gt1_l, sh2_l, sc2_l, gt2_l = _modulation(cond_lat, w_mod[i], b_mod[i], dtype)
        sh1_c, sc1_c, gt1_c, sh2_c, sc2_c, gt2_c = _modulation(cond_ctx, w_mod[i], b_mod[i], dtype)

        h_c = _modulate(_rmsnorm(x_ctx, norm_pre[i, 0]), sh1_c, sc1_c)
        h_l = _modulate(_rmsnorm(x_lat, norm_pre[i, 0]), sh1_l, sc1_l)
        p_c = _split_cols(h_c @ w_in[i])
        p_l = _split_cols(h_l @ w_in[i])
        lam_init = 0.8 - 0.6 * math.exp(-0.3 * i)
        lam = _diff_lambda(da_lambda[i], lam_init)
        a_c, a_l = _diff_attention(*_da_heads(p_c), *_da_heads(p_l), cos, sin, lam, lam_init, da_norm[i], not last)
        g_c, g_l = _gdn_mixer(p_c, p_l, gdn_conv[i], gdn_a_log[i], gdn_dt_bias[i], gdn_norm[i])
        r_c, r_l = _rwkv_mixer(p_c, p_l, rwkv_w0[i], rwkv_w_up[i], rwkv_a0[i], rwkv_a_up[i], rwkv_g_up[i],
                               rwkv_k_k[i], rwkv_k_a[i], rwkv_r_k[i], rwkv_gn_w[i], rwkv_gn_b[i])
        mix_l = jnp.concatenate([a_l, g_l, r_l], axis=-1) @ w_out[i]
        x_lat = x_lat + gt1_l * _rmsnorm(mix_l, norm_post[i, 0])
        if not last:
            mix_c = jnp.concatenate([a_c, g_c, r_c], axis=-1) @ w_out[i]
            x_ctx = x_ctx + gt1_c * _rmsnorm(mix_c, norm_post[i, 0])

        h_l = _modulate(_rmsnorm(x_lat, norm_pre[i, 1]), sh2_l, sc2_l)
        y_l = _expert_choice_moe(h_l, moe_router[i], moe_w_gate[i], moe_w_up[i], moe_w_down[i])
        x_lat = x_lat + gt2_l * _rmsnorm(y_l, norm_post[i, 1])
        if not last:
            h_c = _modulate(_rmsnorm(x_ctx, norm_pre[i, 1]), sh2_c, sc2_c)
            y_c = _expert_choice_moe(h_c, moe_router[i], moe_w_gate[i], moe_w_up[i], moe_w_down[i])
            x_ctx = x_ctx + gt2_c * _rmsnorm(y_c, norm_post[i, 1])
    return x_lat


_drawn_inputs = setup_inputs


def setup_inputs(seed=0):
    import zlib

    import numpy as np

    out = dict(_drawn_inputs(seed))
    spreads = {}
    factors = {'da_norm': 12.066,
     'rwkv_k_k': 179.966,
     'rwkv_gn_w': 7.811,
     'gdn_norm': 20.357,
     'rwkv_gn_b': 23.151,
     'rwkv_k_a': 3.117}
    for name, (base, spread) in spreads.items():
        noise = np.random.default_rng([zlib.crc32(name.encode()), seed]).standard_normal(out[name].shape)
        drawn = base * np.exp(spread * noise) if base else spread * noise
        out[name] = jnp.asarray(drawn.astype(out[name].dtype))
    for name, factor in factors.items():
        out[name] = (out[name] * factor).astype(out[name].dtype)
    return out
```

```python
from contextlib import ExitStack, contextmanager

import concourse.bass as bass
from concourse import mybir

F32 = mybir.dt.float32
ALU = mybir.AluOpType
ACT = mybir.ActivationFunctionType
AX = mybir.AxisListType
ds = bass.ds

P = 128
D = 1024
KD = D // P
CT, LT = 2, 4
NT = CT + LT
T = NT * P
EPS = 1e-6
DEPTH = 2
HD = 64
NH = 4
W = NH * HD
FMT = 15
TMS, TMW = 4, 388
V0, GATE0, AB0, RKV0 = 0, 512, 768, 784
NE = 16
SLOT_L, SLOT_C = 64, 32
SLOTS = SLOT_L + SLOT_C
DECAY = 0.6065306597126334
GN_EPS = 64e-5

IDENT, UPS, UPI, LOS, LOI, CUI, CUS, CLI, CLS, ROT = (P * i for i in range(10))
ONES = P * 10
COLS = P * 11
IOTA = COLS + 4
COS = IOTA + 64
SIN = COS + 512
NCONST = SIN + 512
DLO, DUP, OLO, OUP = (NCONST + P * i for i in range(4))
SELW = NCONST + 4 * P
NCONST2 = SELW + 12 * P


class Steps:

    def __init__(self, sem, names, by=1):
        self.sem, self.names, self.by, self.base, self.at = sem, names, by, 0, 0

    def step(self, name):
        assert self.names[self.at % len(self.names)] == name, (name, self.names[self.at % len(self.names)])
        self.at += 1
        return self.by

    def count(self, name, turn=0):
        return turn * (len(self.names) * self.by) + (self.base + (self.names.index(name) + 1) * self.by)

    def close(self, turns=1):
        assert self.at % len(self.names) == 0, (self.names, self.at)
        self.at = 0
        self.owner["count"] = self.base + turns * len(self.names) * self.by


class Chain:

    def __init__(self, sem):
        self.sem, self.n, self.i, self.per = sem, 0, None, 0

    def up(self):
        self.n += 1
        return 1

    def count(self):
        return self.n if self.i is None else self.i * self.per + self.n

    @contextmanager
    def loop(self, eng, count, per):
        start = self.n
        with eng.Fori(0, count) as i:
            self.i, self.per = i, per
            yield i
        assert self.n - start == per, f"counted per pass: {self.n - start}, said {per}"
        self.i, self.n = None, start + count * per


PRIMED = ["slot_used", "proj_tile", "proj_slab", "proj_tile_out0", "proj_tile_out1", "proj_tile_out2", "proj_slab_scalar",
          "proj_slab_vector", "scores", "probs", "difference_transposed", "difference_copied", "att_out", "att_out_copied",
          "conv_silu", "conv_transposed", "conv_copied", "mixer_vector0", "mixer_vector1", "mixer_scalar0", "mixer_scalar1",
          "expert_gate", "expert_up", "expert_down", "expert_gathered", "expert_modulated", "expert_silu", "expert_hidden",
          "expert_kept"]


class Core:

    def __init__(self, nc, ctx):
        self.nc, self.ctx, self.signals = nc, ctx, {}
        self.size = 52180
        self.big = ctx.enter_context(nc.sbuf_tensor("sbuf_all", [P, self.size], F32))
        self.bank = [ctx.enter_context(nc.psum_tensor(f"bank{i}", [P, 512], F32)) for i in range(2)]
        self.wide = [ctx.enter_context(nc.psum_tensor(f"wide{i}", [P, 1024], F32)) for i in range(3)]
        for name in PRIMED:
            self.signals[name] = ctx.enter_context(nc.semaphore(name)), {"count": 1}
        self.vchain = Chain(ctx.enter_context(nc.semaphore("vector_chain")))
        self.achain = Chain(ctx.enter_context(nc.semaphore("scalar_chain")))

    def steps(self, name, names, by=1):
        if name not in self.signals:
            self.signals[name] = self.ctx.enter_context(self.nc.semaphore(name)), {}
        sem, kinds = self.signals[name]
        s = Steps(sem, names, by)
        s.base = kinds.get("count", 0)
        s.owner = kinds
        return s

    def view(self, at, *shape):
        n = 1
        for s in shape:
            n *= s
        assert at + n <= self.size, (at, shape)
        v = self.big[:, at:at + n]
        if len(shape) == 2:
            v = v.rearrange("p (a b) -> p a b", a=shape[0])
        if len(shape) == 3:
            v = v.rearrange("p (a b c) -> p a b c", a=shape[0], b=shape[1])
        return v


class Region:

    def __init__(self, core, at, end):
        self.core, self.at, self.end = core, at, end

    def __call__(self, *shape):
        n = 1
        for s in shape:
            n *= s
        v = self.core.view(self.at, *shape)
        self.at += n
        assert self.at <= self.end, ("region full", self.at, self.end)
        return v


A_CONST, A_FVEC, A_X, A_HT = 0, 4608, 5376, 11520
A_PT = A_HT + KD * T
A_FM = A_PT + NT * TMS * TMW
A_MIX = A_FM + FMT * T
A_WORK = A_MIX + NT * D
A_END = 52180


class Views:

    def __init__(self, core):
        self.const = core.view(A_CONST, NCONST2)
        self.ident = self.const[:, IDENT:IDENT + P]
        self.ones = self.const[:, ONES:ONES + P]
        self.x = core.view(A_X, NT, D)
        self.ht = core.view(A_HT, KD, T)
        self.pt = core.view(A_PT, NT, TMS * TMW)
        self.fm = core.view(A_FM, FMT * T)
        self.mix = core.view(A_MIX, NT, D)
        r = Region(core, A_FVEC, A_X)
        self.rows_t = r(96)
        self.mod = r(48, 2)
        self.cond = r(KD, 2)
        self.scale = r(2, 2, KD)
        self.gate = r(2, 2, KD)
        self.stat = r(NT)
        self.rstd = r(NT)
        self.std = r(NT)
        self.lam = r(8)
        self.small = r(464)


def load_start(core, v, io):
    nc = core.nc
    came = core.steps("start_loaded", ["all"], 48)
    with nc.Block() as block:
        @block.sync
        def _(sp):
            for name in PRIMED:
                sp.sem_inc(core.signals[name][0], 1)
            sp.dma_start(v.const[:, :], io["consts"]).then_inc(came.sem, 16)
            sp.dma_start(v.x[:, 0:CT, :], io["ctx"].rearrange("(t p) d -> p t d", p=P)).then_inc(came.sem, 16)
            sp.dma_start(v.x[:, CT:NT, :], io["x"].rearrange("(t p) d -> p t d", p=P)).then_inc(came.sem, 16)
            sp.wait_ge(came.sem, came.count("all"))
    came.owner["count"] = came.base + 48


def modulation(core, v, io, i):
    nc = core.nc
    r = Region(core, A_PT, A_MIX)
    SL = 4
    slot = [r(KD, 512) for _ in range(SL)]
    rows = Region(core, A_WORK, A_END)(P)
    rows_in = core.steps("mod_rows_in", ["all"], 80)
    w_in = [core.steps(f"slot_in{s}", ["w"], 16) for s in range(SL)]
    w_used = core.steps("slot_used", [f"w{s}" for s in range(SL)])
    pe_s = core.steps("tensor_steps", ["rows_t"])
    act_s = core.steps("scalar_steps", ["rows_t", "cond0", "cond1"])
    N = 12 // SL
    mp = core.wide[0]
    with nc.Block() as block:
        @block.sync
        def _(sp):
            for at, src in ((0, io["b_mod"][i].rearrange("(r n) -> r n", n=P)),
                            (48, io["norm_pre"][i].rearrange("j (r n) -> (j r) n", n=P)),
                            (64, io["norm_post"][i].rearrange("j (r n) -> (j r) n", n=P)),
                            (80, io["c"].rearrange("a (r n) -> (a r) n", n=P)),
                            (88, io["c_ctx"].rearrange("(r n) -> r n", n=P))):
                sp.dma_start(rows[at:at + src.shape[0], :], src).then_inc(rows_in.sem, 16)
            with sp.Fori(0, N) as n:
                for s in range(SL):
                    sp.wait_ge(w_used.sem, w_used.base + n * SL)
                    sp.dma_start(
                        slot[s], io["w_mod"][i].rearrange("(k p) n -> p k n", p=P)[:, :, ds((n * SL + s) * 512, 512)]).then_inc(w_in[s].sem, w_in[s].step("w"))

        @block.tensor
        def _(pe):
            pe.wait_ge(rows_in.sem, rows_in.count("all"))
            pe.transpose(core.bank[0][:, 0:96], rows[0:96, :], v.ident[0:96, 0:96]).then_inc(pe_s.sem, pe_s.step("rows_t"))
            pe.wait_ge(act_s.sem, act_s.count("cond1"))
            with pe.Fori(0, N) as n:
                for s in range(SL):
                    pe.wait_ge(w_in[s].sem, w_in[s].count("w", n))
                    for f in range(4):
                        for k in range(KD):
                            last = pe.matmul(mp[:, ds((n * SL + s) * 8 + f * 2, 2)], slot[s][:, k, f * P:(f + 1) * P],
                                             v.cond[:, k, :], start=(k == 0), stop=(k == KD - 1))
                    last.then_inc(w_used.sem, w_used.step(f"w{s}"))

        @block.scalar
        def _(act):
            act.wait_ge(pe_s.sem, pe_s.count("rows_t"))
            act.copy(v.rows_t, core.bank[0][:, 0:96]).then_inc(act_s.sem, act_s.step("rows_t"))
            act.wait_ge(act_s.sem, act_s.count("rows_t"))
            act.activation(v.cond[:, :, 0], v.rows_t[:, 80:88], ACT.Silu).then_inc(act_s.sem, act_s.step("cond0"))
            act.activation(v.cond[:, :, 1], v.rows_t[:, 88:96], ACT.Silu).then_inc(act_s.sem, act_s.step("cond1"))

        @block.vector
        def _(dve):
            ch = core.vchain
            dve.wait_ge(act_s.sem, act_s.count("rows_t"))
            dve.wait_ge(w_used.sem, w_used.count(f"w{SL - 1}", N - 1))
            dve.tensor_tensor(v.mod[:, :, :], mp[:, 0:96].rearrange("p (a b) -> p a b", b=2),
                                           v.rows_t[:, 0:48].unsqueeze(2).broadcast_to([P, 48, 2]), ALU.add).then_inc(ch.sem, ch.up())
            dve.wait_ge(ch.sem, ch.count())
            for j in range(2):
                for c in range(2):
                    dve.scalar_tensor_tensor(out=v.scale[:, j, c, :], in0=v.mod[:, 24 * j + 8:24 * j + 16, c], scalar=1.0,
                                             in1=v.rows_t[:, 48 + 8 * j:56 + 8 * j], op0=ALU.add, op1=ALU.mult)
                    last = dve.tensor_tensor(v.gate[:, j, c, :], v.mod[:, 24 * j + 16:24 * j + 24, c],
                                             v.rows_t[:, 64 + 8 * j:72 + 8 * j], ALU.mult)
            last.then_inc(ch.sem, ch.up())
            dve.wait_ge(ch.sem, ch.count())
    for s in (rows_in, pe_s, act_s):
        s.close()
    w_used.close(N)
    for s in w_in:
        s.close(N)


def stream(t):
    return 1 if t < CT else 0


def normed_transposed(core, v, j, tiles, w_start, dst):
    r = Region(core, w_start, w_start + 3 * D)
    junk, xn = r(D), [r(D), r(D)]
    n = len(tiles)
    sq = core.steps("norm_scalar", ["squares", "root"])
    ms = core.steps("norm_vector", ["mean", "rstd"] + [f"xn{t}" for t in range(n)])
    tr = core.steps("norm_transposed", [f"t{t}" for t in range(n)])
    eva = core.steps("norm_evac_scalar", [f"t{t}" for t in range(n)])
    evv = core.steps("norm_evac_vector", [f"t{t}" for t in range(n)])
    lo, hi = tiles[0], tiles[-1] + 1

    def evac(eng, steps, q, odd):
        t = tiles[q]
        c = stream(t)
        eng.wait_ge(tr.sem, tr.count(f"t{q}"))
        for k in range(4 * odd, 4 * odd + 4):
            out, src = dst[:, k, t * P:(t + 1) * P], core.wide[q % 2][:, k * P:(k + 1) * P]
            a, b = v.scale[:, j, c, k:k + 1], v.mod[:, 24 * j + k, c:c + 1]
            if odd:
                last = eng.activation(out, src, ACT.Identity, bias=b, scale=a)
            else:
                last = eng.tensor_scalar(out, src, a, b, ALU.mult, ALU.add)
        last.then_inc(steps.sem, steps.step(f"t{q}"))

    def act_part(act):
        for t in tiles:
            ins = act.activation(junk, v.x[:, t, :], ACT.Square, accum_out=v.stat[:, t:t + 1])
            if t < tiles[-1]:
                ins.then_inc(core.achain.sem, core.achain.up())
                act.wait_ge(core.achain.sem, core.achain.count())
        ins.then_inc(sq.sem, sq.step("squares"))
        act.wait_ge(ms.sem, ms.count("mean"))
        act.activation(v.std[:, lo:hi], v.stat[:, lo:hi], ACT.Sqrt).then_inc(sq.sem, sq.step("root"))
        for q in range(n):
            evac(act, eva, q, 1)

    def dve_part(dve):
        dve.wait_ge(sq.sem, sq.count("squares"))
        dve.tensor_scalar(v.stat[:, lo:hi], v.stat[:, lo:hi], 1.0 / D, EPS, ALU.mult, ALU.add).then_inc(ms.sem, ms.step("mean"))
        dve.wait_ge(sq.sem, sq.count("root"))
        dve.reciprocal(v.rstd[:, lo:hi], v.std[:, lo:hi]).then_inc(ms.sem, ms.step("rstd"))
        dve.wait_ge(ms.sem, ms.count("rstd"))
        for q, t in enumerate(tiles):
            if q >= 2:
                dve.wait_ge(tr.sem, tr.count(f"t{q - 2}"))
            dve.tensor_scalar(xn[q % 2], v.x[:, t, :], v.rstd[:, t:t + 1], None, ALU.mult).then_inc(ms.sem, ms.step(f"xn{q}"))
            if q >= 1:
                evac(dve, evv, q - 1, 0)
        evac(dve, evv, n - 1, 0)

    def pe_part(pe):
        for q in range(n):
            pe.wait_ge(ms.sem, ms.count(f"xn{q}"))
            if q >= 2:
                pe.wait_ge(eva.sem, eva.count(f"t{q - 2}"))
                pe.wait_ge(evv.sem, evv.count(f"t{q - 2}"))
            for k in range(KD):
                last = pe.transpose(core.wide[q % 2][:, k * P:(k + 1) * P], xn[q % 2][:, k * P:(k + 1) * P], v.ident)
            last.then_inc(tr.sem, tr.step(f"t{q}"))

    def ready(eng):
        eng.wait_ge(eva.sem, eva.count(f"t{n - 1}"))
        eng.wait_ge(evv.sem, evv.count(f"t{n - 1}"))

    def close():
        for s in (sq, ms, tr, eva, evv):
            s.close()

    return act_part, dve_part, pe_part, ready, close


def projections(core, v, io, i):
    nc = core.nc
    rm, rw = Region(core, A_MIX, A_WORK), Region(core, A_WORK, A_END)
    SF, ST = 3, 2
    act_n, dve_n, pe_n, ready, close = normed_transposed(core, v, 0, list(range(NT)), rm.at, v.ht)
    rm.at += 3 * D
    fslot = [rm(KD, P) for _ in range(SF)]
    tslot = [rw(KD, TMW) for _ in range(ST)]
    f_in = [core.steps(f"slot_in{s}", ["w"], 16) for s in range(SF)]
    t_in = [core.steps(f"slab_in{s}", ["w"], 16) for s in range(ST)]
    f_mm = core.steps("proj_tile", [f"s{s}" for s in range(SF)])
    t_mm = core.steps("proj_slab", [f"s{s}t{t}" for s in range(ST) for t in range(NT)])
    f_ev = [core.steps(f"proj_tile_out{s}", ["out"]) for s in range(SF)]
    t_eva = core.steps("proj_slab_scalar", [f"s{s}t{t}" for s in range(ST) for t in range(0, NT, 2)])
    t_evv = core.steps("proj_slab_vector", [f"s{s}t{t}" for s in range(ST) for t in range(1, NT, 2)])
    NF, NS = FMT // SF, TMS // ST
    wf, wt = io["w_fm"][i], io["w_tm"][i]

    def slab_psum(t):
        return core.wide[t // 2][:, (t % 2) * 512:(t % 2) * 512 + TMW]

    with nc.Block() as block:
        @block.sync
        def _(sp):
            with sp.Fori(0, NF) as n:
                for s in range(SF):
                    sp.wait_ge(f_mm.sem, f_mm.base + n * SF)
                    sp.dma_start(fslot[s].rearrange("p k n -> p (k n)"), wf[:, ds((n * SF + s) * KD * P, KD * P)]).then_inc(f_in[s].sem, f_in[s].step("w"))

        @block.gpsimd
        def _(pool):
            with pool.Fori(0, NS) as n:
                for s in range(ST):
                    pool.wait_ge(t_mm.sem, t_mm.base + n * (ST * NT))
                    pool.dma_start(tslot[s].rearrange("p k n -> p (k n)"), wt[:, ds((n * ST + s) * KD * TMW, KD * TMW)]).then_inc(t_in[s].sem, t_in[s].step("w"))

        @block.tensor
        def _(pe):
            pe_n(pe)
            ready(pe)
            with pe.Fori(0, NF) as n:
                for s in range(SF):
                    pe.wait_ge(f_in[s].sem, f_in[s].count("w", n))
                    pe.wait_ge(f_ev[s].sem, f_ev[s].base + n)
                    for half, (a, b) in enumerate(((0, 512), (512, T))):
                        for k in range(KD):
                            last = pe.matmul(core.wide[s][:, a:b], fslot[s][:, k, :], v.ht[:, k, a:b],
                                             start=(k == 0), stop=(k == KD - 1))
                    last.then_inc(f_mm.sem, f_mm.step(f"s{s}"))
            for s in range(SF):
                pe.wait_ge(f_ev[s].sem, f_ev[s].count("out", NF - 1))
            with pe.Fori(0, NS) as n:
                for s in range(ST):
                    pe.wait_ge(t_in[s].sem, t_in[s].count("w", n))
                    for t in range(NT):
                        ev, per = (t_evv, NT // 2 * ST) if t % 2 else (t_eva, NT // 2 * ST)
                        if s == 0:
                            pe.wait_ge(ev.sem, ev.base + n * per)
                        else:
                            pe.wait_ge(ev.sem, ev.count(f"s0t{t}", n))
                        for k in range(KD):
                            last = pe.matmul(slab_psum(t), v.ht[:, k, t * P:(t + 1) * P], tslot[s][:, k, :],
                                             start=(k == 0), stop=(k == KD - 1))
                        last.then_inc(t_mm.sem, t_mm.step(f"s{s}t{t}"))

        @block.scalar
        def _(act):
            act_n(act)
            with act.Fori(0, NF) as n:
                for s in (0, 2):
                    act.wait_ge(f_mm.sem, f_mm.count(f"s{s}", n))
                    act.copy(v.fm[:, ds((n * SF + s) * T, T)], core.wide[s][:, 0:T]).then_inc(f_ev[s].sem, f_ev[s].step("out"))
            with act.Fori(0, NS) as n:
                for s in range(ST):
                    for t in range(0, NT, 2):
                        act.wait_ge(t_mm.sem, t_mm.count(f"s{s}t{t}", n))
                        act.copy(v.pt[:, t, ds((n * ST + s) * TMW, TMW)], slab_psum(t)).then_inc(t_eva.sem, t_eva.step(f"s{s}t{t}"))

        @block.vector
        def _(dve):
            dve_n(dve)
            with dve.Fori(0, NF) as n:
                dve.wait_ge(f_mm.sem, f_mm.count("s1", n))
                dve.tensor_copy(v.fm[:, ds((n * SF + 1) * T, T)], core.wide[1][:, 0:T]).then_inc(f_ev[1].sem, f_ev[1].step("out"))
            with dve.Fori(0, NS) as n:
                for s in range(ST):
                    for t in range(1, NT, 2):
                        dve.wait_ge(t_mm.sem, t_mm.count(f"s{s}t{t}", n))
                        dve.tensor_copy(v.pt[:, t, ds((n * ST + s) * TMW, TMW)], slab_psum(t)).then_inc(t_evv.sem, t_evv.step(f"s{s}t{t}"))
    close()
    f_mm.close(NF)
    for s in f_in + f_ev:
        s.close(NF)
    for s in (t_mm, t_eva, t_evv, *t_in):
        s.close(NS)


def attention(core, v, io, i, last):
    import math

    nc = core.nc
    lam_init = 0.8 - 0.6 * math.exp(-0.3 * i)
    SC = HD ** -0.5
    tiles = list(range(CT, NT)) if last else list(range(NT))
    NU = len(tiles)
    lat0, NL = CT * P, LT * P
    r = Region(core, A_HT, A_PT)
    q_h, k_h = r(T), r(T)
    prob = [r(2, T) for _ in range(2)]
    diff_t = [r(T)]
    w = Region(core, A_WORK, A_END)
    diff_t.append(w(T))
    diff = [w(T) for _ in range(2)]
    rot = [w(NL) for _ in range(2)]
    lamv, lamp, norm_g = w(256), w(2, HD), w(P)
    lam = v.lam[:, 0:1]

    stat = v.small[:, 0:24].rearrange("p (b s) -> p b s", b=2)
    group = v.small[:, 32:56]
    group2 = v.small[:, 64:88]
    small_in = core.steps("att_small_in", ["all"], 32)
    rope_mm = core.steps("rope_rotated", ["q", "k"])
    rope_a = core.steps("rope_context", ["q", "k"])
    rope_v = core.steps("rope_done", ["q", "k"])
    U = range(NU)
    s_mm = core.steps("scores", [f"u{u}" for u in U])
    mx = core.steps("score_max", [f"u{u}" for u in U])
    ex = core.steps("probs", [f"u{u}m{m}" for u in U for m in range(2)])
    df = core.steps("probs_difference", [f"u{u}" for u in U])
    tr = core.steps("difference_transposed", [f"u{u}" for u in U])
    te = core.steps("difference_copied", [f"u{u}" for u in U])
    o_mm = core.steps("att_out", [f"u{u}" for u in U])
    o_ev = core.steps("att_out_copied", [f"u{u}" for u in U])
    lam_a = core.steps("scalar_steps", ["lambda", "root"])
    lam_v = core.steps("vector_steps", ["lambda", "mean"])

    def keys(t):
        return lat0 if t < CT else T

    with nc.Block() as block:
        @block.sync
        def _(sp):
            sp.dma_start(lamv, io["da_lambda"][i:i + 1].rearrange("a b c -> a (b c)").partition_broadcast(P)).then_inc(small_in.sem, 16)
            sp.dma_start(norm_g, io["da_norm"][i:i + 1, :].partition_broadcast(P)).then_inc(small_in.sem, 16)

        @block.tensor
        def _(pe):
            def transposed(u, h):
                pe.wait_ge(df.sem, df.count(f"u{u}", h))
                n = keys(tiles[u]) // P
                if u:
                    pe.wait_ge(te.sem, te.count(f"u{u - 1}", h))
                else:
                    pe.wait_ge(te.sem, te.base + h * NU)
                for k in range(n):
                    t = pe.transpose(core.wide[2][:, k * P:(k + 1) * P], diff[u % 2][:, k * P:(k + 1) * P], v.ident)
                t.then_inc(tr.sem, tr.step(f"u{u}"))
                pe.wait_ge(te.sem, te.count(f"u{u}", h))
                if u:
                    pe.wait_ge(o_ev.sem, o_ev.count(f"u{u - 1}", h))
                else:
                    pe.wait_ge(o_ev.sem, o_ev.base + h * NU)
                for k in range(n):
                    t = pe.matmul(core.bank[0][:, 0:P], diff_t[u % 2][:, k * P:(k + 1) * P],
                                  v.pt[:, k, ds(h * P + V0, P)], start=(k == 0), stop=(k == n - 1))
                t.then_inc(o_mm.sem, o_mm.step(f"u{u}"))

            with pe.Fori(0, NH) as h:
                pe.wait_ge(te.sem, te.base + h * NU)
                pe.matmul(core.wide[2][:, 0:512], v.const[:, ROT:ROT + P], v.fm[:, ds(h * T + lat0, NL)],
                                       start=True, stop=True).then_inc(rope_mm.sem, rope_mm.step("q"))
                pe.matmul(core.wide[2][:, 512:1024], v.const[:, ROT:ROT + P], v.fm[:, ds(h * T + (4 * T + lat0), NL)],
                                       start=True, stop=True).then_inc(rope_mm.sem, rope_mm.step("k"))
                pe.wait_ge(rope_v.sem, rope_v.count("k", h))
                pe.wait_ge(rope_a.sem, rope_a.count("k", h))
                for u, t in enumerate(tiles):
                    if u:
                        pe.wait_ge(ex.sem, ex.count(f"u{u - 1}m1", h))
                    else:
                        pe.wait_ge(ex.sem, ex.base + h * (2 * NU))
                    n = keys(t)
                    for m in range(2):
                        a = m * HD
                        for lo in range(0, n, 512):
                            hi = min(lo + 512, n)
                            x = pe.matmul(core.wide[m][:, lo:hi], q_h[a:a + HD, t * P:(t + 1) * P], k_h[a:a + HD, lo:hi],
                                          start=True, stop=True)
                    x.then_inc(s_mm.sem, s_mm.step(f"u{u}"))
                    if u:
                        transposed(u - 1, h)
                transposed(NU - 1, h)

        @block.scalar
        def _(act):
            act.wait_ge(lam_v.sem, lam_v.count("lambda"))
            act.activation(v.lam[:, 2:4], v.lam[:, 2:4], ACT.Exp).then_inc(lam_a.sem, lam_a.step("lambda"))
            with act.Fori(0, NH) as h:
                act.wait_ge(s_mm.sem, s_mm.base + h * NU)
                for nm, dst, off in (("q", q_h, 0), ("k", k_h, 4 * T)):
                    act.copy(dst[:, 0:lat0], v.fm[:, ds(h * T + off, lat0)]).then_inc(rope_a.sem, rope_a.step(nm))
                for u, t in enumerate(tiles):
                    n = keys(t)
                    act.wait_ge(mx.sem, mx.count(f"u{u}", h))
                    b = u % 2
                    for m in range(2):
                        act.activation(prob[b][:, m, 0:n], core.wide[m][:, 0:n], ACT.Exp, bias=stat[:, b, m:m + 1],
                                               scale=SC, accum_out=stat[:, b, 2 + m:3 + m]).then_inc(ex.sem, ex.step(f"u{u}m{m}"))
                    act.wait_ge(tr.sem, tr.count(f"u{u}", h))
                    if u >= 2:
                        act.wait_ge(o_mm.sem, o_mm.count(f"u{u - 2}", h))
                    else:
                        act.wait_ge(o_mm.sem, o_mm.base + h * NU)
                    act.copy(diff_t[b][:, 0:n], core.wide[2][:, 0:n]).then_inc(te.sem, te.step(f"u{u}"))
            act.wait_ge(lam_v.sem, lam_v.count("mean"))
            act.activation(group[:, tiles[0] * NH:], group[:, tiles[0] * NH:], ACT.Sqrt).then_inc(lam_a.sem, lam_a.step("root"))

        @block.vector
        def _(dve):
            ch = core.vchain
            dve.wait_ge(small_in.sem, small_in.count("all"))
            for m in range(2):
                a = 2 * m * HD
                x = dve.tensor_tensor(lamp[:, m, :], lamv[:, a:a + HD], lamv[:, a + HD:a + 2 * HD], ALU.mult)
            x.then_inc(ch.sem, ch.up())
            dve.wait_ge(ch.sem, ch.count())
            dve.tensor_reduce(v.lam[:, 2:4], lamp, AX.X, ALU.add).then_inc(lam_v.sem, lam_v.step("lambda"))
            dve.wait_ge(lam_a.sem, lam_a.count("lambda"))
            dve.tensor_tensor(v.lam[:, 1:2], v.lam[:, 3:4], v.lam[:, 2:3], ALU.subtract).then_inc(ch.sem, ch.up())
            dve.wait_ge(ch.sem, ch.count())
            dve.tensor_scalar(lam, v.lam[:, 1:2], -lam_init, None, ALU.add).then_inc(ch.sem, ch.up())
            dve.wait_ge(ch.sem, ch.count())

            def out_copy(u, h):
                dve.wait_ge(o_mm.sem, o_mm.count(f"u{u}", h))
                dve.tensor_scalar(v.mix[:, tiles[u], ds(h * P, P)], core.bank[0][:, 0:P],
                                            stat[:, u % 2, 4:5], None, ALU.mult).then_inc(o_ev.sem, o_ev.step(f"u{u}"))

            with ch.loop(dve, NH, 4 + 3 * NU) as h:
                dve.wait_ge(s_mm.sem, s_mm.base + h * NU)
                cos, sin = v.const[:, COS:COS + NL], v.const[:, SIN:SIN + NL]
                for j, (nm, dst, off) in enumerate((("q", q_h, 0), ("k", k_h, 4 * T))):
                    dve.wait_ge(rope_mm.sem, rope_mm.count(nm, h))
                    dve.tensor_tensor(rot[j], core.wide[2][:, 512 * j:512 * j + NL], sin, ALU.mult).then_inc(ch.sem, ch.up())
                    dve.wait_ge(ch.sem, ch.count())
                    dve.tensor_tensor(dst[:, lat0:T], v.fm[:, ds(h * T + (off + lat0), NL)], cos, ALU.mult).then_inc(ch.sem, ch.up())
                    dve.wait_ge(ch.sem, ch.count())
                    dve.tensor_tensor(dst[:, lat0:T], dst[:, lat0:T], rot[j], ALU.add).then_inc(rope_v.sem, rope_v.step(nm))
                for u, t in enumerate(tiles):
                    n, b = keys(t), u % 2
                    dve.wait_ge(s_mm.sem, s_mm.count(f"u{u}", h))
                    for m in range(2):
                        x = dve.tensor_reduce(stat[:, b, m:m + 1], core.wide[m][:, 0:n], AX.X, ALU.max)
                    x.then_inc(ch.sem, ch.up())
                    dve.wait_ge(ch.sem, ch.count())
                    if u:
                        out_copy(u - 1, h)
                    dve.tensor_scalar(stat[:, b, 0:2], stat[:, b, 0:2], -SC, None, ALU.mult).then_inc(mx.sem, mx.step(f"u{u}"))
                    dve.wait_ge(ex.sem, ex.count(f"u{u}m1", h))
                    dve.reciprocal(stat[:, b, 4:6], stat[:, b, 2:4]).then_inc(ch.sem, ch.up())
                    dve.wait_ge(ch.sem, ch.count())
                    dve.scalar_tensor_tensor(out=stat[:, b, 6:7], in0=stat[:, b, 2:3], scalar=stat[:, b, 5:6],
                                                          in1=lam, op0=ALU.mult, op1=ALU.mult).then_inc(ch.sem, ch.up())
                    dve.wait_ge(ch.sem, ch.count())
                    if u >= 2:
                        dve.wait_ge(tr.sem, tr.count(f"u{u - 2}", h))
                    else:
                        dve.wait_ge(tr.sem, tr.base + h * NU)
                    dve.scalar_tensor_tensor(out=diff[b][:, 0:n], in0=prob[b][:, 1, 0:n], scalar=stat[:, b, 6:7],
                                                     in1=prob[b][:, 0, 0:n], op0=ALU.mult, op1=ALU.add).then_inc(df.sem, df.step(f"u{u}"))
                out_copy(NU - 1, h)
            dve.wait_ge(o_ev.sem, o_ev.count(f"u{NU - 1}", NH - 1))
            lo = tiles[0]
            sq = core.view(A_FM, NT, NH, P)
            att = v.mix[:, lo:NT, 0:NH * P]
            dve.tensor_tensor(sq[:, lo:NT].rearrange("p t h n -> p t (h n)"), att, att, ALU.mult).then_inc(ch.sem, ch.up())
            dve.wait_ge(ch.sem, ch.count())
            dve.tensor_reduce(group[:, lo * NH:], sq[:, lo:NT].rearrange("p t h n -> p (t h) n"), AX.X, ALU.add).then_inc(ch.sem, ch.up())
            dve.wait_ge(ch.sem, ch.count())
            (dve.tensor_scalar(group, group, 1.0 / P, EPS, ALU.mult, ALU.add) if lo == 0 else
                       dve.tensor_scalar(group[:, lo * NH:], group[:, lo * NH:], 1.0 / P, EPS, ALU.mult, ALU.add)).then_inc(lam_v.sem, lam_v.step("mean"))
            dve.wait_ge(lam_a.sem, lam_a.count("root"))
            dve.reciprocal(group2[:, lo * NH:], group[:, lo * NH:]).then_inc(ch.sem, ch.up())
            dve.wait_ge(ch.sem, ch.count())
            for t in tiles:
                a = v.mix[:, t, 0:NH * P].rearrange("p (h n) -> p h n", h=NH)
                x = dve.tensor_tensor(a, a, group2[:, t * NH:(t + 1) * NH].unsqueeze(2).broadcast_to([P, NH, P]), ALU.mult)
            x.then_inc(ch.sem, ch.up())
            dve.wait_ge(ch.sem, ch.count())
            for t in tiles:
                a = v.mix[:, t, 0:NH * P].rearrange("p (h n) -> p h n", h=NH)
                x = dve.scalar_tensor_tensor(out=a, in0=a, scalar=1.0 - lam_init,
                                             in1=norm_g.unsqueeze(1).broadcast_to([P, NH, P]), op0=ALU.mult, op1=ALU.mult)
            x.then_inc(ch.sem, ch.up())
            dve.wait_ge(ch.sem, ch.count())
    for s in (small_in, lam_a, lam_v):
        s.close()
    for s in (rope_mm, rope_a, rope_v, s_mm, mx, ex, df, tr, te, o_mm, o_ev):
        s.close(NH)


PTW = TMS * TMW
SQUARES = 4
STEPS3 = 3


class Small:

    def __init__(self, v):
        n = NT * 8
        self.g, self.beta, self.gcum, self.gtot, self.e_cum, self.e_tot, self.e_rest = (
            v.small[:, k * n:(k + 1) * n] for k in range(7))
        self.a_log = v.small[:, 336:344]
        self.dt = v.small[:, 344:352]


class MixerViews:

    def __init__(self, core):
        self.qkv = core.view(A_FM, NT * 3 * W)
        self.rw = [core.view(A_FM + n * NT * W, NT * W) for n in range(7)]
        self.kk, self.sig_w, self.kk_a, self.kd = self.rw[0], self.rw[1:3], self.rw[3:5], self.rw[5:7]
        self.pt = core.view(A_PT, NT * PTW)


def recurrence(core, v, kind):
    nc = core.nc
    rwkv = kind == "rwkv"
    mv = MixerViews(core)
    sm = None if rwkv else Small(v)
    hi, lo = Region(core, A_HT, A_PT), Region(core, A_WORK, A_END)
    spare = Region(core, A_FM + NT * 3 * W, A_FM + 14 * T)
    R = range(2)
    ct, bt, kt, rt, l0, lt0, rb, rk, x, xt = ([r(512) for r in (hi, lo)] for _ in range(10))
    u, st = ([r(W) for r in (hi, lo)] for _ in range(2))
    pair = [hi(512), lo(512)]
    tm = [[pair[d][:, 0:W], lo(W), lo(W), pair[d][:, W:512]] for d in R]
    off = pair
    sz = [lo(W), v.small[:, 0:W]] if rwkv else st
    pe8 = [v.small[:, 256 + 16 * d:264 + 16 * d].rearrange("p (h c) -> p h c", c=2) for d in R]
    if not rwkv:
        g_rows, dif, e1, e2, e2s, e1f = ([spare(512) for _ in R] for _ in range(6))
    L, L_T = [(l0[d], ct[d]) for d in R], [(lt0[d], bt[d]) for d in R]
    inv_t = kt if rwkv else rt
    n_t = lt0
    sol = ct
    bank = [[core.bank[0][:, :], core.bank[1][:, :], core.wide[0][:, 0:512], core.wide[0][:, 512:1024]],
            [core.wide[1][:, 0:512], core.wide[1][:, 512:1024], core.wide[2][:, 0:512], core.wide[2][:, 512:1024]]]
    strict_st, incl_st = (UPS, LOS), (UPI, LOI)
    in_ts, in_st, off_ts = (DLO, DUP), (DUP, DLO), (OLO, OUP)
    cum_in, cum_ex = (CUI, CLI), (CUS, CLS)
    half_in, half_out = (0, 1), (1, 0)

    def mask(at):
        return v.const[:, at:at + P].unsqueeze(1).broadcast_to([P, NH, P])

    def heads(ap, n):
        return ap.rearrange("p (h n) -> p h n", n=n)

    def xv_of(ap):
        return ap.rearrange("p (c h n) -> p c h n", c=2, h=NH)

    def xv(d):
        return xv_of(x[d])

    def of(flat, width, tile, at, n):
        return flat[:, ds(tile * width + at, n)]

    def per_head(flat, tile, d, n=P):
        return flat[0:n, ds(tile * 8 + d * 4, 4)]

    def spread(ap, m):
        return ap.unsqueeze(2).broadcast_to([ap.shape[0], NH, m])

    lev = ["sq1", "sqt1"]
    for j in range(1, SQUARES + 1):
        lev += ([f"sq{j + 1}"] if j < SQUARES else []) + ([f"sqt{j + 1}"] if j < SQUARES - 1 else []) + [f"inv{j}"]
    solve = ["x1", "n_t"] + [f"h{j}" for j in range(STEPS3)]
    scores = ["s_l", "s_lt", "s_k", "s_rb", "s_rk", "own"] if rwkv else ["s_l", "s_lt", "s_rb"]
    pe_s = [core.steps(f"mixer_tensor{d}", ["cum"] + ["t_c", "t_b", "t_k", "t_r"] + scores + lev + solve + ["t_x", "u", "out", "state"]) for d in R]
    act_n = (["ld", "e_in", "e_out", "e_half"] if rwkv else ["b_copy", "r_copy", "e1", "e2"]) + ["c_t", "k_t"] \
        + (["own"] if rwkv else []) + ["sq1", "sqt1", "sq2", "sqt2", "sq3", "sqt3", "sq4", "n_t", "x_t", "out"]
    act_s = [core.steps(f"mixer_scalar{d}", act_n) for d in R]
    dve_n = (["c_b", "x_state"] if rwkv else ["rows", "dif", "clip", "c_q", "x"]) + ["b_t", "r_t", "l", "of", "lt"] \
        + (["ak", "rb", "rk", "sz"] if rwkv else ["rb", "kd"]) + [f"inv{j}" for j in range(SQUARES + 1)] + ["x1"] + [f"h{j}" for j in range(STEPS3)] + ["u", "state"]
    dve_s = [core.steps(f"mixer_vector{d}", dve_n) for d in R]
    pool_s = [core.steps(f"mixer_pool{d}", ["k_r"] if rwkv else ["masked"]) for d in R]
    zeroed = core.steps("vector_steps", ["zeroed"])

    def passes(eng, chain, per, body):
        for first, count, tiles in ((0, CT, lambda j: (j, j * -1 + (CT - 1))), (CT, LT, lambda j: (j + CT, j * -1 + (NT - 1)))):
            if chain is None:
                with eng.Fori(0, count) as j:
                    body(j + first, tiles(j))
            else:
                with chain.loop(eng, count, per) as j:
                    body(j + first, tiles(j))

    def turn_over(eng, d, turn, copied=True):
        eng.wait_ge(dve_s[d].sem, dve_s[d].base + turn * len(dve_n))
        if copied:
            eng.wait_ge(act_s[d].sem, act_s[d].base + turn * len(act_n))

    def turned(pe, out, src, first):
        if first:
            return pe.matmul(out, src, v.ident, start=True, stop=True)
        return pe.transpose(out, src, v.ident)

    with nc.Block() as block:
        @block.tensor
        def _(pe):
            pe.wait_ge(zeroed.sem, zeroed.count("zeroed"))

            def body(turn, tile):
                for d in R:
                    turn_over(pe, d, turn, not rwkv)
                    A, B, C, E = bank[d]
                    if rwkv:
                        pe.wait_ge(act_s[d].sem, act_s[d].count("ld", turn))
                        pe.matmul(A[:, 0:W], v.const[:, cum_in[d]:cum_in[d] + P], xt[d][:, 0:W], start=True, stop=True)
                        pe.matmul(A[:, W:512], v.const[:, cum_ex[d]:cum_ex[d] + P], xt[d][:, 0:W], start=True, stop=True)
                        for h in range(NH):
                            m = pe.matmul(B[0:HD, 2 * h:2 * h + 2], xt[d][:, h * HD:(h + 1) * HD], v.const[:, COLS:COLS + 2],
                                          start=True, stop=True)
                    else:
                        pe.wait_ge(dve_s[d].sem, dve_s[d].count("rows", turn))
                        for h in range(NH):
                            m = pe.matmul(A[:, h * P:(h + 1) * P], g_rows[d][:, h * P:(h + 1) * P],
                                          v.const[:, incl_st[d]:incl_st[d] + P], start=True, stop=True)
                    m.then_inc(pe_s[d].sem, pe_s[d].step("cum"))
                for d in R:
                    A, B, C, E = bank[d]
                    if rwkv:
                        pe.wait_ge(dve_s[d].sem, dve_s[d].count("c_b", turn))
                        pe.wait_ge(act_s[d].sem, act_s[d].count("e_half", turn))
                    else:
                        pe.wait_ge(dve_s[d].sem, dve_s[d].count("c_q", turn))
                        pe.wait_ge(act_s[d].sem, act_s[d].count("r_copy", turn))
                        pe.wait_ge(dve_s[d].sem, dve_s[d].count("dif", turn))
                    for nm, bk, src in (("t_c", A, 0), ("t_b", B, 1), ("t_k", C, 2), ("t_r", E, 3)):
                        if rwkv and nm == "t_k":
                            pe.wait_ge(pool_s[d].sem, pool_s[d].count("k_r", turn))
                        for h in range(NH):
                            m = turned(pe, bk[0:HD, h * P:(h + 1) * P], tm[d][src][:, h * HD:(h + 1) * HD], h == 0)
                        m.then_inc(pe_s[d].sem, pe_s[d].step(nm))

                def by_head(d, bk, left, right, name):
                    for h in range(NH):
                        m = pe.matmul(bk[:, h * P:(h + 1) * P], left[0:HD, h * P:(h + 1) * P], right[0:HD, h * P:(h + 1) * P],
                                      start=True, stop=True)
                    m.then_inc(pe_s[d].sem, pe_s[d].step(name))

                for d in R:
                    A, B, C, E = bank[d]
                    pe.wait_ge(act_s[d].sem, act_s[d].count("c_t", turn))
                    pe.wait_ge(dve_s[d].sem, dve_s[d].count("b_t", turn))
                    by_head(d, A, ct[d], bt[d], "s_l")
                    by_head(d, B, bt[d], ct[d], "s_lt")
                    pe.wait_ge(act_s[d].sem, act_s[d].count("k_t", turn))
                    if rwkv:
                        by_head(d, C, kt[d], ct[d], "s_k")
                    pe.wait_ge(dve_s[d].sem, dve_s[d].count("r_t", turn))
                    by_head(d, E, bt[d], rt[d], "s_rb")
                    if rwkv:
                        pe.wait_ge(dve_s[d].sem, dve_s[d].count("of", turn))
                        by_head(d, A, kt[d], rt[d], "s_rk")
                if rwkv:
                    for d in R:
                        pe.wait_ge(dve_s[d].sem, dve_s[d].count("ak", turn))
                        for h in range(NH):
                            m = pe.matmul(bank[d][1][:, h * HD:(h + 1) * HD], xt[d][:, h * P:(h + 1) * P],
                                          of(mv.pt, PTW, tile[d], RKV0 + 2 * W + h * HD, HD), start=True, stop=True)
                        m.then_inc(pe_s[d].sem, pe_s[d].step("own"))
                def squares(d, j):
                    A, B, C, E = bank[d]
                    a, b = L[d][(j - 1) % 2], L_T[d][(j - 1) % 2]
                    for h in range(NH):
                        hp = slice(h * P, (h + 1) * P)
                        m = pe.matmul(A[:, hp], b[:, hp], a[:, hp], start=True, stop=True)
                    m.then_inc(pe_s[d].sem, pe_s[d].step(f"sq{j}"))
                    if j < SQUARES:
                        for h in range(NH):
                            hp = slice(h * P, (h + 1) * P)
                            m = pe.matmul(B[:, hp], a[:, hp], b[:, hp], start=True, stop=True)
                        m.then_inc(pe_s[d].sem, pe_s[d].step(f"sqt{j}"))

                def product(d, bk, left, right, name):
                    for h in range(NH):
                        m = pe.matmul(bk[:, h * P:(h + 1) * P], left[:, h * P:(h + 1) * P], right(h), start=True, stop=True)
                    m.then_inc(pe_s[d].sem, pe_s[d].step(name))

                for d in R:
                    pe.wait_ge(dve_s[d].sem, dve_s[d].count("rk" if rwkv else "rb", turn))
                    if rwkv:
                        pe.wait_ge(act_s[d].sem, act_s[d].count("own", turn))
                    squares(d, 1)
                for j in range(1, SQUARES + 1):
                    for d in R:
                        pe.wait_ge(act_s[d].sem, act_s[d].count(f"sqt{j}" if j < SQUARES else f"sq{j}", turn))
                        if j < SQUARES:
                            squares(d, j + 1)
                        pe.wait_ge(dve_s[d].sem, dve_s[d].count(f"inv{j - 1}", turn))
                        product(d, bank[d][2], L[d][j % 2], lambda h: inv_t[d][:, h * P:(h + 1) * P], f"inv{j}")
                for d in R:
                    pe.wait_ge(dve_s[d].sem, dve_s[d].count(f"inv{SQUARES}", turn))
                    product(d, bank[d][3], inv_t[d], lambda h: xv(d)[:, :, h, :], "x1")
                    product(d, bank[d][0], off[d], lambda h: inv_t[d][:, h * P:(h + 1) * P], "n_t")
                for j in range(STEPS3):
                    for d in R:
                        if j == 0:
                            pe.wait_ge(act_s[d].sem, act_s[d].count("n_t", turn))
                        pe.wait_ge(dve_s[d].sem, dve_s[d].count(f"h{j - 1}" if j else "x1", turn))
                        src = xv(d) if j == 0 else xv_of(sol[d])
                        product(d, bank[d][3], n_t[d], lambda h: src[:, :, h, :], f"h{j}")
                for d in R:
                    pe.wait_ge(dve_s[d].sem, dve_s[d].count(f"h{STEPS3 - 1}", turn))
                    for h in range(NH):
                        m = turned(pe, bank[d][0][0:HD, h * P:(h + 1) * P], xv_of(sol[d])[:, 1, h, :], h == 0)
                    m.then_inc(pe_s[d].sem, pe_s[d].step("t_x"))
                for d in R:
                    pe.wait_ge(act_s[d].sem, act_s[d].count("x_t", turn))
                    if rwkv:
                        pe.wait_ge(dve_s[d].sem, dve_s[d].count("sz", turn))
                    for h in range(NH):
                        m = pe.matmul(bank[d][2][:, h * HD:(h + 1) * HD], xt[d][0:HD, h * P:(h + 1) * P],
                                      sz[d][0:HD, h * HD:(h + 1) * HD], start=True, stop=True)
                    m.then_inc(pe_s[d].sem, pe_s[d].step("u"))
                for d in R:
                    A, B, C, E = bank[d]
                    pe.wait_ge(dve_s[d].sem, dve_s[d].count("u", turn))
                    read = rt[d] if rwkv else kt[d]
                    for h in range(NH):
                        hs, hp = slice(h * HD, (h + 1) * HD), slice(h * P, (h + 1) * P)
                        pe.matmul(E[:, hs], read[0:HD, hp], sz[d][0:HD, hs], start=True, stop=False)
                        m = pe.matmul(E[:, hs], rb[d][:, hp], u[d][:, hs], start=False, stop=not rwkv)
                        if rwkv:
                            m = pe.matmul(E[:, hs], rk[d][:, hp], of(mv.pt, PTW, tile[d], RKV0 + 2 * W + h * HD, HD),
                                          start=False, stop=True)
                    m.then_inc(pe_s[d].sem, pe_s[d].step("out"))
                    for h in range(NH):
                        hs = slice(h * HD, (h + 1) * HD)
                        m = pe.matmul(B[0:HD, hs], tm[d][1][:, hs], u[d][:, hs], start=True, stop=not rwkv)
                        if rwkv:
                            m = pe.matmul(B[0:HD, hs], tm[d][2][:, hs], of(mv.pt, PTW, tile[d], RKV0 + 2 * W + h * HD, HD),
                                          start=False, stop=True)
                    m.then_inc(pe_s[d].sem, pe_s[d].step("state"))

            passes(pe, None, 0, body)

        @block.scalar
        def _(act):
            def body(turn, tile):
                for d in R:
                    turn_over(act, d, turn)
                    if rwkv:
                        act.copy(xt[d][:, 0:W], of(mv.sig_w[d], W, tile[d], 0, W)).then_inc(act_s[d].sem, act_s[d].step("ld"))
                    else:
                        act.copy(tm[d][1], of(mv.qkv, 3 * W, tile[d], W, W)).then_inc(act_s[d].sem, act_s[d].step("b_copy"))
                        act.copy(tm[d][3], of(mv.qkv, 3 * W, tile[d], 0, W)).then_inc(act_s[d].sem, act_s[d].step("r_copy"))
                for d in R:
                    A, B, C, E = bank[d]
                    if rwkv:
                        act.wait_ge(pe_s[d].sem, pe_s[d].count("cum", turn))
                        act.activation(l0[d], A, ACT.Exp, scale=-DECAY).then_inc(act_s[d].sem, act_s[d].step("e_in"))
                        act.activation(lt0[d][:, 0:W], A[:, 0:W], ACT.Exp, scale=DECAY).then_inc(act_s[d].sem, act_s[d].step("e_out"))
                        act.activation(pe8[d][0:HD], B[0:HD, 0:8].rearrange("p (h c) -> p h c", c=2), ACT.Exp, scale=-DECAY).then_inc(act_s[d].sem, act_s[d].step("e_half"))
                    else:
                        act.wait_ge(dve_s[d].sem, dve_s[d].count("clip", turn))
                        act.activation(e1[d], e1[d], ACT.Exp, scale=-1.0).then_inc(act_s[d].sem, act_s[d].step("e1"))
                        act.activation(e2[d], e2[d], ACT.Exp).then_inc(act_s[d].sem, act_s[d].step("e2"))
                for d in R:
                    A, B, C, E = bank[d]
                    act.wait_ge(pe_s[d].sem, pe_s[d].count("t_c", turn))
                    act.copy(ct[d][0:HD, :], A[0:HD, :]).then_inc(act_s[d].sem, act_s[d].step("c_t"))
                    act.wait_ge(pe_s[d].sem, pe_s[d].count("t_k", turn))
                    act.copy(kt[d][0:HD, :], C[0:HD, :]).then_inc(act_s[d].sem, act_s[d].step("k_t"))
                if rwkv:
                    for d in R:
                        act.wait_ge(pe_s[d].sem, pe_s[d].count("own", turn))
                        act.copy(x[d][:, 0:W], bank[d][1][:, 0:W]).then_inc(act_s[d].sem, act_s[d].step("own"))
                for j in range(1, SQUARES + 1):
                    for d in R:
                        act.wait_ge(pe_s[d].sem, pe_s[d].count(f"sq{j}", turn))
                        act.copy(L[d][j % 2], bank[d][0]).then_inc(act_s[d].sem, act_s[d].step(f"sq{j}"))
                        if j < SQUARES:
                            if j == 2:
                                act.wait_ge(dve_s[d].sem, dve_s[d].count("inv0", turn))
                            act.wait_ge(pe_s[d].sem, pe_s[d].count(f"sqt{j}", turn))
                            act.copy(L_T[d][j % 2], bank[d][1]).then_inc(act_s[d].sem, act_s[d].step(f"sqt{j}"))
                for d in R:
                    act.wait_ge(pe_s[d].sem, pe_s[d].count("n_t", turn))
                    act.copy(n_t[d], bank[d][0]).then_inc(act_s[d].sem, act_s[d].step("n_t"))
                for d in R:
                    act.wait_ge(pe_s[d].sem, pe_s[d].count("t_x", turn))
                    act.copy(xt[d][0:HD, :], bank[d][0][0:HD, :]).then_inc(act_s[d].sem, act_s[d].step("x_t"))
                for d in R:
                    act.wait_ge(pe_s[d].sem, pe_s[d].count("out", turn))
                    act.copy(of(mv.pt, PTW, tile[d], V0 + d * W, W), bank[d][3][:, 0:W]).then_inc(act_s[d].sem, act_s[d].step("out"))

            passes(act, None, 0, body)

        @block.gpsimd
        def _(pool):
            def body(turn, tile):
                for d in R:
                    turn_over(pool, d, turn, False)
                    if rwkv:
                        pool.wait_ge(act_s[d].sem, act_s[d].count("e_out", turn))
                        pool.tensor_tensor(tm[d][2], of(mv.kd[d], W, tile[d], 0, W), lt0[d][:, 0:W], ALU.mult)
                        pool.tensor_tensor(tm[d][3], of(mv.pt, PTW, tile[d], RKV0, W), l0[d][:, 0:W], ALU.mult).then_inc(pool_s[d].sem, pool_s[d].step("k_r"))
                    else:
                        pool.wait_ge(act_s[d].sem, act_s[d].count("e2", turn))
                        pool.tensor_tensor(heads(rk[d], P), heads(e2[d], P), mask(incl_st[d]), ALU.mult)
                        pool.tensor_tensor(heads(e2s[d], P), heads(e2[d], P), mask(in_st[d]), ALU.mult)
                        pool.tensor_tensor(heads(e1f[d], P), heads(e1[d], P), mask(off_ts[d]), ALU.mult)
                        pool.tensor_tensor(heads(dif[d], P), heads(e1[d], P), mask(in_ts[d]), ALU.mult).then_inc(pool_s[d].sem, pool_s[d].step("masked"))

            passes(pool, None, 0, body)

        @block.vector
        def _(dve):
            ch = core.vchain
            for d in R:
                m = dve.memset(st[d][0:HD, :], 0.0)
            m.then_inc(zeroed.sem, zeroed.step("zeroed"))
            dve.wait_ge(zeroed.sem, zeroed.count("zeroed"))

            def masked(d, name, src, dst, weights, sign):
                dve.wait_ge(pe_s[d].sem, pe_s[d].count(name[0], turn_[0]))
                dve.scalar_tensor_tensor(out=heads(dst, P), in0=heads(src, P), scalar=sign, in1=weights,
                                                       op0=ALU.mult, op1=ALU.mult).then_inc(dve_s[d].sem, dve_s[d].step(name[1]))

            turn_ = [0]

            def body(turn, tile):
                turn_[0] = turn
                for d in R:
                    turn_over(dve, d, turn)
                    if not rwkv:
                        dve.tensor_copy(heads(g_rows[d], P), spread(per_head(sm.g, tile[d], d), P)).then_inc(dve_s[d].sem, dve_s[d].step("rows"))
                for d in R:
                    A, B, C, E = bank[d]
                    if rwkv:
                        dve.wait_ge(act_s[d].sem, act_s[d].count("e_out", turn))
                        dve.tensor_tensor(tm[d][0], of(mv.kk, W, tile[d], 0, W), l0[d][:, W:512], ALU.mult)
                        dve.tensor_tensor(tm[d][1], of(mv.kk_a[d], W, tile[d], 0, W), lt0[d][:, 0:W], ALU.mult).then_inc(dve_s[d].sem, dve_s[d].step("c_b"))
                    else:
                        dve.wait_ge(pe_s[d].sem, pe_s[d].count("cum", turn))
                        dve.tensor_tensor(heads(dif[d], P), heads(A, P), spread(per_head(sm.gcum, tile[d], d), P), ALU.subtract).then_inc(dve_s[d].sem, dve_s[d].step("dif"))
                        dve.wait_ge(dve_s[d].sem, dve_s[d].count("dif", turn))
                        dve.tensor_scalar(e1[d], dif[d], 0.0, None, ALU.max)
                        dve.tensor_scalar(e2[d], dif[d], 0.0, None, ALU.min).then_inc(dve_s[d].sem, dve_s[d].step("clip"))
                for d in R:
                    if rwkv:
                        dve.wait_ge(dve_s[d].sem, dve_s[d].count("c_b", turn))
                        dve.tensor_scalar(x[d][:, W:512], tm[d][0], -1.0, None, ALU.mult).then_inc(dve_s[d].sem, dve_s[d].step("x_state"))
                    else:
                        q, k, vv = (heads(of(mv.qkv, 3 * W, tile[d], n * W, W), HD) for n in range(3))
                        dve.tensor_tensor(heads(tm[d][0], HD), k, spread(per_head(sm.beta, tile[d], d), HD), ALU.mult)
                        dve.tensor_tensor(heads(tm[d][2], HD), q, spread(per_head(sm.e_cum, tile[d], d), HD), ALU.mult).then_inc(dve_s[d].sem, dve_s[d].step("c_q"))
                        dve.tensor_tensor(heads(x[d][:, 0:W], HD), vv, spread(per_head(sm.beta, tile[d], d), HD), ALU.mult)
                        dve.wait_ge(dve_s[d].sem, dve_s[d].count("c_q", turn))
                        dve.tensor_tensor(heads(x[d][:, W:512], HD), heads(tm[d][0], HD), spread(per_head(sm.e_cum, tile[d], d), HD), ALU.mult).then_inc(ch.sem, ch.up())
                        dve.wait_ge(ch.sem, ch.count())
                        dve.tensor_scalar(x[d][:, W:512], x[d][:, W:512], -1.0, None, ALU.mult).then_inc(dve_s[d].sem, dve_s[d].step("x"))
                for d in R:
                    A, B, C, E = bank[d]
                    dve.wait_ge(pe_s[d].sem, pe_s[d].count("t_b", turn))
                    dve.tensor_copy(bt[d][0:HD, :], B[0:HD, :]).then_inc(dve_s[d].sem, dve_s[d].step("b_t"))
                    dve.wait_ge(pe_s[d].sem, pe_s[d].count("t_r", turn))
                    dve.tensor_copy(rt[d][0:HD, :], E[0:HD, :]).then_inc(dve_s[d].sem, dve_s[d].step("r_t"))
                for d in R:
                    A, B, C, E = bank[d]
                    if not rwkv:
                        dve.wait_ge(pool_s[d].sem, pool_s[d].count("masked", turn))
                    masked(d, ("s_l", "l"), A, l0[d], mask(in_ts[d]) if rwkv else heads(dif[d], P), -1.0)
                    masked(d, ("s_l", "of"), A, off[d], mask(off_ts[d]) if rwkv else heads(e1f[d], P), -1.0)
                    masked(d, ("s_lt", "lt"), B, lt0[d], mask(in_st[d]) if rwkv else heads(e2s[d], P), -1.0)
                    if rwkv:
                        masked(d, ("s_k", "ak"), C, xt[d], mask(strict_st[d]), -1.0)
                    masked(d, ("s_rb", "rb"), E, rb[d], mask(incl_st[d]) if rwkv else heads(rk[d], P), 1.0)
                    if rwkv:
                        masked(d, ("s_rk", "rk"), A, rk[d], mask(incl_st[d]), 1.0)
                        dve.tensor_tensor(heads(sz[d][0:HD, :], HD), heads(st[d][0:HD, :], HD),
                                                        spread(pe8[d][0:HD, :, half_in[d]], HD), ALU.mult).then_inc(dve_s[d].sem, dve_s[d].step("sz"))
                    else:
                        k = heads(of(mv.qkv, 3 * W, tile[d], W, W), HD)
                        dve.tensor_tensor(heads(tm[d][1], HD), k, spread(per_head(sm.e_rest, tile[d], d), HD), ALU.mult).then_inc(dve_s[d].sem, dve_s[d].step("kd"))
                for d in R:
                    dve.wait_ge(dve_s[d].sem, dve_s[d].count("lt", turn))
                    if rwkv:
                        dve.wait_ge(pe_s[d].sem, pe_s[d].count("s_rk", turn))
                    dve.tensor_tensor(heads(inv_t[d], P), heads(lt0[d], P), mask(IDENT), ALU.add).then_inc(dve_s[d].sem, dve_s[d].step("inv0"))
                for j in range(1, SQUARES + 1):
                    for d in R:
                        dve.wait_ge(pe_s[d].sem, pe_s[d].count(f"inv{j}", turn))
                        dve.wait_ge(dve_s[d].sem, dve_s[d].count(f"inv{j - 1}", turn))
                        dve.tensor_tensor(inv_t[d], inv_t[d], bank[d][2], ALU.add).then_inc(dve_s[d].sem, dve_s[d].step(f"inv{j}"))

                def by_part(ap):
                    return xv_of(ap).rearrange("p c h n -> p h c n")

                for d in R:
                    dve.wait_ge(pe_s[d].sem, pe_s[d].count("x1", turn))
                    E = bank[d][3].rearrange("p (h c n) -> p h c n", h=NH, c=2)
                    dve.tensor_copy(by_part(x[d]), E).then_inc(dve_s[d].sem, dve_s[d].step("x1"))
                for j in range(STEPS3):
                    for d in R:
                        dve.wait_ge(pe_s[d].sem, pe_s[d].count(f"h{j}", turn))
                        if j == 0:
                            dve.wait_ge(dve_s[d].sem, dve_s[d].count("x1", turn))
                        E = bank[d][3].rearrange("p (h c n) -> p h c n", h=NH, c=2)
                        dve.tensor_tensor(by_part(sol[d]), by_part(x[d]), E, ALU.add).then_inc(dve_s[d].sem, dve_s[d].step(f"h{j}"))
                for d in R:
                    dve.wait_ge(pe_s[d].sem, pe_s[d].count("u", turn))
                    dve.wait_ge(dve_s[d].sem, dve_s[d].count(f"h{STEPS3 - 1}", turn))
                    dve.tensor_tensor(u[d], bank[d][2][:, 0:W], sol[d][:, 0:W], ALU.add).then_inc(dve_s[d].sem, dve_s[d].step("u"))
                for d in R:
                    s, fresh = heads(st[d][0:HD, :], HD), heads(bank[d][1][0:HD, 0:W], HD)
                    dve.wait_ge(pe_s[d].sem, pe_s[d].count("state", turn))
                    if rwkv:
                        dve.tensor_tensor(s, heads(sz[d][0:HD, :], HD), fresh, ALU.add).then_inc(ch.sem, ch.up())
                        dve.wait_ge(ch.sem, ch.count())
                        dve.tensor_tensor(s, s, spread(pe8[d][0:HD, :, half_out[d]], HD), ALU.mult).then_inc(dve_s[d].sem, dve_s[d].step("state"))
                    else:
                        dve.tensor_tensor(s, s, spread(per_head(sm.e_tot, tile[d], d, HD), HD), ALU.mult).then_inc(ch.sem, ch.up())
                        dve.wait_ge(ch.sem, ch.count())
                        dve.tensor_tensor(s, s, fresh, ALU.add).then_inc(dve_s[d].sem, dve_s[d].step("state"))

            passes(dve, ch, 2 if rwkv else 4, body)
    for s in (*pe_s, *act_s, *dve_s, *pool_s):
        s.at = 0
        s.close(NT)
    zeroed.close()


def gdn(core, v, io, i):
    nc = core.nc
    mv, sm = MixerViews(core), Small(v)
    hi, lo = Region(core, A_HT, A_PT), Region(core, A_WORK, A_END)
    acc, conv = [lo(T) for _ in range(2)], [lo(T) for _ in range(2)]
    rows, taps = lo(P), lo(32)
    sp8 = [lo(NT * 8) for _ in range(3)]
    sq = hi(NT, 512)
    inv = hi(NT * 8)
    norm_g = hi(HD)
    F0 = 8 * T
    segs = ((0, CT * P), (CT * P, T))
    small_in = core.steps("gdn_small_in", ["all"], 64)
    NC = 3
    cv = core.steps("conv_sum", ["s0", "s1"])
    ca = core.steps("conv_silu", ["s0", "s1"])
    ctp = core.steps("conv_transposed", ["s0", "s1"])
    ce = core.steps("conv_copied", ["s0", "s1"])
    pe_s = core.steps("tensor_steps", ["taps", "cums"])
    act_s = core.steps("scalar_steps", ["taps", "root", "exps", "log", "beta", "cums"])
    dve_s = core.steps("vector_steps", ["sums", "arg", "plus1", "g", "rest"])
    ab = v.pt[:, :, AB0:AB0 + 16]

    def t8(ap):
        return ap.rearrange("p (t c) -> p t c", c=8)

    with nc.Block() as block:
        @block.sync
        def _(sp):
            sp.dma_start(rows[0:30, :], io["gdn_conv"][i].rearrange("j (r n) -> (j r) n", n=P)).then_inc(small_in.sem, 16)
            sp.dma_start(sm.a_log, io["gdn_a_log"][i:i + 1].rearrange("a b c -> a (b c)").partition_broadcast(P)).then_inc(small_in.sem, 16)
            sp.dma_start(sm.dt, io["gdn_dt_bias"][i:i + 1].rearrange("a b c -> a (b c)").partition_broadcast(P)).then_inc(small_in.sem, 16)
            sp.dma_start(norm_g, io["gdn_norm"][i:i + 1, :].partition_broadcast(P)).then_inc(small_in.sem, 16)

        @block.tensor
        def _(pe):
            pe.wait_ge(small_in.sem, small_in.count("all"))
            pe.transpose(core.bank[0][:, 0:30], rows[0:30, :], v.ident[0:30, 0:30]).then_inc(pe_s.sem, pe_s.step("taps"))
            with pe.Fori(0, NC) as n:
                for s in range(2):
                    pe.wait_ge(ca.sem, ca.count(f"s{s}", n))
                    pe.wait_ge(ce.sem, ce.base + n * 2)
                    for t in range(NT):
                        x = pe.transpose(core.wide[s][:, t * P:(t + 1) * P], conv[s][:, t * P:(t + 1) * P], v.ident)
                    x.then_inc(ctp.sem, ctp.step(f"s{s}"))
            pe.wait_ge(dve_s.sem, dve_s.count("g"))
            for b, m in enumerate((UPI, LOI, ONES)):
                x = pe.matmul(core.wide[2][:, 64 * b:64 * b + 48], v.const[:, m:m + P], sm.g, start=True, stop=True)
            x.then_inc(pe_s.sem, pe_s.step("cums"))

        @block.scalar
        def _(act):
            act.wait_ge(pe_s.sem, pe_s.count("taps"))
            act.copy(taps[:, 0:30], core.bank[0][:, 0:30]).then_inc(act_s.sem, act_s.step("taps"))
            with act.Fori(0, NC) as n:
                for s in range(2):
                    act.wait_ge(cv.sem, cv.count(f"s{s}", n))
                    act.wait_ge(ctp.sem, ctp.base + n * 2)
                    act.activation(conv[s], acc[s], ACT.Silu).then_inc(ca.sem, ca.step(f"s{s}"))
                for s in range(2):
                    act.wait_ge(ctp.sem, ctp.count(f"s{s}", n))
                    act.copy(mv.qkv.rearrange("p (t c) -> p t c", t=NT)[:, :, ds((n * 2 + s) * P, P)],
                                     core.wide[s][:, 0:T].rearrange("p (t c) -> p t c", t=NT)).then_inc(ce.sem, ce.step(f"s{s}"))
            act.wait_ge(dve_s.sem, dve_s.count("sums"))
            act.activation(inv, inv, ACT.Sqrt).then_inc(act_s.sem, act_s.step("root"))
            act.wait_ge(dve_s.sem, dve_s.count("arg"))
            act.activation(sm.a_log, sm.a_log, ACT.Exp)
            act.activation(sp8[1], sp8[1], ACT.Exp, scale=-1.0).then_inc(act_s.sem, act_s.step("exps"))
            act.wait_ge(dve_s.sem, dve_s.count("plus1"))
            act.activation(sp8[2], sp8[2], ACT.Ln).then_inc(act_s.sem, act_s.step("log"))
            act.activation(t8(sm.beta), ab[:, :, 8:16], ACT.Sigmoid).then_inc(act_s.sem, act_s.step("beta"))
            act.wait_ge(dve_s.sem, dve_s.count("rest"))
            act.activation(sm.e_cum, sm.gcum, ACT.Exp)
            act.activation(sm.e_tot, sm.gtot, ACT.Exp)
            act.activation(sm.e_rest, sm.e_rest, ACT.Exp).then_inc(act_s.sem, act_s.step("cums"))

        @block.vector
        def _(dve):
            ch = core.vchain
            dve.wait_ge(act_s.sem, act_s.count("taps"))
            with ch.loop(dve, NC, 8) as n:
                for s in range(2):
                    f = n * 2 + s
                    dve.wait_ge(ca.sem, ca.base + n * 2)

                    def tap(j):
                        return taps[:, ds(f + j * 6, 1)]
                    dve.tensor_scalar(acc[s], v.fm[:, ds(f * T + F0, T)], tap(2), None, ALU.mult).then_inc(ch.sem, ch.up())
                    dve.wait_ge(ch.sem, ch.count())
                    for q, j in enumerate((0, 1, 3, 4)):
                        o = j - 2
                        for a0, b0 in segs:
                            a, b = max(a0, a0 - o), min(b0, b0 - o)
                            x = dve.scalar_tensor_tensor(out=acc[s][:, a:b], in0=v.fm[:, ds(f * T + (F0 + a + o), b - a)],
                                                         scalar=tap(j), in1=acc[s][:, a:b], op0=ALU.mult, op1=ALU.add)
                        if q < 3:
                            x.then_inc(ch.sem, ch.up())
                            dve.wait_ge(ch.sem, ch.count())
                    x.then_inc(cv.sem, cv.step(f"s{s}"))
            dve.wait_ge(ce.sem, ce.count("s1", NC - 1))
            qk = mv.qkv.rearrange("p (t c) -> p t c", t=NT)[:, :, 0:512]
            dve.tensor_tensor(sq, qk, qk, ALU.mult).then_inc(ch.sem, ch.up())
            dve.wait_ge(ch.sem, ch.count())
            dve.tensor_reduce(inv, sq.rearrange("p t (h n) -> p (t h) n", n=HD), AX.X, ALU.add).then_inc(ch.sem, ch.up())
            dve.wait_ge(ch.sem, ch.count())
            dve.tensor_scalar(inv, inv, 1e-12, None, ALU.add).then_inc(dve_s.sem, dve_s.step("sums"))
            dve.wait_ge(act_s.sem, act_s.count("root"))
            dve.reciprocal(inv, inv).then_inc(ch.sem, ch.up())
            dve.wait_ge(ch.sem, ch.count())
            dve.tensor_scalar(t8(inv)[:, :, 0:4], t8(inv)[:, :, 0:4], HD ** -0.5, None, ALU.mult).then_inc(ch.sem, ch.up())
            dve.wait_ge(ch.sem, ch.count())
            for t in range(NT):
                w = mv.qkv[:, t * 3 * W:t * 3 * W + 512].rearrange("p (h n) -> p h n", n=HD)
                x = dve.tensor_tensor(w, w, inv[:, t * 8:t * 8 + 8].unsqueeze(2).broadcast_to([P, 8, HD]), ALU.mult)
            x.then_inc(ch.sem, ch.up())
            dve.wait_ge(ch.sem, ch.count())
            dve.tensor_tensor(t8(sp8[0]), ab[:, :, 0:8], sm.dt.unsqueeze(1).broadcast_to([P, NT, 8]), ALU.add).then_inc(ch.sem, ch.up())
            dve.wait_ge(ch.sem, ch.count())
            dve.scalar_tensor_tensor(out=sp8[1], in0=sp8[0], scalar=-1.0, in1=sp8[0], op0=ALU.mult, op1=ALU.max).then_inc(dve_s.sem, dve_s.step("arg"))
            dve.wait_ge(act_s.sem, act_s.count("exps"))
            dve.tensor_scalar(sp8[2], sp8[1], 1.0, None, ALU.add).then_inc(dve_s.sem, dve_s.step("plus1"))
            dve.wait_ge(act_s.sem, act_s.count("log"))
            dve.scalar_tensor_tensor(out=sp8[0], in0=sp8[0], scalar=0.0, in1=sp8[2], op0=ALU.max, op1=ALU.add).then_inc(ch.sem, ch.up())
            dve.wait_ge(ch.sem, ch.count())
            dve.scalar_tensor_tensor(out=t8(sm.g), in0=t8(sp8[0]), scalar=-1.0,
                                                in1=sm.a_log.unsqueeze(1).broadcast_to([P, NT, 8]), op0=ALU.mult, op1=ALU.mult).then_inc(dve_s.sem, dve_s.step("g"))
            dve.wait_ge(pe_s.sem, pe_s.count("cums"))
            for d in range(2):
                dve.tensor_copy(t8(sm.gcum)[:, :, 4 * d:4 * d + 4], t8(core.wide[2][:, 64 * d:64 * d + 48])[:, :, 4 * d:4 * d + 4])
            dve.tensor_copy(sm.gtot, core.wide[2][:, 128:176]).then_inc(ch.sem, ch.up())
            dve.wait_ge(ch.sem, ch.count())
            dve.tensor_tensor(sm.e_rest, sm.gtot, sm.gcum, ALU.subtract).then_inc(dve_s.sem, dve_s.step("rest"))
            dve.wait_ge(act_s.sem, act_s.count("cums"))
    for s in (small_in, pe_s, act_s, dve_s):
        s.close()
    for s in (cv, ca, ctp, ce):
        s.close(NC)

    recurrence(core, v, "gdn")

    hi = Region(core, A_HT, A_PT)
    sq, gate = hi(NT, W), hi(NT, W)
    norm_g = hi(HD)
    ss = hi(NT * NH)
    o = v.mix[:, :, 512:512 + W]
    small_in = core.steps("gdn_norm_in", ["all"], 16)
    act_s = core.steps("scalar_steps", ["root", "gate"])
    dve_s = core.steps("vector_steps", ["mean"])
    with nc.Block() as block:
        @block.sync
        def _(sp):
            sp.dma_start(norm_g, io["gdn_norm"][i:i + 1, :].partition_broadcast(P)).then_inc(small_in.sem, 16)

        @block.scalar
        def _(act):
            act.wait_ge(dve_s.sem, dve_s.count("mean"))
            act.activation(ss, ss, ACT.Sqrt).then_inc(act_s.sem, act_s.step("root"))
            act.activation(gate, v.pt[:, :, GATE0:GATE0 + W], ACT.Silu).then_inc(act_s.sem, act_s.step("gate"))

        @block.vector
        def _(dve):
            ch = core.vchain
            dve.tensor_tensor(o, v.pt[:, :, V0:V0 + W], v.pt[:, :, V0 + W:V0 + 2 * W], ALU.add).then_inc(ch.sem, ch.up())
            dve.wait_ge(ch.sem, ch.count())
            dve.tensor_tensor(sq, o, o, ALU.mult).then_inc(ch.sem, ch.up())
            dve.wait_ge(ch.sem, ch.count())
            dve.tensor_reduce(ss, sq.rearrange("p t (h n) -> p (t h) n", n=HD), AX.X, ALU.add).then_inc(ch.sem, ch.up())
            dve.wait_ge(ch.sem, ch.count())
            dve.tensor_scalar(ss, ss, 1.0 / HD, EPS, ALU.mult, ALU.add).then_inc(dve_s.sem, dve_s.step("mean"))
            dve.wait_ge(act_s.sem, act_s.count("root"))
            dve.reciprocal(ss, ss).then_inc(ch.sem, ch.up())
            dve.wait_ge(ch.sem, ch.count())
            dve.wait_ge(act_s.sem, act_s.count("gate"))
            dve.tensor_tensor(o, o, gate, ALU.mult).then_inc(ch.sem, ch.up())
            dve.wait_ge(ch.sem, ch.count())
            dve.wait_ge(small_in.sem, small_in.count("all"))
            for t in range(NT):
                w = v.mix[:, t, 512:512 + W].rearrange("p (h n) -> p h n", h=NH)
                x = dve.tensor_tensor(w, w, ss[:, t * NH:(t + 1) * NH].unsqueeze(2).broadcast_to([P, NH, HD]), ALU.mult)
            x.then_inc(ch.sem, ch.up())
            dve.wait_ge(ch.sem, ch.count())
            for t in range(NT):
                w = v.mix[:, t, 512:512 + W].rearrange("p (h n) -> p h n", h=NH)
                x = dve.tensor_tensor(w, w, norm_g.unsqueeze(1).broadcast_to([P, NH, HD]), ALU.mult)
            x.then_inc(ch.sem, ch.up())
            dve.wait_ge(ch.sem, ch.count())
    for s in (small_in, act_s, dve_s):
        s.close()


def rwkv(core, v, io, i):
    nc = core.nc
    mv = MixerViews(core)
    lora = v.fm[:, 14 * T:15 * T]
    lo, hi = Region(core, A_WORK, A_END), Region(core, A_HT, A_PT)
    ups = lo(512)
    w0, a0, k_k, k_a = lo(512), lo(512), lo(W), lo(W)
    act_in = lo(T)
    pre = [[lo(512) for _ in range(2)] for _ in range(2)]
    inv = lo(NT * NH)
    sq = hi(NT, W)
    key = hi(NT * W)
    r_, k_, v_ = (v.pt[:, :, RKV0 + n * W:RKV0 + (n + 1) * W] for n in range(3))

    def t3(ap):
        return ap.rearrange("p (t n) -> p t n", t=NT)

    def row(name):
        return io[name][i:i + 1].rearrange("a b c -> a (b c)") if len(io[name].shape) == 3 else io[name][i:i + 1, :]

    small_in = core.steps("rwkv_small_in", ["all"], 16 * 7)
    lora_s = core.steps("scalar_steps", ["tanh", "root"])
    mm = core.steps("lora_up", [f"{a}{t}" for t in range(NT) for a in "wa"])
    add = core.steps("lora_biased", ["mean"] + [f"{a}{t}" for t in range(NT) for a in "wa"])
    sg = core.steps("lora_sigmoid", [f"{a}{t}" for t in range(NT) for a in "wa"])
    with nc.Block() as block:
        @block.sync
        def _(sp):
            for dst, src in ((ups[0:32, :].rearrange("p (d n) -> p d n", d=2), io["rwkv_w_up"][i].rearrange("d k n -> k d n")),
                             (ups[32:64, :].rearrange("p (d n) -> p d n", d=2), io["rwkv_a_up"][i].rearrange("d k n -> k d n")),
                             (ups[64:128, 0:W], io["rwkv_g_up"][i]),
                             (w0, row("rwkv_w0").partition_broadcast(P)), (a0, row("rwkv_a0").partition_broadcast(P)),
                             (k_k, row("rwkv_k_k").partition_broadcast(P)), (k_a, row("rwkv_k_a").partition_broadcast(P))):
                sp.dma_start(dst, src).then_inc(small_in.sem, 16)

        @block.tensor
        def _(pe):
            pe.wait_ge(small_in.sem, small_in.count("all"))
            pe.wait_ge(lora_s.sem, lora_s.count("tanh"))
            for t in range(NT):
                ts = slice(t * P, (t + 1) * P)
                if t >= 2:
                    pe.wait_ge(add.sem, add.count(f"w{t - 2}"))
                pe.matmul(core.bank[t % 2][:, :], act_in[0:32, ts], ups[0:32, :], start=True, stop=True).then_inc(mm.sem, mm.step(f"w{t}"))
                if t >= 2:
                    pe.wait_ge(add.sem, add.count(f"a{t - 2}"))
                pe.matmul(core.wide[t % 2][:, 0:512], act_in[32:64, ts], ups[32:64, :], start=True, stop=True).then_inc(mm.sem, mm.step(f"a{t}"))

        @block.scalar
        def _(act):
            act.activation(act_in[0:32, :], lora[0:32, :], ACT.Tanh)
            act.copy(act_in[32:64, :], lora[32:64, :]).then_inc(lora_s.sem, lora_s.step("tanh"))
            act.wait_ge(add.sem, add.count("mean"))
            act.activation(inv, inv, ACT.Sqrt).then_inc(lora_s.sem, lora_s.step("root"))
            for t in range(NT):
                for a, out, src in (("w", mv.sig_w, pre[t % 2][0]), ("a", mv.kk_a, pre[t % 2][1])):
                    act.wait_ge(add.sem, add.count(f"{a}{t}"))
                    act.activation(out[0][:, t * W:(t + 1) * W], src[:, 0:W], ACT.Sigmoid)
                    act.activation(out[1][:, t * W:(t + 1) * W], src[:, W:512], ACT.Sigmoid).then_inc(sg.sem, sg.step(f"{a}{t}"))

        @block.vector
        def _(dve):
            ch = core.vchain
            dve.wait_ge(small_in.sem, small_in.count("all"))

            def over_tiles(ap):
                return ap.unsqueeze(1).broadcast_to([P, NT, W])
            dve.tensor_tensor(t3(mv.kk), k_, over_tiles(k_k), ALU.mult).then_inc(ch.sem, ch.up())
            dve.wait_ge(ch.sem, ch.count())
            dve.tensor_tensor(sq, t3(mv.kk), t3(mv.kk), ALU.mult).then_inc(ch.sem, ch.up())
            dve.wait_ge(ch.sem, ch.count())
            dve.tensor_reduce(inv, sq.rearrange("p t (h n) -> p (t h) n", n=HD), AX.X, ALU.add).then_inc(ch.sem, ch.up())
            dve.wait_ge(ch.sem, ch.count())
            dve.tensor_scalar(inv, inv, 1e-12, None, ALU.add).then_inc(add.sem, add.step("mean"))
            for t in range(NT):
                if t >= 2:
                    dve.wait_ge(sg.sem, sg.count(f"a{t - 2}"))
                dve.wait_ge(mm.sem, mm.count(f"w{t}"))
                dve.tensor_tensor(pre[t % 2][0], core.bank[t % 2][:, :], w0, ALU.add).then_inc(add.sem, add.step(f"w{t}"))
                dve.wait_ge(mm.sem, mm.count(f"a{t}"))
                dve.tensor_tensor(pre[t % 2][1], core.wide[t % 2][:, 0:512], a0, ALU.add).then_inc(add.sem, add.step(f"a{t}"))
            dve.wait_ge(lora_s.sem, lora_s.count("root"))
            dve.reciprocal(inv, inv).then_inc(ch.sem, ch.up())
            dve.wait_ge(ch.sem, ch.count())
            kk = mv.kk.rearrange("p (g n) -> p g n", n=HD)
            dve.tensor_tensor(kk, kk, inv.unsqueeze(2).broadcast_to([P, NT * NH, HD]), ALU.mult).then_inc(ch.sem, ch.up())
            dve.wait_ge(ch.sem, ch.count())
            dve.wait_ge(sg.sem, sg.count(f"a{NT - 1}"))
            dve.tensor_tensor(t3(key), k_, over_tiles(k_a), ALU.mult).then_inc(ch.sem, ch.up())
            dve.wait_ge(ch.sem, ch.count())
            for d in range(2):
                dve.scalar_tensor_tensor(out=mv.kd[d], in0=mv.kk_a[d], scalar=-1.0, in1=key, op0=ALU.add, op1=ALU.mult).then_inc(ch.sem, ch.up())
                dve.wait_ge(ch.sem, ch.count())
                dve.tensor_tensor(t3(mv.kd[d]), t3(mv.kd[d]), k_, ALU.add)
                x = dve.tensor_tensor(mv.kk_a[d], mv.kk_a[d], mv.kk, ALU.mult)
            x.then_inc(ch.sem, ch.up())
            dve.wait_ge(ch.sem, ch.count())
    for s in (small_in, lora_s, mm, add, sg):
        s.close()

    recurrence(core, v, "rwkv")

    lo, hi = Region(core, A_WORK, A_END), Region(core, A_HT, A_PT)
    g_up, sig_g = lo(W), lo(T)
    r_k, gn_w, gn_b = lo(W), lo(W), lo(W)
    mu, ss, bon = lo(NT * NH), lo(NT * NH), lo(NT * NH)
    y, tmp, bonus = hi(NT * W), hi(NT * W), hi(NT * W)
    out = v.mix[:, :, 768:1024]
    small_in = core.steps("rwkv_norm_in", ["all"], 16 * 4)
    act_s = core.steps("scalar_steps", ["sigmoid", "root"])
    dve_s = core.steps("vector_steps", ["mean"])
    g_mm = core.steps("lora_up", [f"g{t}" for t in range(NT)])
    g_ev = core.steps("lora_biased", [f"g{t}" for t in range(NT)])

    def groups(ap):
        return ap.rearrange("p (g n) -> p g n", n=HD)

    def per_group(ap):
        return ap.unsqueeze(2).broadcast_to([P, NT * NH, HD])

    def over_tiles(ap):
        return ap.unsqueeze(1).broadcast_to([P, NT, W])

    def r_v(t):
        return v.pt[:, t, RKV0 + 2 * W:RKV0 + 3 * W].rearrange("p (h n) -> p h n", h=NH)

    with nc.Block() as block:
        @block.sync
        def _(sp):
            for dst, src in ((g_up[64:128, :], io["rwkv_g_up"][i]), (r_k, row("rwkv_r_k").partition_broadcast(P)),
                             (gn_w, row("rwkv_gn_w").partition_broadcast(P)), (gn_b, row("rwkv_gn_b").partition_broadcast(P))):
                sp.dma_start(dst, src).then_inc(small_in.sem, 16)

        @block.tensor
        def _(pe):
            pe.wait_ge(small_in.sem, small_in.count("all"))
            pe.wait_ge(act_s.sem, act_s.count("sigmoid"))
            for t in range(NT):
                if t >= 2:
                    pe.wait_ge(g_ev.sem, g_ev.count(f"g{t - 2}"))
                pe.matmul(core.bank[t % 2][:, 0:W], sig_g[64:128, t * P:(t + 1) * P], g_up[64:128, :], start=True, stop=True).then_inc(g_mm.sem, g_mm.step(f"g{t}"))

        @block.scalar
        def _(act):
            act.activation(sig_g[64:128, :], lora[64:128, :], ACT.Sigmoid).then_inc(act_s.sem, act_s.step("sigmoid"))
            act.wait_ge(dve_s.sem, dve_s.count("mean"))
            act.activation(ss, ss, ACT.Sqrt).then_inc(act_s.sem, act_s.step("root"))

        @block.vector
        def _(dve):
            ch = core.vchain
            dve.wait_ge(small_in.sem, small_in.count("all"))
            dve.tensor_tensor(t3(y), v.pt[:, :, V0:V0 + W], v.pt[:, :, V0 + W:V0 + 2 * W], ALU.add)
            dve.tensor_tensor(tmp, mv.kd[0], mv.kd[1], ALU.add).then_inc(ch.sem, ch.up())
            dve.wait_ge(ch.sem, ch.count())
            dve.tensor_reduce(mu, groups(y), AX.X, ALU.add).then_inc(ch.sem, ch.up())
            dve.wait_ge(ch.sem, ch.count())
            dve.tensor_tensor(t3(tmp), t3(tmp), r_, ALU.mult).then_inc(ch.sem, ch.up())
            dve.wait_ge(ch.sem, ch.count())
            dve.tensor_scalar(mu, mu, 1.0 / HD, None, ALU.mult)
            dve.tensor_tensor(t3(tmp), t3(tmp), over_tiles(r_k), ALU.mult).then_inc(ch.sem, ch.up())
            dve.wait_ge(ch.sem, ch.count())
            dve.tensor_reduce(bon, groups(tmp), AX.X, ALU.add).then_inc(ch.sem, ch.up())
            dve.wait_ge(ch.sem, ch.count())
            dve.tensor_tensor(groups(y), groups(y), per_group(mu), ALU.subtract).then_inc(ch.sem, ch.up())
            dve.wait_ge(ch.sem, ch.count())
            dve.tensor_tensor(tmp, y, y, ALU.mult).then_inc(ch.sem, ch.up())
            dve.wait_ge(ch.sem, ch.count())
            dve.tensor_reduce(ss, groups(tmp), AX.X, ALU.add).then_inc(ch.sem, ch.up())
            dve.wait_ge(ch.sem, ch.count())
            dve.tensor_scalar(ss, ss, 1.0 / HD, GN_EPS, ALU.mult, ALU.add).then_inc(dve_s.sem, dve_s.step("mean"))
            for t in range(NT):
                b = bonus[:, t * W:(t + 1) * W].rearrange("p (h n) -> p h n", h=NH)
                x = dve.tensor_tensor(b, r_v(t), bon[:, t * NH:(t + 1) * NH].unsqueeze(2).broadcast_to([P, NH, HD]), ALU.mult)
            x.then_inc(ch.sem, ch.up())
            dve.wait_ge(ch.sem, ch.count())
            dve.tensor_tensor(t3(bonus), t3(bonus), over_tiles(gn_b), ALU.add).then_inc(ch.sem, ch.up())
            dve.wait_ge(ch.sem, ch.count())
            dve.wait_ge(act_s.sem, act_s.count("root"))
            dve.reciprocal(ss, ss).then_inc(ch.sem, ch.up())
            dve.wait_ge(ch.sem, ch.count())
            dve.tensor_tensor(groups(y), groups(y), per_group(ss), ALU.mult).then_inc(ch.sem, ch.up())
            dve.wait_ge(ch.sem, ch.count())
            dve.tensor_tensor(t3(y), t3(y), over_tiles(gn_w), ALU.mult).then_inc(ch.sem, ch.up())
            dve.wait_ge(ch.sem, ch.count())
            dve.tensor_tensor(y, y, bonus, ALU.add).then_inc(ch.sem, ch.up())
            dve.wait_ge(ch.sem, ch.count())
            for t in range(NT):
                dve.wait_ge(g_mm.sem, g_mm.count(f"g{t}"))
                dve.tensor_tensor(v.mix[:, t, 768:1024], core.bank[t % 2][:, 0:W], y[:, t * W:(t + 1) * W], ALU.mult).then_inc(g_ev.sem, g_ev.step(f"g{t}"))
            dve.wait_ge(g_ev.sem, g_ev.count(f"g{NT - 1}"))

    for s in (small_in, act_s, dve_s, g_mm, g_ev):
        s.close()


def gate_rows(core, v, j, streams, region):
    rows = {c: region(D) for c in streams}
    col = region(KD, P)
    g_v = core.steps("gate_spread", [f"c{c}" for c in streams])
    g_mm = core.steps("gate_rows", [f"c{c}" for c in streams])
    g_ev = core.steps("gate_copied", [f"c{c}" for c in streams])

    def dve_part(dve):
        for n, c in enumerate(streams):
            if n:
                dve.wait_ge(g_mm.sem, g_mm.count(f"c{streams[n - 1]}"))
            for k in range(KD):
                x = dve.tensor_scalar(col[:, k, :], v.ones, v.gate[:, j, c, k:k + 1], None, ALU.mult)
            x.then_inc(g_v.sem, g_v.step(f"c{c}"))

    def pe_part(pe):
        for n, c in enumerate(streams):
            pe.wait_ge(g_v.sem, g_v.count(f"c{c}"))
            if n:
                pe.wait_ge(g_ev.sem, g_ev.count(f"c{streams[n - 1]}"))
            for k in range(KD):
                x = pe.matmul(core.wide[2][:, k * P:(k + 1) * P], col[:, k, :], v.ident, start=True, stop=True)
            x.then_inc(g_mm.sem, g_mm.step(f"c{c}"))

    def act_part(act):
        for c in streams:
            act.wait_ge(g_mm.sem, g_mm.count(f"c{c}"))
            act.copy(rows[c], core.wide[2][:, :]).then_inc(g_ev.sem, g_ev.step(f"c{c}"))

    def ready(eng):
        eng.wait_ge(g_ev.sem, g_ev.count(f"c{streams[-1]}"))

    def close():
        for s in (g_v, g_mm, g_ev):
            s.close()

    return rows, dve_part, pe_part, act_part, ready, close


def post_norm(core, v, tiles, rows, region):
    junk, tmp = [region(D) for _ in range(2)], [region(D) for _ in range(2)]
    n = len(tiles)
    y_mm = core.steps("y_product", [f"t{q}" for q in range(n)])
    y_a = core.steps("y_scalar", [f"{a}{q}" for q in range(n) for a in ("square", "root")])
    y_v = core.steps("y_vector", [f"{a}{q}" for q in range(n) for a in ("mean", "scaled")])
    done = core.steps("x_updated", ["all"])

    def act_part(act):
        for q, t in enumerate(tiles):
            act.wait_ge(y_mm.sem, y_mm.count(f"t{q}"))
            if q >= 2:
                act.wait_ge(y_a.sem, y_a.count(f"square{q - 2}"))
            act.activation(junk[q % 2], core.wide[q % 3][:, :], ACT.Square, accum_out=v.stat[:, t:t + 1]).then_inc(y_a.sem, y_a.step(f"square{q}"))
            act.wait_ge(y_v.sem, y_v.count(f"mean{q}"))
            act.activation(v.std[:, t:t + 1], v.stat[:, t:t + 1], ACT.Sqrt).then_inc(y_a.sem, y_a.step(f"root{q}"))

    def dve_part(dve):
        ch = core.vchain
        for q, t in enumerate(tiles):
            dve.wait_ge(y_a.sem, y_a.count(f"square{q}"))
            dve.tensor_scalar(v.stat[:, t:t + 1], v.stat[:, t:t + 1], 1.0 / D, EPS, ALU.mult, ALU.add).then_inc(y_v.sem, y_v.step(f"mean{q}"))
            dve.wait_ge(y_a.sem, y_a.count(f"root{q}"))
            dve.reciprocal(v.rstd[:, t:t + 1], v.std[:, t:t + 1]).then_inc(ch.sem, ch.up())
            dve.wait_ge(ch.sem, ch.count())
            dve.scalar_tensor_tensor(out=tmp[q % 2], in0=core.wide[q % 3][:, :], scalar=v.rstd[:, t:t + 1],
                                              in1=rows[stream(t)], op0=ALU.mult, op1=ALU.mult).then_inc(y_v.sem, y_v.step(f"scaled{q}"))
            dve.wait_ge(y_v.sem, y_v.count(f"scaled{q}"))
            x = dve.tensor_tensor(v.x[:, t, :], v.x[:, t, :], tmp[q % 2], ALU.add)
            if q < n - 1:
                x.then_inc(ch.sem, ch.up())
                dve.wait_ge(ch.sem, ch.count())
        x.then_inc(done.sem, done.step("all"))
        dve.wait_ge(done.sem, done.count("all"))

    def before_product(pe, q):
        if q >= 3:
            pe.wait_ge(y_v.sem, y_v.count(f"scaled{q - 3}"))

    def close():
        for s in (y_mm, y_a, y_v, done):
            s.close()

    return y_mm, act_part, dve_part, before_product, close


def merge(core, v, io, i, last):
    nc = core.nc
    tiles = list(range(CT, NT)) if last else list(range(NT))
    n = len(tiles)
    r = Region(core, A_PT, A_MIX)
    w = r(KD, D)
    rows, dve_g, pe_g, act_g, g_ready, g_close = gate_rows(core, v, 0, [0] if last else [0, 1], r)
    y_mm, act_y, dve_y, before_product, y_close = post_norm(core, v, tiles, rows, r)
    w_in = core.steps("slot_in0", ["w"], 16)
    tr = core.steps("norm_transposed", [f"t{q}" for q in range(n)])
    eva = core.steps("norm_evac_scalar", [f"t{q}" for q in range(n)])
    evv = core.steps("norm_evac_vector", [f"t{q}" for q in range(n)])
    H = KD // 2
    with nc.Block() as block:
        @block.sync
        def _(sp):
            sp.dma_start(w, io["w_out"][i].rearrange("(k p) n -> p k n", p=P)).then_inc(w_in.sem, w_in.step("w"))

        @block.tensor
        def _(pe):
            pe_g(pe)
            for q, t in enumerate(tiles):
                if q >= 2:
                    pe.wait_ge(eva.sem, eva.count(f"t{q - 2}"))
                    pe.wait_ge(evv.sem, evv.count(f"t{q - 2}"))
                for k in range(KD):
                    x = pe.transpose(core.wide[q % 2][:, k * P:(k + 1) * P], v.mix[:, t, k * P:(k + 1) * P], v.ident)
                x.then_inc(tr.sem, tr.step(f"t{q}"))
            pe.wait_ge(eva.sem, eva.count(f"t{n - 1}"))
            pe.wait_ge(evv.sem, evv.count(f"t{n - 1}"))
            g_ready(pe)
            pe.wait_ge(w_in.sem, w_in.count("w"))
            for q, t in enumerate(tiles):
                before_product(pe, q)
                for half in range(2):
                    for k in range(KD):
                        x = pe.matmul(core.wide[q % 3][:, half * 512:(half + 1) * 512], v.ht[:, k, t * P:(t + 1) * P],
                                      w[:, k, half * 512:(half + 1) * 512], start=(k == 0), stop=(k == KD - 1))
                x.then_inc(y_mm.sem, y_mm.step(f"t{q}"))

        def copied(eng_copy, q, odd):
            t = tiles[q]
            return eng_copy(v.ht[:, H * odd:H * odd + H, t * P:(t + 1) * P],
                            core.wide[q % 2][:, 512 * odd:512 * odd + 512].rearrange("p (k n) -> p k n", n=P))

        @block.scalar
        def _(act):
            act_g(act)
            for q in range(n):
                act.wait_ge(tr.sem, tr.count(f"t{q}"))
                copied(act.copy, q, 1).then_inc(eva.sem, eva.step(f"t{q}"))
            act_y(act)

        @block.vector
        def _(dve):
            dve_g(dve)
            for q in range(n):
                dve.wait_ge(tr.sem, tr.count(f"t{q}"))
                copied(dve.tensor_copy, q, 0).then_inc(evv.sem, evv.step(f"t{q}"))
            g_ready(dve)
            dve_y(dve)
    for s in (w_in, tr, eva, evv):
        s.close()
    g_close()
    y_close()


class MoeViews:

    def __init__(self, core, v):
        self.rank_t = v.small[:, 0:NT * NE]
        self.weight = v.small[:, NT * NE:2 * NT * NE]
        r = Region(core, A_HT, A_END)
        self.out = r(12 * D)
        self.rank = r(T)
        self.rest = r.at


def route(core, v, io, i, last):
    nc = core.nc
    mo = MoeViews(core, v)
    tiles = list(range(CT, NT)) if last else list(range(NT))
    n, lo = len(tiles), tiles[0]
    act_n, dve_n, pe_n, ready, close = normed_transposed(core, v, 1, tiles, mo.rest, (h_t := core.view(mo.rest + 3 * D, KD, T)))
    r = Region(core, mo.rest + 3 * D + KD * T, A_END)
    router = r(KD, NE)
    aff = r(NT * NE)
    aff_t, work, taken, ones = r(T), r(T), r(T), r(T)
    mx, sm = r(NT), r(NT)
    best = r(8)
    w_in = core.steps("slot_in0", ["w"], 16)
    pe_s = core.steps("tensor_steps", ["logits", "aff_t", "rank_t"])
    act_s = core.steps("scalar_steps", ["exp", "aff_t"])
    dve_s = core.steps("vector_steps", ["shifted", "aff", "rank"])
    segs = ([] if last else [(0, CT * P, SLOT_C)]) + [(CT * P, T, SLOT_L)]
    cols = slice(lo * NE, NT * NE)

    def t3(ap):
        return ap[:, cols].rearrange("p (t e) -> p t e", e=NE)

    with nc.Block() as block:
        @block.sync
        def _(sp):
            sp.dma_start(router, io["moe_router"][i].rearrange("(k p) e -> p k e", p=P)).then_inc(w_in.sem, w_in.step("w"))

        @block.tensor
        def _(pe):
            pe_n(pe)
            ready(pe)
            pe.wait_ge(w_in.sem, w_in.count("w"))
            for t in tiles:
                for k in range(KD):
                    x = pe.matmul(core.bank[0][:, t * NE:(t + 1) * NE], h_t[:, k, t * P:(t + 1) * P], router[:, k, :],
                                  start=(k == 0), stop=(k == KD - 1))
            x.then_inc(pe_s.sem, pe_s.step("logits"))
            pe.wait_ge(dve_s.sem, dve_s.count("aff"))
            for t in tiles:
                x = pe.transpose(core.wide[2][0:NE, t * P:(t + 1) * P], aff[:, t * NE:(t + 1) * NE], v.ident)
            x.then_inc(pe_s.sem, pe_s.step("aff_t"))
            pe.wait_ge(dve_s.sem, dve_s.count("rank"))
            for t in tiles:
                x = pe.transpose(core.bank[1][:, t * NE:(t + 1) * NE], mo.rank[0:NE, t * P:(t + 1) * P], v.ident[0:NE, 0:NE])
            x.then_inc(pe_s.sem, pe_s.step("rank_t"))

        @block.scalar
        def _(act):
            act_n(act)
            act.wait_ge(dve_s.sem, dve_s.count("shifted"))
            act.activation(aff[:, cols], aff[:, cols], ACT.Exp).then_inc(act_s.sem, act_s.step("exp"))
            act.wait_ge(pe_s.sem, pe_s.count("aff_t"))
            act.copy(aff_t[0:NE, lo * P:T], core.wide[2][0:NE, lo * P:T]).then_inc(act_s.sem, act_s.step("aff_t"))

        @block.vector
        def _(dve):
            ch = core.vchain
            dve_n(dve)
            dve.memset(ones[0:NE, :], 1.0)
            dve.wait_ge(pe_s.sem, pe_s.count("logits"))
            dve.tensor_reduce(mx[:, lo:], t3(core.bank[0]), AX.X, ALU.max).then_inc(ch.sem, ch.up())
            dve.wait_ge(ch.sem, ch.count())
            dve.tensor_tensor(t3(aff), t3(core.bank[0]), mx[:, lo:].unsqueeze(2).broadcast_to([P, n, NE]), ALU.subtract).then_inc(dve_s.sem, dve_s.step("shifted"))
            dve.wait_ge(act_s.sem, act_s.count("exp"))
            dve.tensor_reduce(sm[:, lo:], t3(aff), AX.X, ALU.add).then_inc(ch.sem, ch.up())
            dve.wait_ge(ch.sem, ch.count())
            dve.reciprocal(sm[:, lo:], sm[:, lo:]).then_inc(ch.sem, ch.up())
            dve.wait_ge(ch.sem, ch.count())
            dve.tensor_tensor(t3(aff), t3(aff), sm[:, lo:].unsqueeze(2).broadcast_to([P, n, NE]), ALU.mult).then_inc(dve_s.sem, dve_s.step("aff"))
            dve.wait_ge(dve_s.sem, dve_s.count("aff"))
            dve.tensor_tensor(t3(mo.weight), t3(aff), v.std[:, lo:NT].unsqueeze(2).broadcast_to([P, n, NE]), ALU.mult)
            dve.wait_ge(act_s.sem, act_s.count("aff_t"))
            dve.tensor_copy(work[0:NE, lo * P:T], aff_t[0:NE, lo * P:T]).then_inc(ch.sem, ch.up())
            dve.wait_ge(ch.sem, ch.count())
            for a, b, cap in segs:
                for _ in range(cap // 8):
                    dve.max(best[0:NE, :], work[0:NE, a:b]).then_inc(ch.sem, ch.up())
                    dve.wait_ge(ch.sem, ch.count())
                    dve.match_replace(out=work[0:NE, a:b], in_to_replace=best[0:NE, :], in_values=work[0:NE, a:b], imm_value=-1.0).then_inc(ch.sem, ch.up())
                    dve.wait_ge(ch.sem, ch.count())
            dve.tensor_scalar(taken[0:NE, lo * P:T], work[0:NE, lo * P:T], 0.0, None, ALU.is_lt).then_inc(ch.sem, ch.up())
            dve.wait_ge(ch.sem, ch.count())
            for a, b, cap in segs:
                x = dve.tensor_tensor_scan(work[0:NE, a:b], ones[0:NE, a:b], taken[0:NE, a:b], 0.0, ALU.mult, ALU.add)
            x.then_inc(ch.sem, ch.up())
            dve.wait_ge(ch.sem, ch.count())
            dve.tensor_tensor(mo.rank[0:NE, lo * P:T], work[0:NE, lo * P:T], taken[0:NE, lo * P:T], ALU.mult).then_inc(dve_s.sem, dve_s.step("rank"))
            dve.wait_ge(pe_s.sem, pe_s.count("rank_t"))
            dve.tensor_copy(mo.rank_t[:, cols], core.bank[1][:, cols]).then_inc(ch.sem, ch.up())
            dve.wait_ge(ch.sem, ch.count())
    close()
    for s in (w_in, pe_s, act_s, dve_s):
        s.close()


def experts(core, v, io, i, last):
    nc = core.nc
    mo = MoeViews(core, v)
    tiles = list(range(CT, NT)) if last else list(range(NT))
    r = Region(core, mo.rest, A_END)
    wg, wu, wd = (r(KD, D) for _ in range(3))
    take = r(NT, SLOTS)
    xe, hid = r(KD, SLOTS), r(KD, SLOTS)
    wcol, wslot = r(NT), r(2)
    S = SLOT_L if last else SLOTS
    G = 4
    parts = [(0, CT, NT, 0, SLOT_L)] + ([] if last else [(1, 0, CT, SLOT_L, SLOTS)])
    names = [f"e{e}" for e in range(G)]
    in_ = {a: core.steps(f"expert_{a}_in", ["w"], 16) for a in ("gate", "up", "down")}
    g_mm, u_mm, d_mm, x_mm = (core.steps(f"expert_{a}", names) for a in ("gate", "up", "down", "gathered"))
    tk = core.steps("expert_slots", ["zero"])
    sel = core.steps("expert_selected", names)
    mod = core.steps("expert_modulated", names)
    silu = core.steps("expert_silu", names)
    hd = core.steps("expert_hidden", names)
    kept = core.steps("expert_kept", [f"e{e}h{h}" for e in range(G) for h in range(2)])
    NG = NE // G

    def before(s, eng, g, e):
        if e:
            eng.wait_ge(s.sem, s.count(names[e - 1], g))
        else:
            eng.wait_ge(s.sem, s.base + g * G)

    def w_of(name, e):
        return io[name][i].rearrange("e (k p) n -> e p k n", p=P)[ds(e, 1)].rearrange("e p k n -> p (e k) n")

    def psum3(bank):
        return bank[:, :].rearrange("p (k s) -> p k s", s=P)

    with nc.Block() as block:
        @block.sync
        def _(sp):
            with sp.Fori(0, NG) as g:
                for e in range(G):
                    for a, buf, src, used in (("gate", wg, "moe_w_gate", g_mm), ("up", wu, "moe_w_up", u_mm), ("down", wd, "moe_w_down", d_mm)):
                        before(used, sp, g, e)
                        sp.dma_start(buf, w_of(src, g * G + e)).then_inc(in_[a].sem, 16)

        def arrived(eng, a, g, e):
            eng.wait_ge(in_[a].sem, g * (16 * G) + (in_[a].base + 16 * (e + 1)))

        @block.tensor
        def _(pe):
            xp, gp, up = (psum3(w) for w in core.wide)

            def gather(g, e):
                pe.wait_ge(sel.sem, sel.count(names[e], g))
                before(mod, pe, g, e)
                for _, t0, t1, s0, s1 in parts:
                    for k in range(KD):
                        for t in range(t0, t1):
                            pe.matmul(xp[:, k, s0:s1], v.x[:, t, k * P:(k + 1) * P], take[:, t, s0:s1], start=(t == t0), stop=(t == t1 - 1))
                for t in tiles:
                    x = pe.matmul(xp[0:S, 0, SLOTS:SLOTS + 1], take[:, t, 0:S], wcol[:, t:t + 1], start=(t == tiles[0]), stop=(t == NT - 1))
                x.then_inc(x_mm.sem, x_mm.step(names[e]))

            def hidden(g, e):
                for a, buf, out, steps in (("gate", wg, gp, g_mm), ("up", wu, up, u_mm)):
                    arrived(pe, a, g, e)
                    if a == "gate":
                        pe.wait_ge(mod.sem, mod.count(names[e], g))
                        before(silu, pe, g, e)
                    else:
                        before(hd, pe, g, e)
                    for f in range(KD):
                        for k in range(KD):
                            x = pe.matmul(out[:, f, 0:S], buf[:, k, f * P:(f + 1) * P], xe[:, k, 0:S], start=(k == 0), stop=(k == KD - 1))
                    x.then_inc(steps.sem, steps.step(names[e]))

            def down(g, e):
                arrived(pe, "down", g, e)
                pe.wait_ge(hd.sem, hd.count(names[e], g))
                if e:
                    pe.wait_ge(kept.sem, kept.count(f"e{e - 1}h1", g))
                else:
                    pe.wait_ge(kept.sem, kept.base + g * (2 * G))
                for h in range(2):
                    for k in range(KD):
                        x = pe.matmul(core.bank[h][0:S, :], hid[:, k, 0:S], wd[:, k, h * 512:(h + 1) * 512], start=(k == 0), stop=(k == KD - 1))
                x.then_inc(d_mm.sem, d_mm.step(names[e]))

            with pe.Fori(0, NG) as g:
                for e in range(G):
                    gather(g, e)
                    hidden(g, e)
                    down(g, e)

        @block.scalar
        def _(act):
            with act.Fori(0, NG) as g:
                for e in range(G):
                    act.wait_ge(g_mm.sem, g_mm.count(names[e], g))
                    before(d_mm, act, g, e)
                    act.activation(hid[:, :, 0:S], psum3(core.wide[1])[:, :, 0:S], ACT.Silu).then_inc(silu.sem, silu.step(names[e]))
                    act.wait_ge(d_mm.sem, d_mm.count(names[e], g))
                    for h in range(2):
                        p0 = SLOT_L * (e % 2)
                        x = act.activation(mo.out[p0:p0 + SLOT_L, ds((g * 2 + e // 2) * D + h * 512, 512)], core.bank[h][0:SLOT_L, :],
                                           ACT.Copy, scale=wslot[0:SLOT_L, 0:1])
                        if not last:
                            c0 = SLOT_C * e
                            x = act.activation(mo.out[c0:c0 + SLOT_C, ds((g + 8) * D + h * 512, 512)], core.bank[h][SLOT_L:SLOTS, :],
                                               ACT.Copy, scale=wslot[SLOT_L:SLOTS, 0:1])
                        x.then_inc(kept.sem, kept.step(f"e{e}h{h}"))

        @block.vector
        def _(dve):
            ch = core.vchain
            dve.memset(take[:, :, :], 0.0).then_inc(tk.sem, tk.step("zero"))
            dve.wait_ge(tk.sem, tk.count("zero"))
            with ch.loop(dve, NG, G) as g:
                for e in range(G):
                    ex = g * G + e
                    before(x_mm, dve, g, e)
                    for c, t0, t1, s0, s1 in parts:
                        for t in range(t0, t1):
                            dve.tensor_scalar(take[:, t, s0:s1], v.const[:, IOTA:IOTA + s1 - s0], mo.rank_t[:, ds(ex + t * NE, 1)],
                                              v.rstd[:, t:t + 1], ALU.is_equal, ALU.mult)
                    dve.tensor_copy(wcol[:, tiles[0]:NT], mo.weight[:, ds(ex, NE * (NT - 1) + 1)][:, ::NE][:, tiles[0]:NT]).then_inc(sel.sem, sel.step(names[e]))
                    dve.wait_ge(x_mm.sem, x_mm.count(names[e], g))
                    before(u_mm, dve, g, e)
                    xp = psum3(core.wide[0])
                    for c, t0, t1, s0, s1 in parts:
                        x = dve.tensor_tensor(xe[:, :, s0:s1], xp[:, :, s0:s1], v.scale[:, 1, c, :].unsqueeze(2).broadcast_to([P, KD, s1 - s0]), ALU.mult)
                    x.then_inc(ch.sem, ch.up())
                    dve.wait_ge(ch.sem, ch.count())
                    if e:
                        dve.wait_ge(kept.sem, kept.count(f"e{e - 1}h1", g))
                    else:
                        dve.wait_ge(kept.sem, kept.base + g * (2 * G))
                    dve.tensor_copy(wslot[0:S, 0:1], xp[0:S, 0, SLOTS:SLOTS + 1])
                    for c, t0, t1, s0, s1 in parts:
                        x = dve.tensor_tensor(xe[:, :, s0:s1], xe[:, :, s0:s1], v.mod[:, 24:32, c].unsqueeze(2).broadcast_to([P, KD, s1 - s0]), ALU.add)
                    x.then_inc(mod.sem, mod.step(names[e]))
                    dve.wait_ge(silu.sem, silu.count(names[e], g))
                    dve.wait_ge(u_mm.sem, u_mm.count(names[e], g))
                    dve.tensor_tensor(hid[:, :, 0:S], hid[:, :, 0:S], psum3(core.wide[2])[:, :, 0:S], ALU.mult).then_inc(hd.sem, hd.step(names[e]))
    for s in (g_mm, u_mm, d_mm, x_mm, sel, mod, silu, hd, kept):
        s.close(NG)
    for s in in_.values():
        s.close(NE)
    tk.close()


def combine(core, v, io, i, last):
    nc = core.nc
    mo = MoeViews(core, v)
    tiles = list(range(CT, NT)) if last else list(range(NT))
    r = Region(core, mo.rest, A_END)
    put = {q: r(LT * P if q < 8 else CT * P) for q in range(8 if last else 12)}
    rows, dve_g, pe_g, act_g, g_ready, g_close = gate_rows(core, v, 1, [0] if last else [0, 1], r)
    y_mm, act_y, dve_y, before_product, y_close = post_norm(core, v, tiles, rows, r)
    sp_mm = core.steps("rank_spread", [f"q{q}" for q in put])
    eq = core.steps("slots_matched", [f"q{q}" for q in put])

    def span(q):
        return (CT * P, T) if q < 8 else (0, CT * P)

    with nc.Block() as block:
        @block.tensor
        def _(pe):
            pe_g(pe)
            for q in put:
                a, b = span(q)
                if q >= 2:
                    pe.wait_ge(eq.sem, eq.count(f"q{q - 2}"))
                pe.matmul(core.bank[q % 2][:, 0:b - a], v.const[0:NE, SELW + q * P:SELW + (q + 1) * P], mo.rank[0:NE, a:b],
                                     start=True, stop=True).then_inc(sp_mm.sem, sp_mm.step(f"q{q}"))
            pe.wait_ge(eq.sem, eq.count(f"q{max(put)}"))
            g_ready(pe)
            for n, t in enumerate(tiles):
                before_product(pe, n)
                qs = range(8) if t >= CT else range(8, 12)
                c = (t - CT if t >= CT else t) * P
                for half in range(2):
                    for q in qs:
                        x = pe.matmul(core.wide[n % 3][:, half * 512:(half + 1) * 512], put[q][:, c:c + P],
                                      mo.out[:, q * D + half * 512:q * D + half * 512 + 512], start=(q == qs[0]), stop=(q == qs[-1]))
                x.then_inc(y_mm.sem, y_mm.step(f"t{n}"))

        @block.scalar
        def _(act):
            act_g(act)
            act_y(act)

        @block.vector
        def _(dve):
            dve_g(dve)
            for q in put:
                a, b = span(q)
                col = COLS + (2 if q < 8 else 3)
                dve.wait_ge(sp_mm.sem, sp_mm.count(f"q{q}"))
                dve.tensor_scalar(put[q], core.bank[q % 2][:, 0:b - a], v.const[:, col:col + 1], None, ALU.is_equal).then_inc(eq.sem, eq.step(f"q{q}"))
            g_ready(dve)
            dve_y(dve)
    for s in (sp_mm, eq):
        s.close()
    g_close()
    y_close()


def store_result(core, v, out):
    stored = core.steps("stored", ["all"], 16)
    with core.nc.Block() as block:
        @block.sync
        def _(sp):
            sp.dma_start(out.rearrange("(t p) d -> p t d", p=P), v.x[:, CT:NT, :]).then_inc(stored.sem, stored.step("all"))
            sp.wait_ge(stored.sem, stored.count("all"))


def trunk(nc, io, out, stop=None):
    with ExitStack() as ctx:
        core = Core(nc, ctx)
        v = Views(core)
        load_start(core, v, io)
        for i in range(DEPTH):
            last = i == DEPTH - 1
            for name, part in PHASES:
                part(core, v, io, i, last) if part in WITH_LAST else part(core, v, io, i)
                if stop == (i, name):
                    return
        store_result(core, v, out)


PHASES = [("mod", modulation), ("proj", projections), ("att", attention), ("gdn", gdn), ("rwkv", rwkv),
          ("merge", merge), ("route", route), ("experts", experts), ("moe", combine)]
WITH_LAST = (attention, merge, route, experts, combine)


def constants():
    import numpy as np

    c = np.zeros((P, NCONST2), np.float32)
    p, f = np.arange(P)[:, None], np.arange(P)[None, :]
    c[:, IDENT:IDENT + P] = p == f
    c[:, UPS:UPS + P] = f > p
    c[:, UPI:UPI + P] = f >= p
    c[:, LOS:LOS + P] = f < p
    c[:, LOI:LOI + P] = f <= p
    first, second = (p < HD).astype(np.float32), (p >= HD).astype(np.float32)
    c[:, CUI:CUI + P] = (f >= p) - first
    c[:, CUS:CUS + P] = (f > p) - first
    c[:, CLI:CLI + P] = (f <= p) - second
    c[:, CLS:CLS + P] = (f < p) - second
    low = f % 32 < 16
    c[:, ROT:ROT + P] = np.where(low, -1.0 * (p == f + 16), 1.0 * (p == f - 16))
    c[:, ONES:ONES + P] = 1.0
    c[:, COLS:COLS + 1] = first
    c[:, COLS + 1:COLS + 2] = second
    c[:, COLS + 2:COLS + 3] = p % SLOT_L + 1
    c[:, COLS + 3:COLS + 4] = p % SLOT_C + 1
    c[:, IOTA:IOTA + 64] = np.arange(64)[None, :] + 1
    tok = np.arange(512)
    freqs = (np.float32(10000.0) ** (-np.arange(16, dtype=np.float32) / np.float32(16))).astype(np.float32)
    dim = np.arange(P) % HD
    pos = np.where((dim // 32)[:, None] == 0, (tok // 64)[None, :], (tok % 64)[None, :]).astype(np.float32)
    ang = pos * freqs[dim % 16][:, None]
    c[:, COS:COS + 512] = np.cos(ang)
    c[:, SIN:SIN + 512] = np.sin(ang)
    same = p // 32 == f // 32
    c[:, DLO:DLO + P], c[:, DUP:DUP + P] = (f < p) & same, (f > p) & same
    c[:, OLO:OLO + P], c[:, OUP:OUP + P] = (f < p) & ~same, (f > p) & ~same
    for t in range(8):
        c[:NE, SELW + t * P:SELW + (t + 1) * P] = np.arange(NE)[:, None] == 2 * t + np.arange(P)[None, :] // SLOT_L
    for t in range(4):
        c[:NE, SELW + (8 + t) * P:SELW + (9 + t) * P] = np.arange(NE)[:, None] == 4 * t + np.arange(P)[None, :] // SLOT_C
    return c


_PLAIN = ["c", "c_ctx", "w_mod", "b_mod", "norm_pre", "norm_post", "w_out", "da_lambda", "da_norm", "gdn_conv",
          "gdn_a_log", "gdn_dt_bias", "gdn_norm", "rwkv_w0", "rwkv_w_up", "rwkv_a0", "rwkv_a_up", "rwkv_g_up",
          "rwkv_k_k", "rwkv_k_a", "rwkv_r_k", "rwkv_gn_w", "rwkv_gn_b", "moe_router", "moe_w_gate", "moe_w_up",
          "moe_w_down"]


def layouts(inputs):
    import numpy as np

    a = {n: np.ascontiguousarray(inputs[n]) for n in _PLAIN}
    a["x"] = np.ascontiguousarray(inputs["x"])[0]
    a["ctx"] = np.ascontiguousarray(inputs["ctx"])[0]
    w = np.ascontiguousarray(inputs["w_in"])
    fm = np.concatenate([w[..., 0:1024], w[..., 1536:2304], w[..., 3344:3472]], -1)
    tm = np.concatenate([w[..., 1024:1536], w[..., 2304:2576], w[..., 2576:3344]], -1)

    def tiles(m, n):
        return np.ascontiguousarray(
            m.reshape(DEPTH, KD, P, m.shape[-1] // n, n).transpose(0, 2, 3, 1, 4).reshape(DEPTH, P, -1))

    a["w_fm"], a["w_tm"] = tiles(fm, P), tiles(tm, TMW)
    a["consts"] = constants()
    return a


def kernel(**inputs):
    import numpy as _np
    import concourse.bacc as _bacc
    from concourse import mybir as _mybir
    from concourse.bass_utils import run_bass_kernel_spmd as _run

    nc = _bacc.Bacc("TRN2", target_bir_lowering=False, num_devices=1)
    arrays = {f"in_{n}": a for n, a in layouts(inputs).items()}
    io = {n[3:]: nc.dram_tensor(n, a.shape, _mybir.dt.from_np(a.dtype), kind="ExternalInput").ap()
          for n, a in arrays.items()}
    out = nc.dram_tensor("out_0", (LT * P, D), _mybir.dt.float32, kind="ExternalOutput").ap()
    trunk(nc, io, out)
    r = _run(nc, [arrays], core_ids=[0])
    return _np.asarray(r.results[0]["out_0"]).reshape(1, LT * P, D)
```

```python
from contextlib import ExitStack, contextmanager

import concourse.bass as bass
from concourse import mybir

F32 = mybir.dt.float32
ALU = mybir.AluOpType
ACT = mybir.ActivationFunctionType
AX = mybir.AxisListType
ds = bass.ds

P = 128
D = 1024
KD = D // P
CT, LT = 2, 4
NT = CT + LT
T = NT * P
EPS = 1e-6
DEPTH = 2
HD = 64
NH = 4
W = NH * HD
FMT = 15
TMS, TMW = 4, 388
V0, GATE0, AB0, RKV0 = 0, 512, 768, 784
NE = 16
SLOT_L, SLOT_C = 64, 32
SLOTS = SLOT_L + SLOT_C
DECAY = 0.6065306597126334
GN_EPS = 64e-5

IDENT, UPS, UPI, LOS, LOI, CUI, CUS, CLI, CLS, ROT = (P * i for i in range(10))
ONES = P * 10
COLS = P * 11
IOTA = COLS + 4
COS = IOTA + 64
SIN = COS + 512
NCONST = SIN + 512
DLO, DUP, OLO, OUP = (NCONST + P * i for i in range(4))
SELW = NCONST + 4 * P
NCONST2 = SELW + 12 * P


class Steps:

    def __init__(self, sem, names, by=1):
        self.sem, self.names, self.by, self.base, self.at = sem, names, by, 0, 0

    def step(self, name):
        assert self.names[self.at % len(self.names)] == name, (name, self.names[self.at % len(self.names)])
        self.at += 1
        return self.by

    def count(self, name, turn=0):
        return turn * (len(self.names) * self.by) + (self.base + (self.names.index(name) + 1) * self.by)

    def close(self, turns=1):
        assert self.at % len(self.names) == 0, (self.names, self.at)
        self.at = 0
        self.owner["count"] = self.base + turns * len(self.names) * self.by


class Chain:

    def __init__(self, sem):
        self.sem, self.n, self.i, self.per = sem, 0, None, 0

    def up(self):
        self.n += 1
        return 1

    def count(self):
        return self.n if self.i is None else self.i * self.per + self.n

    @contextmanager
    def loop(self, eng, count, per):
        start = self.n
        with eng.Fori(0, count) as i:
            self.i, self.per = i, per
            yield i
        assert self.n - start == per, f"counted per pass: {self.n - start}, said {per}"
        self.i, self.n = None, start + count * per


PRIMED = ["slot_used", "mod_copied", "proj_tile", "proj_slab", "proj_tile_out0", "proj_tile_out1", "proj_tile_out2", "proj_slab_scalar",
          "proj_slab_vector", "scores", "probs", "difference_transposed", "difference_copied", "att_out", "att_out_copied",
          "conv_silu", "conv_transposed", "conv_copied", "mixer_vector0", "mixer_vector1", "mixer_scalar0", "mixer_scalar1",
          "expert_gate", "expert_up", "expert_down", "expert_gathered", "expert_modulated", "expert_silu", "expert_hidden",
          "expert_kept"]


class Core:

    def __init__(self, nc, ctx):
        self.nc, self.ctx, self.signals = nc, ctx, {}
        self.size = 52180
        self.big = ctx.enter_context(nc.sbuf_tensor("sbuf_all", [P, self.size], F32))
        self.bank = [ctx.enter_context(nc.psum_tensor(f"bank{i}", [P, 512], F32)) for i in range(2)]
        self.wide = [ctx.enter_context(nc.psum_tensor(f"wide{i}", [P, 1024], F32)) for i in range(3)]
        for name in PRIMED:
            self.signals[name] = ctx.enter_context(nc.semaphore(name)), {"count": 1}
        self.vchain = Chain(ctx.enter_context(nc.semaphore("vector_chain")))
        self.achain = Chain(ctx.enter_context(nc.semaphore("scalar_chain")))

    def steps(self, name, names, by=1):
        if name not in self.signals:
            self.signals[name] = self.ctx.enter_context(self.nc.semaphore(name)), {}
        sem, kinds = self.signals[name]
        s = Steps(sem, names, by)
        s.base = kinds.get("count", 0)
        s.owner = kinds
        return s

    def view(self, at, *shape):
        n = 1
        for s in shape:
            n *= s
        assert at + n <= self.size, (at, shape)
        v = self.big[:, at:at + n]
        if len(shape) == 2:
            v = v.rearrange("p (a b) -> p a b", a=shape[0])
        if len(shape) == 3:
            v = v.rearrange("p (a b c) -> p a b c", a=shape[0], b=shape[1])
        return v


class Region:

    def __init__(self, core, at, end):
        self.core, self.at, self.end = core, at, end

    def __call__(self, *shape):
        n = 1
        for s in shape:
            n *= s
        v = self.core.view(self.at, *shape)
        self.at += n
        assert self.at <= self.end, ("region full", self.at, self.end)
        return v


A_CONST, A_FVEC, A_X, A_HT = 0, 4608, 5376, 11520
A_PT = A_HT + KD * T
A_FM = A_PT + NT * TMS * TMW
A_MIX = A_FM + FMT * T
A_WORK = A_MIX + NT * D
A_END = 52180


class Views:

    def __init__(self, core):
        self.const = core.view(A_CONST, NCONST2)
        self.ident = self.const[:, IDENT:IDENT + P]
        self.ones = self.const[:, ONES:ONES + P]
        self.x = core.view(A_X, NT, D)
        self.ht = core.view(A_HT, KD, T)
        self.pt = core.view(A_PT, NT, TMS * TMW)
        self.fm = core.view(A_FM, FMT * T)
        self.mix = core.view(A_MIX, NT, D)
        r = Region(core, A_FVEC, A_X)
        self.rows_t = r(96)
        self.mod = r(48, 2)
        self.cond = r(KD, 2)
        self.scale = r(2, 2, KD)
        self.gate = r(2, 2, KD)
        self.stat = r(NT)
        self.rstd = r(NT)
        self.std = r(NT)
        self.lam = r(8)
        self.small = r(464)


def load_start(core, v, io):
    nc = core.nc
    came = core.steps("start_loaded", ["all"], 48)
    with nc.Block() as block:
        @block.sync
        def _(sp):
            for name in PRIMED:
                sp.sem_inc(core.signals[name][0], 1)
            sp.dma_start(v.const[:, :], io["consts"]).then_inc(came.sem, 16)
            sp.dma_start(v.x[:, 0:CT, :], io["ctx"].rearrange("(t p) d -> p t d", p=P)).then_inc(came.sem, 16)
            sp.dma_start(v.x[:, CT:NT, :], io["x"].rearrange("(t p) d -> p t d", p=P)).then_inc(came.sem, 16)
            sp.wait_ge(came.sem, came.count("all"))
    came.owner["count"] = came.base + 48


def modulation(core, v, io, i):
    nc = core.nc
    r = Region(core, A_PT, A_MIX)
    SL = 4
    slot = [r(KD, 512) for _ in range(SL)]
    rows = Region(core, A_WORK, A_END)(P)
    rows_in = core.steps("mod_rows_in", ["all"], 80)
    w_in = [core.steps(f"slot_in{s}", ["w"], 16) for s in range(SL)]
    w_used = core.steps("slot_used", [f"w{s}" for s in range(SL)])
    pe_s = core.steps("tensor_steps", ["rows_t", "mod_t"])
    act_s = core.steps("scalar_steps", ["rows_t", "cond0", "cond1"])
    N = 12 // SL
    chunk = [core.bank[0][0:2, :], core.bank[1][0:2, :], core.wide[0][0:2, 0:512], core.wide[1][0:2, 0:512]]
    copied = core.steps("mod_copied", [f"w{s}" for s in range(SL)])
    by_row = core.view(A_MIX, 6 * D)
    with nc.Block() as block:
        @block.sync
        def _(sp):
            for at, src in ((0, io["b_mod"][i].rearrange("(r n) -> r n", n=P)),
                            (48, io["norm_pre"][i].rearrange("j (r n) -> (j r) n", n=P)),
                            (64, io["norm_post"][i].rearrange("j (r n) -> (j r) n", n=P)),
                            (80, io["c"].rearrange("a (r n) -> (a r) n", n=P)),
                            (88, io["c_ctx"].rearrange("(r n) -> r n", n=P))):
                sp.dma_start(rows[at:at + src.shape[0], :], src).then_inc(rows_in.sem, 16)
            with sp.Fori(0, N) as n:
                for s in range(SL):
                    sp.wait_ge(w_used.sem, w_used.base + n * SL)
                    sp.dma_start(
                        slot[s], io["w_mod"][i].rearrange("(k p) n -> p k n", p=P)[:, :, ds((n * SL + s) * 512, 512)]).then_inc(w_in[s].sem, w_in[s].step("w"))

        @block.tensor
        def _(pe):
            pe.wait_ge(rows_in.sem, rows_in.count("all"))
            pe.transpose(core.wide[2][:, 0:96], rows[0:96, :], v.ident[0:96, 0:96]).then_inc(pe_s.sem, pe_s.step("rows_t"))
            pe.wait_ge(act_s.sem, act_s.count("cond1"))
            with pe.Fori(0, N) as n:
                for s in range(SL):
                    pe.wait_ge(w_in[s].sem, w_in[s].count("w", n))
                    pe.wait_ge(copied.sem, copied.base + n * SL)
                    for k in range(KD):
                        last = pe.matmul(chunk[s], v.cond[:, k, :], slot[s][:, k, :], start=(k == 0), stop=(k == KD - 1))
                    last.then_inc(w_used.sem, w_used.step(f"w{s}"))
            pe.wait_ge(copied.sem, copied.count(f"w{SL - 1}", N - 1))
            for f in range(6 * KD):
                last = pe.transpose(core.wide[2][:, 2 * f:2 * f + 2], by_row[0:2, f * P:(f + 1) * P], v.ident[0:2, 0:2])
            last.then_inc(pe_s.sem, pe_s.step("mod_t"))

        @block.scalar
        def _(act):
            act.wait_ge(pe_s.sem, pe_s.count("rows_t"))
            act.copy(v.rows_t, core.wide[2][:, 0:96]).then_inc(act_s.sem, act_s.step("rows_t"))
            act.wait_ge(act_s.sem, act_s.count("rows_t"))
            act.activation(v.cond[:, :, 0], v.rows_t[:, 80:88], ACT.Silu).then_inc(act_s.sem, act_s.step("cond0"))
            act.activation(v.cond[:, :, 1], v.rows_t[:, 88:96], ACT.Silu).then_inc(act_s.sem, act_s.step("cond1"))
            with act.Fori(0, N) as n:
                for s in range(SL):
                    act.wait_ge(w_used.sem, w_used.count(f"w{s}", n))
                    act.copy(by_row[0:2, ds((n * SL + s) * 512, 512)], chunk[s]).then_inc(copied.sem, copied.step(f"w{s}"))

        @block.vector
        def _(dve):
            ch = core.vchain
            dve.wait_ge(act_s.sem, act_s.count("rows_t"))
            dve.wait_ge(pe_s.sem, pe_s.count("mod_t"))
            dve.tensor_tensor(v.mod[:, :, :], core.wide[2][:, 0:12 * KD].rearrange("p (a b) -> p a b", b=2),
                                           v.rows_t[:, 0:48].unsqueeze(2).broadcast_to([P, 48, 2]), ALU.add).then_inc(ch.sem, ch.up())
            dve.wait_ge(ch.sem, ch.count())
            for j in range(2):
                for c in range(2):
                    dve.scalar_tensor_tensor(out=v.scale[:, j, c, :], in0=v.mod[:, 24 * j + 8:24 * j + 16, c], scalar=1.0,
                                             in1=v.rows_t[:, 48 + 8 * j:56 + 8 * j], op0=ALU.add, op1=ALU.mult)
                    last = dve.tensor_tensor(v.gate[:, j, c, :], v.mod[:, 24 * j + 16:24 * j + 24, c],
                                             v.rows_t[:, 64 + 8 * j:72 + 8 * j], ALU.mult)
            last.then_inc(ch.sem, ch.up())
            dve.wait_ge(ch.sem, ch.count())
    for s in (rows_in, pe_s, act_s):
        s.close()
    w_used.close(N)
    copied.close(N)
    for s in w_in:
        s.close(N)


def stream(t):
    return 1 if t < CT else 0


def normed_transposed(core, v, j, tiles, w_start, dst):
    r = Region(core, w_start, w_start + 3 * D)
    junk, xn = r(D), [r(D), r(D)]
    n = len(tiles)
    sq = core.steps("norm_scalar", ["squares", "root"])
    ms = core.steps("norm_vector", ["mean", "rstd"] + [f"xn{t}" for t in range(n)])
    tr = core.steps("norm_transposed", [f"t{t}" for t in range(n)])
    eva = core.steps("norm_evac_scalar", [f"t{t}" for t in range(n)])
    evv = core.steps("norm_evac_vector", [f"t{t}" for t in range(n)])
    lo, hi = tiles[0], tiles[-1] + 1

    def evac(eng, steps, q, odd):
        t = tiles[q]
        c = stream(t)
        eng.wait_ge(tr.sem, tr.count(f"t{q}"))
        for k in range(4 * odd, 4 * odd + 4):
            out, src = dst[:, k, t * P:(t + 1) * P], core.wide[q % 2][:, k * P:(k + 1) * P]
            a, b = v.scale[:, j, c, k:k + 1], v.mod[:, 24 * j + k, c:c + 1]
            if odd:
                last = eng.activation(out, src, ACT.Identity, bias=b, scale=a)
            else:
                last = eng.tensor_scalar(out, src, a, b, ALU.mult, ALU.add)
        last.then_inc(steps.sem, steps.step(f"t{q}"))

    def act_part(act):
        for t in tiles:
            ins = act.activation(junk, v.x[:, t, :], ACT.Square, accum_out=v.stat[:, t:t + 1])
            if t < tiles[-1]:
                ins.then_inc(core.achain.sem, core.achain.up())
                act.wait_ge(core.achain.sem, core.achain.count())
        ins.then_inc(sq.sem, sq.step("squares"))
        act.wait_ge(ms.sem, ms.count("mean"))
        act.activation(v.std[:, lo:hi], v.stat[:, lo:hi], ACT.Sqrt).then_inc(sq.sem, sq.step("root"))
        for q in range(n):
            evac(act, eva, q, 1)

    def dve_part(dve):
        dve.wait_ge(sq.sem, sq.count("squares"))
        dve.tensor_scalar(v.stat[:, lo:hi], v.stat[:, lo:hi], 1.0 / D, EPS, ALU.mult, ALU.add).then_inc(ms.sem, ms.step("mean"))
        dve.wait_ge(sq.sem, sq.count("root"))
        dve.reciprocal(v.rstd[:, lo:hi], v.std[:, lo:hi]).then_inc(ms.sem, ms.step("rstd"))
        dve.wait_ge(ms.sem, ms.count("rstd"))
        for q, t in enumerate(tiles):
            if q >= 2:
                dve.wait_ge(tr.sem, tr.count(f"t{q - 2}"))
            dve.tensor_scalar(xn[q % 2], v.x[:, t, :], v.rstd[:, t:t + 1], None, ALU.mult).then_inc(ms.sem, ms.step(f"xn{q}"))
            if q >= 1:
                evac(dve, evv, q - 1, 0)
        evac(dve, evv, n - 1, 0)

    def pe_part(pe):
        for q in range(n):
            pe.wait_ge(ms.sem, ms.count(f"xn{q}"))
            if q >= 2:
                pe.wait_ge(eva.sem, eva.count(f"t{q - 2}"))
                pe.wait_ge(evv.sem, evv.count(f"t{q - 2}"))
            for k in range(KD):
                last = pe.transpose(core.wide[q % 2][:, k * P:(k + 1) * P], xn[q % 2][:, k * P:(k + 1) * P], v.ident)
            last.then_inc(tr.sem, tr.step(f"t{q}"))

    def ready(eng):
        eng.wait_ge(eva.sem, eva.count(f"t{n - 1}"))
        eng.wait_ge(evv.sem, evv.count(f"t{n - 1}"))

    def close():
        for s in (sq, ms, tr, eva, evv):
            s.close()

    return act_part, dve_part, pe_part, ready, close


def projections(core, v, io, i):
    nc = core.nc
    rm, rw = Region(core, A_MIX, A_WORK), Region(core, A_WORK, A_END)
    SF, ST = 3, 2
    act_n, dve_n, pe_n, ready, close = normed_transposed(core, v, 0, list(range(NT)), rm.at, v.ht)
    rm.at += 3 * D
    fslot = [rm(KD, P) for _ in range(SF)]
    tslot = [rw(KD, TMW) for _ in range(ST)]
    f_in = [core.steps(f"slot_in{s}", ["w"], 16) for s in range(SF)]
    t_in = [core.steps(f"slab_in{s}", ["w"], 16) for s in range(ST)]
    f_mm = core.steps("proj_tile", [f"s{s}" for s in range(SF)])
    t_mm = core.steps("proj_slab", [f"s{s}t{t}" for s in range(ST) for t in range(NT)])
    f_ev = [core.steps(f"proj_tile_out{s}", ["out"]) for s in range(SF)]
    t_eva = core.steps("proj_slab_scalar", [f"s{s}t{t}" for s in range(ST) for t in range(0, NT, 2)])
    t_evv = core.steps("proj_slab_vector", [f"s{s}t{t}" for s in range(ST) for t in range(1, NT, 2)])
    NF, NS = FMT // SF, TMS // ST
    wf, wt = io["w_fm"][i], io["w_tm"][i]

    def slab_psum(t):
        return core.wide[t // 2][:, (t % 2) * 512:(t % 2) * 512 + TMW]

    with nc.Block() as block:
        @block.sync
        def _(sp):
            with sp.Fori(0, NF) as n:
                for s in range(SF):
                    sp.wait_ge(f_mm.sem, f_mm.base + n * SF)
                    sp.dma_start(fslot[s].rearrange("p k n -> p (k n)"), wf[:, ds((n * SF + s) * KD * P, KD * P)]).then_inc(f_in[s].sem, f_in[s].step("w"))

        @block.gpsimd
        def _(pool):
            with pool.Fori(0, NS) as n:
                for s in range(ST):
                    pool.wait_ge(t_mm.sem, t_mm.base + n * (ST * NT))
                    pool.dma_start(tslot[s].rearrange("p k n -> p (k n)"), wt[:, ds((n * ST + s) * KD * TMW, KD * TMW)]).then_inc(t_in[s].sem, t_in[s].step("w"))

        @block.tensor
        def _(pe):
            pe_n(pe)
            ready(pe)
            with pe.Fori(0, NF) as n:
                for s in range(SF):
                    pe.wait_ge(f_in[s].sem, f_in[s].count("w", n))
                    pe.wait_ge(f_ev[s].sem, f_ev[s].base + n)
                    for half, (a, b) in enumerate(((0, 512), (512, T))):
                        for k in range(KD):
                            last = pe.matmul(core.wide[s][:, a:b], fslot[s][:, k, :], v.ht[:, k, a:b],
                                             start=(k == 0), stop=(k == KD - 1))
                    last.then_inc(f_mm.sem, f_mm.step(f"s{s}"))
            for s in range(SF):
                pe.wait_ge(f_ev[s].sem, f_ev[s].count("out", NF - 1))
            with pe.Fori(0, NS) as n:
                for s in range(ST):
                    pe.wait_ge(t_in[s].sem, t_in[s].count("w", n))
                    for t in range(NT):
                        ev, per = (t_evv, NT // 2 * ST) if t % 2 else (t_eva, NT // 2 * ST)
                        if s == 0:
                            pe.wait_ge(ev.sem, ev.base + n * per)
                        else:
                            pe.wait_ge(ev.sem, ev.count(f"s0t{t}", n))
                        for k in range(KD):
                            last = pe.matmul(slab_psum(t), v.ht[:, k, t * P:(t + 1) * P], tslot[s][:, k, :],
                                             start=(k == 0), stop=(k == KD - 1))
                        last.then_inc(t_mm.sem, t_mm.step(f"s{s}t{t}"))

        @block.scalar
        def _(act):
            act_n(act)
            with act.Fori(0, NF) as n:
                for s in (0, 2):
                    act.wait_ge(f_mm.sem, f_mm.count(f"s{s}", n))
                    act.copy(v.fm[:, ds((n * SF + s) * T, T)], core.wide[s][:, 0:T]).then_inc(f_ev[s].sem, f_ev[s].step("out"))
            with act.Fori(0, NS) as n:
                for s in range(ST):
                    for t in range(0, NT, 2):
                        act.wait_ge(t_mm.sem, t_mm.count(f"s{s}t{t}", n))
                        act.copy(v.pt[:, t, ds((n * ST + s) * TMW, TMW)], slab_psum(t)).then_inc(t_eva.sem, t_eva.step(f"s{s}t{t}"))

        @block.vector
        def _(dve):
            dve_n(dve)
            with dve.Fori(0, NF) as n:
                dve.wait_ge(f_mm.sem, f_mm.count("s1", n))
                dve.tensor_copy(v.fm[:, ds((n * SF + 1) * T, T)], core.wide[1][:, 0:T]).then_inc(f_ev[1].sem, f_ev[1].step("out"))
            with dve.Fori(0, NS) as n:
                for s in range(ST):
                    for t in range(1, NT, 2):
                        dve.wait_ge(t_mm.sem, t_mm.count(f"s{s}t{t}", n))
                        dve.tensor_copy(v.pt[:, t, ds((n * ST + s) * TMW, TMW)], slab_psum(t)).then_inc(t_evv.sem, t_evv.step(f"s{s}t{t}"))
    close()
    f_mm.close(NF)
    for s in f_in + f_ev:
        s.close(NF)
    for s in (t_mm, t_eva, t_evv, *t_in):
        s.close(NS)


def attention(core, v, io, i, last):
    import math

    nc = core.nc
    lam_init = 0.8 - 0.6 * math.exp(-0.3 * i)
    SC = HD ** -0.5
    tiles = list(range(CT, NT)) if last else list(range(NT))
    NU = len(tiles)
    lat0, NL = CT * P, LT * P
    r = Region(core, A_HT, A_PT)
    k_h = r(T)
    q_m = r(2, T)
    prob = [r(2, T) for _ in range(2)]
    w = Region(core, A_WORK, A_END)
    diff_t = [w(T) for _ in range(2)]
    diff = [w(T) for _ in range(2)]
    rot = [w(NL) for _ in range(2)]
    cosd = w(NL)
    lamv, lamp, norm_g = w(256), w(2, HD), w(P)
    lam = v.lam[:, 0:1]

    stat = v.small[:, 0:24].rearrange("p (b s) -> p b s", b=2)
    group = v.small[:, 32:56]
    group2 = v.small[:, 64:88]
    small_in = core.steps("att_small_in", ["all"], 32)
    rope_mm = core.steps("rope_rotated", ["q", "k"])
    rope_a = core.steps("rope_context", ["q", "k"])
    rope_v = core.steps("rope_done", ["q", "k"])
    U = range(NU)
    s_mm = core.steps("scores", [f"u{u}" for u in U])
    mx = core.steps("score_max", [f"u{u}" for u in U])
    ex = core.steps("probs", [f"u{u}m{m}" for u in U for m in range(2)])
    df = core.steps("probs_difference", [f"u{u}" for u in U])
    tr = core.steps("difference_transposed", [f"u{u}" for u in U])
    te = core.steps("difference_copied", [f"u{u}" for u in U])
    o_mm = core.steps("att_out", [f"u{u}" for u in U])
    o_ev = core.steps("att_out_copied", [f"u{u}" for u in U])
    lam_a = core.steps("scalar_steps", ["lambda", "root"])
    lam_v = core.steps("vector_steps", ["zero", "lambda", "mean"])

    def keys(t):
        return lat0 if t < CT else T

    with nc.Block() as block:
        @block.sync
        def _(sp):
            sp.dma_start(lamv, io["da_lambda"][i:i + 1].rearrange("a b c -> a (b c)").partition_broadcast(P)).then_inc(small_in.sem, 16)
            sp.dma_start(norm_g, io["da_norm"][i:i + 1, :].partition_broadcast(P)).then_inc(small_in.sem, 16)

        @block.tensor
        def _(pe):
            def transposed(u, h):
                pe.wait_ge(df.sem, df.count(f"u{u}", h))
                n = keys(tiles[u]) // P
                if u:
                    pe.wait_ge(te.sem, te.count(f"u{u - 1}", h))
                else:
                    pe.wait_ge(te.sem, te.base + h * NU)
                for k in range(n):
                    t = pe.transpose(core.wide[2][:, k * P:(k + 1) * P], diff[u % 2][:, k * P:(k + 1) * P], v.ident)
                t.then_inc(tr.sem, tr.step(f"u{u}"))
                pe.wait_ge(te.sem, te.count(f"u{u}", h))
                if u:
                    pe.wait_ge(o_ev.sem, o_ev.count(f"u{u - 1}", h))
                else:
                    pe.wait_ge(o_ev.sem, o_ev.base + h * NU)
                for k in range(n):
                    t = pe.matmul(core.bank[0][:, 0:P], diff_t[u % 2][:, k * P:(k + 1) * P],
                                  v.pt[:, k, ds(h * P + V0, P)], start=(k == 0), stop=(k == n - 1))
                t.then_inc(o_mm.sem, o_mm.step(f"u{u}"))

            with pe.Fori(0, NH) as h:
                pe.wait_ge(te.sem, te.base + h * NU)
                pe.matmul(core.wide[2][:, 0:512], v.const[:, ROT:ROT + P], v.fm[:, ds(h * T + lat0, NL)],
                                       start=True, stop=True).then_inc(rope_mm.sem, rope_mm.step("q"))
                pe.matmul(core.wide[2][:, 512:1024], v.const[:, ROT:ROT + P], v.fm[:, ds(h * T + (4 * T + lat0), NL)],
                                       start=True, stop=True).then_inc(rope_mm.sem, rope_mm.step("k"))
                pe.wait_ge(rope_v.sem, rope_v.count("k", h))
                pe.wait_ge(rope_a.sem, rope_a.count("k", h))
                for u, t in enumerate(tiles):
                    if u:
                        pe.wait_ge(ex.sem, ex.count(f"u{u - 1}m1", h))
                    else:
                        pe.wait_ge(ex.sem, ex.base + h * (2 * NU))
                    n = keys(t)
                    for m in range(2):
                        for lo in range(0, n, 512):
                            hi = min(lo + 512, n)
                            x = pe.matmul(core.wide[m][:, lo:hi], q_m[:, m, t * P:(t + 1) * P], k_h[:, lo:hi],
                                          start=True, stop=True)
                    x.then_inc(s_mm.sem, s_mm.step(f"u{u}"))
                    if u:
                        transposed(u - 1, h)
                transposed(NU - 1, h)

        @block.scalar
        def _(act):
            act.wait_ge(lam_v.sem, lam_v.count("lambda"))
            act.activation(v.lam[:, 2:4], v.lam[:, 2:4], ACT.Exp).then_inc(lam_a.sem, lam_a.step("lambda"))
            with act.Fori(0, NH) as h:
                act.wait_ge(s_mm.sem, s_mm.base + h * NU)
                for m in range(2):
                    rows = slice(m * HD, (m + 1) * HD)
                    x = act.copy(q_m[rows, m, 0:lat0], v.fm[rows, ds(h * T, lat0)])
                x.then_inc(rope_a.sem, rope_a.step("q"))
                act.copy(k_h[:, 0:lat0], v.fm[:, ds(h * T + 4 * T, lat0)]).then_inc(rope_a.sem, rope_a.step("k"))
                for u, t in enumerate(tiles):
                    n = keys(t)
                    act.wait_ge(mx.sem, mx.count(f"u{u}", h))
                    b = u % 2
                    for m in range(2):
                        act.activation(prob[b][:, m, 0:n], core.wide[m][:, 0:n], ACT.Exp, bias=stat[:, b, m:m + 1],
                                               scale=SC, accum_out=stat[:, b, 2 + m:3 + m]).then_inc(ex.sem, ex.step(f"u{u}m{m}"))
                    act.wait_ge(tr.sem, tr.count(f"u{u}", h))
                    if u >= 2:
                        act.wait_ge(o_mm.sem, o_mm.count(f"u{u - 2}", h))
                    else:
                        act.wait_ge(o_mm.sem, o_mm.base + h * NU)
                    act.copy(diff_t[b][:, 0:n], core.wide[2][:, 0:n]).then_inc(te.sem, te.step(f"u{u}"))
            act.wait_ge(lam_v.sem, lam_v.count("mean"))
            act.activation(group[:, tiles[0] * NH:], group[:, tiles[0] * NH:], ACT.Sqrt).then_inc(lam_a.sem, lam_a.step("root"))

        @block.vector
        def _(dve):
            ch = core.vchain
            dve.memset(q_m[:, :, :], 0.0).then_inc(lam_v.sem, lam_v.step("zero"))
            dve.wait_ge(lam_v.sem, lam_v.count("zero"))
            dve.wait_ge(small_in.sem, small_in.count("all"))
            for m in range(2):
                a = 2 * m * HD
                x = dve.tensor_tensor(lamp[:, m, :], lamv[:, a:a + HD], lamv[:, a + HD:a + 2 * HD], ALU.mult)
            x.then_inc(ch.sem, ch.up())
            dve.wait_ge(ch.sem, ch.count())
            dve.tensor_reduce(v.lam[:, 2:4], lamp, AX.X, ALU.add).then_inc(lam_v.sem, lam_v.step("lambda"))
            dve.wait_ge(lam_a.sem, lam_a.count("lambda"))
            dve.tensor_tensor(v.lam[:, 1:2], v.lam[:, 3:4], v.lam[:, 2:3], ALU.subtract).then_inc(ch.sem, ch.up())
            dve.wait_ge(ch.sem, ch.count())
            dve.tensor_scalar(lam, v.lam[:, 1:2], -lam_init, None, ALU.add).then_inc(ch.sem, ch.up())
            dve.wait_ge(ch.sem, ch.count())

            def out_copy(u, h):
                dve.wait_ge(o_mm.sem, o_mm.count(f"u{u}", h))
                dve.tensor_scalar(v.mix[:, tiles[u], ds(h * P, P)], core.bank[0][:, 0:P],
                                            stat[:, u % 2, 4:5], None, ALU.mult).then_inc(o_ev.sem, o_ev.step(f"u{u}"))

            with ch.loop(dve, NH, 4 + 3 * NU) as h:
                dve.wait_ge(s_mm.sem, s_mm.base + h * NU)
                cos, sin = v.const[:, COS:COS + NL], v.const[:, SIN:SIN + NL]
                for j, (nm, off) in enumerate((("q", 0), ("k", 4 * T))):
                    dve.wait_ge(rope_mm.sem, rope_mm.count(nm, h))
                    dve.tensor_tensor(rot[j], core.wide[2][:, 512 * j:512 * j + NL], sin, ALU.mult).then_inc(ch.sem, ch.up())
                    dve.wait_ge(ch.sem, ch.count())
                    turned = k_h[:, lat0:T] if nm == "k" else cosd
                    dve.tensor_tensor(turned, v.fm[:, ds(h * T + (off + lat0), NL)], cos, ALU.mult).then_inc(ch.sem, ch.up())
                    dve.wait_ge(ch.sem, ch.count())
                    if nm == "k":
                        x = dve.tensor_tensor(turned, turned, rot[j], ALU.add)
                    else:
                        for m in range(2):
                            rows = slice(m * HD, (m + 1) * HD)
                            x = dve.tensor_tensor(q_m[rows, m, lat0:T], turned[rows, :], rot[j][rows, :], ALU.add)
                    x.then_inc(rope_v.sem, rope_v.step(nm))
                for u, t in enumerate(tiles):
                    n, b = keys(t), u % 2
                    dve.wait_ge(s_mm.sem, s_mm.count(f"u{u}", h))
                    for m in range(2):
                        x = dve.tensor_reduce(stat[:, b, m:m + 1], core.wide[m][:, 0:n], AX.X, ALU.max)
                    x.then_inc(ch.sem, ch.up())
                    dve.wait_ge(ch.sem, ch.count())
                    if u:
                        out_copy(u - 1, h)
                    dve.tensor_scalar(stat[:, b, 0:2], stat[:, b, 0:2], -SC, None, ALU.mult).then_inc(mx.sem, mx.step(f"u{u}"))
                    dve.wait_ge(ex.sem, ex.count(f"u{u}m1", h))
                    dve.reciprocal(stat[:, b, 4:6], stat[:, b, 2:4]).then_inc(ch.sem, ch.up())
                    dve.wait_ge(ch.sem, ch.count())
                    dve.scalar_tensor_tensor(out=stat[:, b, 6:7], in0=stat[:, b, 2:3], scalar=stat[:, b, 5:6],
                                                          in1=lam, op0=ALU.mult, op1=ALU.mult).then_inc(ch.sem, ch.up())
                    dve.wait_ge(ch.sem, ch.count())
                    if u >= 2:
                        dve.wait_ge(tr.sem, tr.count(f"u{u - 2}", h))
                    else:
                        dve.wait_ge(tr.sem, tr.base + h * NU)
                    dve.scalar_tensor_tensor(out=diff[b][:, 0:n], in0=prob[b][:, 1, 0:n], scalar=stat[:, b, 6:7],
                                                     in1=prob[b][:, 0, 0:n], op0=ALU.mult, op1=ALU.add).then_inc(df.sem, df.step(f"u{u}"))
                out_copy(NU - 1, h)
            dve.wait_ge(o_ev.sem, o_ev.count(f"u{NU - 1}", NH - 1))
            lo = tiles[0]
            sq = core.view(A_FM, NT, NH, P)
            att = v.mix[:, lo:NT, 0:NH * P]
            dve.tensor_tensor(sq[:, lo:NT].rearrange("p t h n -> p t (h n)"), att, att, ALU.mult).then_inc(ch.sem, ch.up())
            dve.wait_ge(ch.sem, ch.count())
            dve.tensor_reduce(group[:, lo * NH:], sq[:, lo:NT].rearrange("p t h n -> p (t h) n"), AX.X, ALU.add).then_inc(ch.sem, ch.up())
            dve.wait_ge(ch.sem, ch.count())
            (dve.tensor_scalar(group, group, 1.0 / P, EPS, ALU.mult, ALU.add) if lo == 0 else
                       dve.tensor_scalar(group[:, lo * NH:], group[:, lo * NH:], 1.0 / P, EPS, ALU.mult, ALU.add)).then_inc(lam_v.sem, lam_v.step("mean"))
            dve.wait_ge(lam_a.sem, lam_a.count("root"))
            dve.reciprocal(group2[:, lo * NH:], group[:, lo * NH:]).then_inc(ch.sem, ch.up())
            dve.wait_ge(ch.sem, ch.count())
            for t in tiles:
                a = v.mix[:, t, 0:NH * P].rearrange("p (h n) -> p h n", h=NH)
                x = dve.tensor_tensor(a, a, group2[:, t * NH:(t + 1) * NH].unsqueeze(2).broadcast_to([P, NH, P]), ALU.mult)
            x.then_inc(ch.sem, ch.up())
            dve.wait_ge(ch.sem, ch.count())
            for t in tiles:
                a = v.mix[:, t, 0:NH * P].rearrange("p (h n) -> p h n", h=NH)
                x = dve.scalar_tensor_tensor(out=a, in0=a, scalar=1.0 - lam_init,
                                             in1=norm_g.unsqueeze(1).broadcast_to([P, NH, P]), op0=ALU.mult, op1=ALU.mult)
            x.then_inc(ch.sem, ch.up())
            dve.wait_ge(ch.sem, ch.count())
    for s in (small_in, lam_a, lam_v):
        s.close()
    for s in (rope_mm, rope_a, rope_v, s_mm, mx, ex, df, tr, te, o_mm, o_ev):
        s.close(NH)


PTW = TMS * TMW
SQUARES = 4
STEPS3 = 3


class Small:

    def __init__(self, v):
        n = NT * 8
        self.g, self.beta, self.gcum, self.gtot, self.e_cum, self.e_tot, self.e_rest = (
            v.small[:, k * n:(k + 1) * n] for k in range(7))
        self.a_log = v.small[:, 336:344]
        self.dt = v.small[:, 344:352]


class MixerViews:

    def __init__(self, core):
        self.qkv = core.view(A_FM, NT * 3 * W)
        self.rw = [core.view(A_FM + n * NT * W, NT * W) for n in range(7)]
        self.kk, self.sig_w, self.kk_a, self.kd = self.rw[0], self.rw[1:3], self.rw[3:5], self.rw[5:7]
        self.pt = core.view(A_PT, NT * PTW)


def recurrence(core, v, kind):
    nc = core.nc
    rwkv = kind == "rwkv"
    mv = MixerViews(core)
    sm = None if rwkv else Small(v)
    hi, lo = Region(core, A_HT, A_PT), Region(core, A_WORK, A_END)
    spare = Region(core, A_FM + NT * 3 * W, A_FM + 14 * T)
    R = range(2)
    ct, bt, kt, rt, l0, lt0, rb, rk, x, xt = ([r(512) for r in (hi, lo)] for _ in range(10))
    u, st = ([r(W) for r in (hi, lo)] for _ in range(2))
    pair = [hi(512), lo(512)]
    tm = [[pair[d][:, 0:W], lo(W), lo(W), pair[d][:, W:512]] for d in R]
    off = pair
    sz = [lo(W), v.small[:, 0:W]] if rwkv else st
    e_halves = [v.small[:, 256 + 16 * d:260 + 16 * d].rearrange("p (a c) -> p a c", c=2) for d in R]
    if not rwkv:
        g_rows, dif, e1, e2, e2s, e1f = ([spare(512) for _ in R] for _ in range(6))
    L, L_T = [(l0[d], ct[d]) for d in R], [(lt0[d], bt[d]) for d in R]
    inv_t = kt if rwkv else rt
    n_t = lt0
    sol = ct
    bank = [[core.bank[0][:, :], core.bank[1][:, :], core.wide[0][:, 0:512], core.wide[0][:, 512:1024]],
            [core.wide[1][:, 0:512], core.wide[1][:, 512:1024], core.wide[2][:, 0:512], core.wide[2][:, 512:1024]]]
    strict_st, incl_st = (UPS, LOS), (UPI, LOI)
    in_ts, in_st, off_ts = (DLO, DUP), (DUP, DLO), (OLO, OUP)
    cum_in, cum_ex = (CUI, CLI), (CUS, CLS)
    half_in, half_out = (0, 1), (1, 0)

    def mask(at):
        return v.const[:, at:at + P].unsqueeze(1).broadcast_to([P, NH, P])

    def heads(ap, n):
        return ap.rearrange("p (h n) -> p h n", n=n)

    def pairs(ap):
        return ap.rearrange("p (a n) -> p a n", n=P)

    def of_head(ap, b):
        return ap.rearrange("p (a b n) -> p a b n", a=2, b=2)[:, :, b, :]

    def one_head(ap, b):
        return of_head(ap, b)[:, :, b * HD:(b + 1) * HD]

    def xv_of(ap):
        return ap.rearrange("p (c h n) -> p c h n", c=2, h=NH)

    def xv(d):
        return xv_of(x[d])

    def of(flat, width, tile, at, n):
        return flat[:, ds(tile * width + at, n)]

    def per_head(flat, tile, d):
        return flat[:, ds(tile * 8 + d * 4, 4)]

    def over_pair(ap):
        return ap.unsqueeze(2).broadcast_to([P, 2, P])

    def spread(ap, m):
        return ap.unsqueeze(2).broadcast_to([ap.shape[0], NH, m])

    lev = ["sq1", "sqt1"]
    for j in range(1, SQUARES + 1):
        lev += ([f"sq{j + 1}"] if j < SQUARES else []) + ([f"sqt{j + 1}"] if j < SQUARES - 1 else []) + [f"inv{j}"]
    solve = ["x1", "n_t"] + [f"h{j}" for j in range(STEPS3)]
    scores = ["s_l", "s_lt", "s_k", "s_rb", "s_rk", "own"] if rwkv else ["s_l", "s_lt", "s_rb"]
    pe_s = [core.steps(f"mixer_tensor{d}", ["cum"] + ["t_c", "t_b", "t_k", "t_r"] + scores + lev + solve + ["t_x", "u", "out", "state"]) for d in R]
    act_n = (["ld", "e_in", "e_out", "e_half"] if rwkv else ["b_copy", "r_copy", "e1", "e2"]) + ["c_t", "k_t"] \
        + (["own"] if rwkv else []) + ["sq1", "sqt1", "sq2", "sqt2", "sq3", "sqt3", "sq4", "n_t", "x_t", "out"]
    act_s = [core.steps(f"mixer_scalar{d}", act_n) for d in R]
    dve_n = (["c_b", "x_state"] if rwkv else ["rows", "dif", "clip", "c_q", "x"]) + ["b_t", "r_t", "l", "of", "lt"] \
        + (["ak", "rb", "rk", "sz"] if rwkv else ["rb", "kd"]) + [f"inv{j}" for j in range(SQUARES + 1)] + ["x1"] + [f"h{j}" for j in range(STEPS3)] + ["u", "state"]
    dve_s = [core.steps(f"mixer_vector{d}", dve_n) for d in R]
    pool_s = [core.steps(f"mixer_pool{d}", ["k_r"] if rwkv else ["masked"]) for d in R]
    zeroed = core.steps("vector_steps", ["zeroed"])

    def passes(eng, chain, per, body):
        for first, count, tiles in ((0, CT, lambda j: (j, j * -1 + (CT - 1))), (CT, LT, lambda j: (j + CT, j * -1 + (NT - 1)))):
            if chain is None:
                with eng.Fori(0, count) as j:
                    body(j + first, tiles(j))
            else:
                with chain.loop(eng, count, per) as j:
                    body(j + first, tiles(j))

    def turn_over(eng, d, turn, copied=True):
        eng.wait_ge(dve_s[d].sem, dve_s[d].base + turn * len(dve_n))
        if copied:
            eng.wait_ge(act_s[d].sem, act_s[d].base + turn * len(act_n))

    def turned(pe, out, src, first):
        if first:
            return pe.matmul(out, src, v.ident, start=True, stop=True)
        return pe.transpose(out, src, v.ident)

    with nc.Block() as block:
        @block.tensor
        def _(pe):
            pe.wait_ge(zeroed.sem, zeroed.count("zeroed"))

            def body(turn, tile):
                for d in R:
                    turn_over(pe, d, turn, not rwkv)
                    A, B, C, E = bank[d]
                    if rwkv:
                        pe.wait_ge(act_s[d].sem, act_s[d].count("ld", turn))
                        pe.matmul(A[:, 0:W], v.const[:, cum_in[d]:cum_in[d] + P], xt[d][:, 0:W], start=True, stop=True)
                        pe.matmul(A[:, W:512], v.const[:, cum_ex[d]:cum_ex[d] + P], xt[d][:, 0:W], start=True, stop=True)
                        for a in range(2):
                            m = pe.matmul(B[:, 2 * a:2 * a + 2], xt[d][:, a * P:(a + 1) * P], v.const[:, COLS:COLS + 2],
                                          start=True, stop=True)
                    else:
                        pe.wait_ge(dve_s[d].sem, dve_s[d].count("rows", turn))
                        for h in range(NH):
                            m = pe.matmul(A[:, h * P:(h + 1) * P], g_rows[d][:, h * P:(h + 1) * P],
                                          v.const[:, incl_st[d]:incl_st[d] + P], start=True, stop=True)
                    m.then_inc(pe_s[d].sem, pe_s[d].step("cum"))
                for d in R:
                    A, B, C, E = bank[d]
                    if rwkv:
                        pe.wait_ge(dve_s[d].sem, dve_s[d].count("c_b", turn))
                        pe.wait_ge(act_s[d].sem, act_s[d].count("e_half", turn))
                    else:
                        pe.wait_ge(dve_s[d].sem, dve_s[d].count("c_q", turn))
                        pe.wait_ge(act_s[d].sem, act_s[d].count("r_copy", turn))
                        pe.wait_ge(dve_s[d].sem, dve_s[d].count("dif", turn))
                    for nm, bk, src in (("t_c", A, 0), ("t_b", B, 1), ("t_k", C, 2), ("t_r", E, 3)):
                        if rwkv and nm == "t_k":
                            pe.wait_ge(pool_s[d].sem, pool_s[d].count("k_r", turn))
                        for a in range(2):
                            m = turned(pe, bk[:, a * P:(a + 1) * P], tm[d][src][:, a * P:(a + 1) * P], a == 0)
                        m.then_inc(pe_s[d].sem, pe_s[d].step(nm))

                def by_head(d, bk, left, right, name):
                    for h in range(NH):
                        hp, ap = slice(h * P, (h + 1) * P), slice(h // 2 * P, (h // 2 + 1) * P)
                        lp, rp = (hp, ap) if left is bt[d] or left is kt[d] else (ap, hp)
                        m = pe.matmul(bk[:, hp], left[:, lp], right[:, rp], start=True, stop=True)
                    m.then_inc(pe_s[d].sem, pe_s[d].step(name))

                for d in R:
                    A, B, C, E = bank[d]
                    pe.wait_ge(act_s[d].sem, act_s[d].count("c_t", turn))
                    pe.wait_ge(dve_s[d].sem, dve_s[d].count("b_t", turn))
                    by_head(d, A, ct[d], bt[d], "s_l")
                    by_head(d, B, bt[d], ct[d], "s_lt")
                    pe.wait_ge(act_s[d].sem, act_s[d].count("k_t", turn))
                    if rwkv:
                        by_head(d, C, kt[d], ct[d], "s_k")
                    pe.wait_ge(dve_s[d].sem, dve_s[d].count("r_t", turn))
                    by_head(d, E, bt[d], rt[d], "s_rb")
                    if rwkv:
                        pe.wait_ge(dve_s[d].sem, dve_s[d].count("of", turn))
                        by_head(d, A, kt[d], rt[d], "s_rk")
                if rwkv:
                    for d in R:
                        pe.wait_ge(dve_s[d].sem, dve_s[d].count("ak", turn))
                        for h in range(NH):
                            m = pe.matmul(bank[d][1][:, h * P:(h + 1) * P], xt[d][:, h * P:(h + 1) * P],
                                          of(mv.pt, PTW, tile[d], RKV0 + 2 * W + h // 2 * P, P), start=True, stop=True)
                        m.then_inc(pe_s[d].sem, pe_s[d].step("own"))
                def squares(d, j):
                    A, B, C, E = bank[d]
                    a, b = L[d][(j - 1) % 2], L_T[d][(j - 1) % 2]
                    for h in range(NH):
                        hp = slice(h * P, (h + 1) * P)
                        m = pe.matmul(A[:, hp], b[:, hp], a[:, hp], start=True, stop=True)
                    m.then_inc(pe_s[d].sem, pe_s[d].step(f"sq{j}"))
                    if j < SQUARES:
                        for h in range(NH):
                            hp = slice(h * P, (h + 1) * P)
                            m = pe.matmul(B[:, hp], a[:, hp], b[:, hp], start=True, stop=True)
                        m.then_inc(pe_s[d].sem, pe_s[d].step(f"sqt{j}"))

                def product(d, bk, left, right, name):
                    for h in range(NH):
                        m = pe.matmul(bk[:, h * P:(h + 1) * P], left[:, h * P:(h + 1) * P], right(h), start=True, stop=True)
                    m.then_inc(pe_s[d].sem, pe_s[d].step(name))

                for d in R:
                    pe.wait_ge(dve_s[d].sem, dve_s[d].count("rk" if rwkv else "rb", turn))
                    if rwkv:
                        pe.wait_ge(act_s[d].sem, act_s[d].count("own", turn))
                    squares(d, 1)
                for j in range(1, SQUARES + 1):
                    for d in R:
                        pe.wait_ge(act_s[d].sem, act_s[d].count(f"sqt{j}" if j < SQUARES else f"sq{j}", turn))
                        if j < SQUARES:
                            squares(d, j + 1)
                        pe.wait_ge(dve_s[d].sem, dve_s[d].count(f"inv{j - 1}", turn))
                        product(d, bank[d][2], L[d][j % 2], lambda h: inv_t[d][:, h * P:(h + 1) * P], f"inv{j}")
                for d in R:
                    pe.wait_ge(dve_s[d].sem, dve_s[d].count(f"inv{SQUARES}", turn))
                    product(d, bank[d][3], inv_t[d], lambda h: xv(d)[:, :, h, :], "x1")
                    product(d, bank[d][0], off[d], lambda h: inv_t[d][:, h * P:(h + 1) * P], "n_t")
                for j in range(STEPS3):
                    for d in R:
                        if j == 0:
                            pe.wait_ge(act_s[d].sem, act_s[d].count("n_t", turn))
                        pe.wait_ge(dve_s[d].sem, dve_s[d].count(f"h{j - 1}" if j else "x1", turn))
                        src = xv(d) if j == 0 else xv_of(sol[d])
                        product(d, bank[d][3], n_t[d], lambda h: src[:, :, h, :], f"h{j}")
                for d in R:
                    pe.wait_ge(dve_s[d].sem, dve_s[d].count(f"h{STEPS3 - 1}", turn))
                    for a in range(2):
                        m = turned(pe, bank[d][0][:, a * P:(a + 1) * P], sol[d][:, W + a * P:W + (a + 1) * P], a == 0)
                    m.then_inc(pe_s[d].sem, pe_s[d].step("t_x"))
                for d in R:
                    pe.wait_ge(act_s[d].sem, act_s[d].count("x_t", turn))
                    if rwkv:
                        pe.wait_ge(dve_s[d].sem, dve_s[d].count("sz", turn))
                    for a in range(2):
                        ap = slice(a * P, (a + 1) * P)
                        m = pe.matmul(bank[d][2][:, ap], xt[d][:, ap], sz[d][:, ap], start=True, stop=True)
                    m.then_inc(pe_s[d].sem, pe_s[d].step("u"))
                for d in R:
                    A, B, C, E = bank[d]
                    pe.wait_ge(dve_s[d].sem, dve_s[d].count("u", turn))
                    read = rt[d] if rwkv else kt[d]
                    for h in range(NH):
                        hp, ap = slice(h * P, (h + 1) * P), slice(h // 2 * P, (h // 2 + 1) * P)
                        pe.matmul(E[:, hp], read[:, ap], sz[d][:, ap], start=True, stop=False)
                        m = pe.matmul(E[:, hp], rb[d][:, hp], u[d][:, ap], start=False, stop=not rwkv)
                        if rwkv:
                            m = pe.matmul(E[:, hp], rk[d][:, hp], of(mv.pt, PTW, tile[d], RKV0 + 2 * W + h // 2 * P, P),
                                          start=False, stop=True)
                    m.then_inc(pe_s[d].sem, pe_s[d].step("out"))
                    for a in range(2):
                        ap = slice(a * P, (a + 1) * P)
                        m = pe.matmul(B[:, ap], tm[d][1][:, ap], u[d][:, ap], start=True, stop=not rwkv)
                        if rwkv:
                            m = pe.matmul(B[:, ap], tm[d][2][:, ap], of(mv.pt, PTW, tile[d], RKV0 + 2 * W + a * P, P), start=False, stop=True)
                    m.then_inc(pe_s[d].sem, pe_s[d].step("state"))

            passes(pe, None, 0, body)

        @block.scalar
        def _(act):
            def body(turn, tile):
                for d in R:
                    turn_over(act, d, turn)
                    if rwkv:
                        act.copy(xt[d][:, 0:W], of(mv.sig_w[d], W, tile[d], 0, W)).then_inc(act_s[d].sem, act_s[d].step("ld"))
                    else:
                        act.copy(tm[d][1], of(mv.qkv, 3 * W, tile[d], W, W)).then_inc(act_s[d].sem, act_s[d].step("b_copy"))
                        act.copy(tm[d][3], of(mv.qkv, 3 * W, tile[d], 0, W)).then_inc(act_s[d].sem, act_s[d].step("r_copy"))
                for d in R:
                    A, B, C, E = bank[d]
                    if rwkv:
                        act.wait_ge(pe_s[d].sem, pe_s[d].count("cum", turn))
                        act.activation(l0[d], A, ACT.Exp, scale=-DECAY).then_inc(act_s[d].sem, act_s[d].step("e_in"))
                        act.activation(lt0[d][:, 0:W], A[:, 0:W], ACT.Exp, scale=DECAY).then_inc(act_s[d].sem, act_s[d].step("e_out"))
                        act.activation(e_halves[d], B[:, 0:4].rearrange("p (a c) -> p a c", c=2), ACT.Exp, scale=-DECAY).then_inc(act_s[d].sem, act_s[d].step("e_half"))
                    else:
                        act.wait_ge(dve_s[d].sem, dve_s[d].count("clip", turn))
                        act.activation(e1[d], e1[d], ACT.Exp, scale=-1.0).then_inc(act_s[d].sem, act_s[d].step("e1"))
                        act.activation(e2[d], e2[d], ACT.Exp).then_inc(act_s[d].sem, act_s[d].step("e2"))
                for d in R:
                    A, B, C, E = bank[d]
                    act.wait_ge(pe_s[d].sem, pe_s[d].count("t_c", turn))
                    act.copy(ct[d][:, 0:W], A[:, 0:W]).then_inc(act_s[d].sem, act_s[d].step("c_t"))
                    act.wait_ge(pe_s[d].sem, pe_s[d].count("t_k", turn))
                    if rwkv:
                        act.activation(of_head(kt[d], 0), pairs(C[:, 0:W]), ACT.Copy, scale=v.const[:, COLS:COLS + 1])
                        act.activation(of_head(kt[d], 1), pairs(C[:, 0:W]), ACT.Copy, scale=v.const[:, COLS + 1:COLS + 2]).then_inc(act_s[d].sem, act_s[d].step("k_t"))
                    else:
                        act.copy(kt[d][:, 0:W], C[:, 0:W]).then_inc(act_s[d].sem, act_s[d].step("k_t"))
                if rwkv:
                    for d in R:
                        act.wait_ge(pe_s[d].sem, pe_s[d].count("own", turn))
                        act.copy(pairs(x[d][:, 0:W])[:, :, 0:HD], one_head(bank[d][1], 0))
                        act.copy(pairs(x[d][:, 0:W])[:, :, HD:P], one_head(bank[d][1], 1)).then_inc(act_s[d].sem, act_s[d].step("own"))
                for j in range(1, SQUARES + 1):
                    for d in R:
                        act.wait_ge(pe_s[d].sem, pe_s[d].count(f"sq{j}", turn))
                        act.copy(L[d][j % 2], bank[d][0]).then_inc(act_s[d].sem, act_s[d].step(f"sq{j}"))
                        if j < SQUARES:
                            if j == 2:
                                act.wait_ge(dve_s[d].sem, dve_s[d].count("inv0", turn))
                            act.wait_ge(pe_s[d].sem, pe_s[d].count(f"sqt{j}", turn))
                            act.copy(L_T[d][j % 2], bank[d][1]).then_inc(act_s[d].sem, act_s[d].step(f"sqt{j}"))
                for d in R:
                    act.wait_ge(pe_s[d].sem, pe_s[d].count("n_t", turn))
                    act.copy(n_t[d], bank[d][0]).then_inc(act_s[d].sem, act_s[d].step("n_t"))
                for d in R:
                    act.wait_ge(pe_s[d].sem, pe_s[d].count("t_x", turn))
                    act.copy(xt[d][:, 0:W], bank[d][0][:, 0:W]).then_inc(act_s[d].sem, act_s[d].step("x_t"))
                for d in R:
                    act.wait_ge(pe_s[d].sem, pe_s[d].count("out", turn))
                    out = pairs(of(mv.pt, PTW, tile[d], V0 + d * W, W))
                    act.copy(out[:, :, 0:HD], one_head(bank[d][3], 0))
                    act.copy(out[:, :, HD:P], one_head(bank[d][3], 1)).then_inc(act_s[d].sem, act_s[d].step("out"))

            passes(act, None, 0, body)

        @block.gpsimd
        def _(pool):
            def body(turn, tile):
                for d in R:
                    turn_over(pool, d, turn, False)
                    if rwkv:
                        pool.wait_ge(act_s[d].sem, act_s[d].count("e_out", turn))
                        pool.tensor_tensor(tm[d][2], of(mv.kd[d], W, tile[d], 0, W), lt0[d][:, 0:W], ALU.mult)
                        pool.tensor_tensor(tm[d][3], of(mv.pt, PTW, tile[d], RKV0, W), l0[d][:, 0:W], ALU.mult).then_inc(pool_s[d].sem, pool_s[d].step("k_r"))
                    else:
                        pool.wait_ge(act_s[d].sem, act_s[d].count("e2", turn))
                        pool.tensor_tensor(heads(rk[d], P), heads(e2[d], P), mask(incl_st[d]), ALU.mult)
                        pool.tensor_tensor(heads(e2s[d], P), heads(e2[d], P), mask(in_st[d]), ALU.mult)
                        pool.tensor_tensor(heads(e1f[d], P), heads(e1[d], P), mask(off_ts[d]), ALU.mult)
                        pool.tensor_tensor(heads(dif[d], P), heads(e1[d], P), mask(in_ts[d]), ALU.mult).then_inc(pool_s[d].sem, pool_s[d].step("masked"))

            passes(pool, None, 0, body)

        @block.vector
        def _(dve):
            ch = core.vchain
            for d in R:
                m = dve.memset(st[d], 0.0)
            m.then_inc(zeroed.sem, zeroed.step("zeroed"))
            dve.wait_ge(zeroed.sem, zeroed.count("zeroed"))

            def masked(d, name, src, dst, weights, sign):
                dve.wait_ge(pe_s[d].sem, pe_s[d].count(name[0], turn_[0]))
                dve.scalar_tensor_tensor(out=heads(dst, P), in0=heads(src, P), scalar=sign, in1=weights,
                                                       op0=ALU.mult, op1=ALU.mult).then_inc(dve_s[d].sem, dve_s[d].step(name[1]))

            turn_ = [0]

            def body(turn, tile):
                turn_[0] = turn
                for d in R:
                    turn_over(dve, d, turn)
                    if not rwkv:
                        dve.tensor_copy(heads(g_rows[d], P), spread(per_head(sm.g, tile[d], d), P)).then_inc(dve_s[d].sem, dve_s[d].step("rows"))
                for d in R:
                    A, B, C, E = bank[d]
                    if rwkv:
                        dve.wait_ge(act_s[d].sem, act_s[d].count("e_out", turn))
                        dve.tensor_tensor(tm[d][0], of(mv.kk, W, tile[d], 0, W), l0[d][:, W:512], ALU.mult)
                        dve.tensor_tensor(tm[d][1], of(mv.kk_a[d], W, tile[d], 0, W), lt0[d][:, 0:W], ALU.mult).then_inc(dve_s[d].sem, dve_s[d].step("c_b"))
                    else:
                        dve.wait_ge(pe_s[d].sem, pe_s[d].count("cum", turn))
                        dve.tensor_tensor(heads(dif[d], P), heads(A, P), spread(per_head(sm.gcum, tile[d], d), P), ALU.subtract).then_inc(dve_s[d].sem, dve_s[d].step("dif"))
                        dve.wait_ge(dve_s[d].sem, dve_s[d].count("dif", turn))
                        dve.tensor_scalar(e1[d], dif[d], 0.0, None, ALU.max)
                        dve.tensor_scalar(e2[d], dif[d], 0.0, None, ALU.min).then_inc(dve_s[d].sem, dve_s[d].step("clip"))
                for d in R:
                    if rwkv:
                        dve.wait_ge(dve_s[d].sem, dve_s[d].count("c_b", turn))
                        dve.tensor_scalar(x[d][:, W:512], tm[d][0], -1.0, None, ALU.mult).then_inc(dve_s[d].sem, dve_s[d].step("x_state"))
                    else:
                        q, k, vv = (heads(of(mv.qkv, 3 * W, tile[d], n * W, W), HD) for n in range(3))
                        dve.tensor_tensor(heads(tm[d][0], HD), k, spread(per_head(sm.beta, tile[d], d), HD), ALU.mult)
                        dve.tensor_tensor(heads(tm[d][2], HD), q, spread(per_head(sm.e_cum, tile[d], d), HD), ALU.mult).then_inc(dve_s[d].sem, dve_s[d].step("c_q"))
                        dve.tensor_tensor(heads(x[d][:, 0:W], HD), vv, spread(per_head(sm.beta, tile[d], d), HD), ALU.mult)
                        dve.wait_ge(dve_s[d].sem, dve_s[d].count("c_q", turn))
                        dve.tensor_tensor(heads(x[d][:, W:512], HD), heads(tm[d][0], HD), spread(per_head(sm.e_cum, tile[d], d), HD), ALU.mult).then_inc(ch.sem, ch.up())
                        dve.wait_ge(ch.sem, ch.count())
                        dve.tensor_scalar(x[d][:, W:512], x[d][:, W:512], -1.0, None, ALU.mult).then_inc(dve_s[d].sem, dve_s[d].step("x"))
                for d in R:
                    A, B, C, E = bank[d]
                    dve.wait_ge(pe_s[d].sem, pe_s[d].count("t_b", turn))
                    dve.tensor_scalar(of_head(bt[d], 0), pairs(B[:, 0:W]), v.const[:, COLS:COLS + 1], None, ALU.mult)
                    dve.tensor_scalar(of_head(bt[d], 1), pairs(B[:, 0:W]), v.const[:, COLS + 1:COLS + 2], None, ALU.mult).then_inc(dve_s[d].sem, dve_s[d].step("b_t"))
                    dve.wait_ge(pe_s[d].sem, pe_s[d].count("t_r", turn))
                    dve.tensor_copy(rt[d][:, 0:W], E[:, 0:W]).then_inc(dve_s[d].sem, dve_s[d].step("r_t"))
                for d in R:
                    A, B, C, E = bank[d]
                    if not rwkv:
                        dve.wait_ge(pool_s[d].sem, pool_s[d].count("masked", turn))
                    masked(d, ("s_l", "l"), A, l0[d], mask(in_ts[d]) if rwkv else heads(dif[d], P), -1.0)
                    masked(d, ("s_l", "of"), A, off[d], mask(off_ts[d]) if rwkv else heads(e1f[d], P), -1.0)
                    masked(d, ("s_lt", "lt"), B, lt0[d], mask(in_st[d]) if rwkv else heads(e2s[d], P), -1.0)
                    if rwkv:
                        masked(d, ("s_k", "ak"), C, xt[d], mask(strict_st[d]), -1.0)
                    masked(d, ("s_rb", "rb"), E, rb[d], mask(incl_st[d]) if rwkv else heads(rk[d], P), 1.0)
                    if rwkv:
                        masked(d, ("s_rk", "rk"), A, rk[d], mask(incl_st[d]), 1.0)
                        dve.tensor_tensor(pairs(sz[d]), pairs(st[d]), over_pair(e_halves[d][:, :, half_in[d]]), ALU.mult).then_inc(dve_s[d].sem, dve_s[d].step("sz"))
                    else:
                        k = heads(of(mv.qkv, 3 * W, tile[d], W, W), HD)
                        dve.tensor_tensor(heads(tm[d][1], HD), k, spread(per_head(sm.e_rest, tile[d], d), HD), ALU.mult).then_inc(dve_s[d].sem, dve_s[d].step("kd"))
                for d in R:
                    dve.wait_ge(dve_s[d].sem, dve_s[d].count("lt", turn))
                    if rwkv:
                        dve.wait_ge(pe_s[d].sem, pe_s[d].count("s_rk", turn))
                    dve.tensor_tensor(heads(inv_t[d], P), heads(lt0[d], P), mask(IDENT), ALU.add).then_inc(dve_s[d].sem, dve_s[d].step("inv0"))
                for j in range(1, SQUARES + 1):
                    for d in R:
                        dve.wait_ge(pe_s[d].sem, pe_s[d].count(f"inv{j}", turn))
                        dve.wait_ge(dve_s[d].sem, dve_s[d].count(f"inv{j - 1}", turn))
                        dve.tensor_tensor(inv_t[d], inv_t[d], bank[d][2], ALU.add).then_inc(dve_s[d].sem, dve_s[d].step(f"inv{j}"))

                def by_part(ap):
                    return xv_of(ap).rearrange("p c h n -> p h c n")

                for d in R:
                    dve.wait_ge(pe_s[d].sem, pe_s[d].count("x1", turn))
                    E = bank[d][3].rearrange("p (h c n) -> p h c n", h=NH, c=2)
                    dve.tensor_copy(by_part(x[d]), E).then_inc(dve_s[d].sem, dve_s[d].step("x1"))
                for j in range(STEPS3):
                    for d in R:
                        dve.wait_ge(pe_s[d].sem, pe_s[d].count(f"h{j}", turn))
                        if j == 0:
                            dve.wait_ge(dve_s[d].sem, dve_s[d].count("x1", turn))
                        E = bank[d][3].rearrange("p (h c n) -> p h c n", h=NH, c=2)
                        dve.tensor_tensor(by_part(sol[d]), by_part(x[d]), E, ALU.add).then_inc(dve_s[d].sem, dve_s[d].step(f"h{j}"))
                for d in R:
                    dve.wait_ge(pe_s[d].sem, pe_s[d].count("u", turn))
                    dve.wait_ge(dve_s[d].sem, dve_s[d].count(f"h{STEPS3 - 1}", turn))
                    dve.tensor_tensor(u[d], bank[d][2][:, 0:W], sol[d][:, 0:W], ALU.add).then_inc(dve_s[d].sem, dve_s[d].step("u"))
                for d in R:
                    dve.wait_ge(pe_s[d].sem, pe_s[d].count("state", turn))
                    if not rwkv:
                        dve.tensor_tensor(heads(st[d], HD), heads(st[d], HD), spread(per_head(sm.e_tot, tile[d], d), HD), ALU.mult).then_inc(ch.sem, ch.up())
                        dve.wait_ge(ch.sem, ch.count())
                    for b in range(2):
                        hp = slice(b * HD, (b + 1) * HD)
                        s, old, fresh = (pairs(ap)[hp, :, hp] for ap in (st[d], sz[d], bank[d][1][:, 0:W]))
                        m = dve.tensor_tensor(s, old, fresh, ALU.add)
                    if rwkv:
                        m.then_inc(ch.sem, ch.up())
                        dve.wait_ge(ch.sem, ch.count())
                        m = dve.tensor_tensor(pairs(st[d]), pairs(st[d]), over_pair(e_halves[d][:, :, half_out[d]]), ALU.mult)
                    m.then_inc(dve_s[d].sem, dve_s[d].step("state"))

            passes(dve, ch, 2 if rwkv else 4, body)
    for s in (*pe_s, *act_s, *dve_s, *pool_s):
        s.at = 0
        s.close(NT)
    zeroed.close()


def gdn(core, v, io, i):
    nc = core.nc
    mv, sm = MixerViews(core), Small(v)
    hi, lo = Region(core, A_HT, A_PT), Region(core, A_WORK, A_END)
    acc, conv = [lo(T) for _ in range(2)], [lo(T) for _ in range(2)]
    rows, taps = lo(P), lo(32)
    sp8 = [lo(NT * 8) for _ in range(3)]
    sq = hi(NT, 512)
    inv = hi(NT * 8)
    norm_g = hi(HD)
    F0 = 8 * T
    segs = ((0, CT * P), (CT * P, T))
    small_in = core.steps("gdn_small_in", ["all"], 64)
    NC = 3
    cv = core.steps("conv_sum", ["s0", "s1"])
    ca = core.steps("conv_silu", ["s0", "s1"])
    ctp = core.steps("conv_transposed", ["s0", "s1"])
    ce = core.steps("conv_copied", ["s0", "s1"])
    pe_s = core.steps("tensor_steps", ["taps", "cums"])
    act_s = core.steps("scalar_steps", ["taps", "root", "exps", "log", "beta", "cums"])
    dve_s = core.steps("vector_steps", ["sums", "arg", "plus1", "g", "rest"])
    ab = v.pt[:, :, AB0:AB0 + 16]

    def t8(ap):
        return ap.rearrange("p (t c) -> p t c", c=8)

    with nc.Block() as block:
        @block.sync
        def _(sp):
            sp.dma_start(rows[0:30, :], io["gdn_conv"][i].rearrange("j (r n) -> (j r) n", n=P)).then_inc(small_in.sem, 16)
            sp.dma_start(sm.a_log, io["gdn_a_log"][i:i + 1].rearrange("a b c -> a (b c)").partition_broadcast(P)).then_inc(small_in.sem, 16)
            sp.dma_start(sm.dt, io["gdn_dt_bias"][i:i + 1].rearrange("a b c -> a (b c)").partition_broadcast(P)).then_inc(small_in.sem, 16)
            sp.dma_start(norm_g, io["gdn_norm"][i:i + 1, :].partition_broadcast(P)).then_inc(small_in.sem, 16)

        @block.tensor
        def _(pe):
            pe.wait_ge(small_in.sem, small_in.count("all"))
            pe.transpose(core.bank[0][:, 0:30], rows[0:30, :], v.ident[0:30, 0:30]).then_inc(pe_s.sem, pe_s.step("taps"))
            with pe.Fori(0, NC) as n:
                for s in range(2):
                    pe.wait_ge(ca.sem, ca.count(f"s{s}", n))
                    pe.wait_ge(ce.sem, ce.base + n * 2)
                    for t in range(NT):
                        x = pe.transpose(core.wide[s][:, t * P:(t + 1) * P], conv[s][:, t * P:(t + 1) * P], v.ident)
                    x.then_inc(ctp.sem, ctp.step(f"s{s}"))
            pe.wait_ge(dve_s.sem, dve_s.count("g"))
            for b, m in enumerate((UPI, LOI, ONES)):
                x = pe.matmul(core.wide[2][:, 64 * b:64 * b + 48], v.const[:, m:m + P], sm.g, start=True, stop=True)
            x.then_inc(pe_s.sem, pe_s.step("cums"))

        @block.scalar
        def _(act):
            act.wait_ge(pe_s.sem, pe_s.count("taps"))
            act.copy(taps[:, 0:30], core.bank[0][:, 0:30]).then_inc(act_s.sem, act_s.step("taps"))
            with act.Fori(0, NC) as n:
                for s in range(2):
                    act.wait_ge(cv.sem, cv.count(f"s{s}", n))
                    act.wait_ge(ctp.sem, ctp.base + n * 2)
                    act.activation(conv[s], acc[s], ACT.Silu).then_inc(ca.sem, ca.step(f"s{s}"))
                for s in range(2):
                    act.wait_ge(ctp.sem, ctp.count(f"s{s}", n))
                    act.copy(mv.qkv.rearrange("p (t c) -> p t c", t=NT)[:, :, ds((n * 2 + s) * P, P)],
                                     core.wide[s][:, 0:T].rearrange("p (t c) -> p t c", t=NT)).then_inc(ce.sem, ce.step(f"s{s}"))
            act.wait_ge(dve_s.sem, dve_s.count("sums"))
            act.activation(inv, inv, ACT.Sqrt).then_inc(act_s.sem, act_s.step("root"))
            act.wait_ge(dve_s.sem, dve_s.count("arg"))
            act.activation(sm.a_log, sm.a_log, ACT.Exp)
            act.activation(sp8[1], sp8[1], ACT.Exp, scale=-1.0).then_inc(act_s.sem, act_s.step("exps"))
            act.wait_ge(dve_s.sem, dve_s.count("plus1"))
            act.activation(sp8[2], sp8[2], ACT.Ln).then_inc(act_s.sem, act_s.step("log"))
            act.activation(t8(sm.beta), ab[:, :, 8:16], ACT.Sigmoid).then_inc(act_s.sem, act_s.step("beta"))
            act.wait_ge(dve_s.sem, dve_s.count("rest"))
            act.activation(sm.e_cum, sm.gcum, ACT.Exp)
            act.activation(sm.e_tot, sm.gtot, ACT.Exp)
            act.activation(sm.e_rest, sm.e_rest, ACT.Exp).then_inc(act_s.sem, act_s.step("cums"))

        @block.vector
        def _(dve):
            ch = core.vchain
            dve.wait_ge(act_s.sem, act_s.count("taps"))
            with ch.loop(dve, NC, 8) as n:
                for s in range(2):
                    f = n * 2 + s
                    dve.wait_ge(ca.sem, ca.base + n * 2)

                    def tap(j):
                        return taps[:, ds(f + j * 6, 1)]
                    dve.tensor_scalar(acc[s], v.fm[:, ds(f * T + F0, T)], tap(2), None, ALU.mult).then_inc(ch.sem, ch.up())
                    dve.wait_ge(ch.sem, ch.count())
                    for q, j in enumerate((0, 1, 3, 4)):
                        o = j - 2
                        for a0, b0 in segs:
                            a, b = max(a0, a0 - o), min(b0, b0 - o)
                            x = dve.scalar_tensor_tensor(out=acc[s][:, a:b], in0=v.fm[:, ds(f * T + (F0 + a + o), b - a)],
                                                         scalar=tap(j), in1=acc[s][:, a:b], op0=ALU.mult, op1=ALU.add)
                        if q < 3:
                            x.then_inc(ch.sem, ch.up())
                            dve.wait_ge(ch.sem, ch.count())
                    x.then_inc(cv.sem, cv.step(f"s{s}"))
            dve.wait_ge(ce.sem, ce.count("s1", NC - 1))
            qk = mv.qkv.rearrange("p (t c) -> p t c", t=NT)[:, :, 0:512]
            dve.tensor_tensor(sq, qk, qk, ALU.mult).then_inc(ch.sem, ch.up())
            dve.wait_ge(ch.sem, ch.count())
            dve.tensor_reduce(inv, sq.rearrange("p t (h n) -> p (t h) n", n=HD), AX.X, ALU.add).then_inc(ch.sem, ch.up())
            dve.wait_ge(ch.sem, ch.count())
            dve.tensor_scalar(inv, inv, 1e-12, None, ALU.add).then_inc(dve_s.sem, dve_s.step("sums"))
            dve.wait_ge(act_s.sem, act_s.count("root"))
            dve.reciprocal(inv, inv).then_inc(ch.sem, ch.up())
            dve.wait_ge(ch.sem, ch.count())
            dve.tensor_scalar(t8(inv)[:, :, 0:4], t8(inv)[:, :, 0:4], HD ** -0.5, None, ALU.mult).then_inc(ch.sem, ch.up())
            dve.wait_ge(ch.sem, ch.count())
            for t in range(NT):
                w = mv.qkv[:, t * 3 * W:t * 3 * W + 512].rearrange("p (h n) -> p h n", n=HD)
                x = dve.tensor_tensor(w, w, inv[:, t * 8:t * 8 + 8].unsqueeze(2).broadcast_to([P, 8, HD]), ALU.mult)
            x.then_inc(ch.sem, ch.up())
            dve.wait_ge(ch.sem, ch.count())
            dve.tensor_tensor(t8(sp8[0]), ab[:, :, 0:8], sm.dt.unsqueeze(1).broadcast_to([P, NT, 8]), ALU.add).then_inc(ch.sem, ch.up())
            dve.wait_ge(ch.sem, ch.count())
            dve.scalar_tensor_tensor(out=sp8[1], in0=sp8[0], scalar=-1.0, in1=sp8[0], op0=ALU.mult, op1=ALU.max).then_inc(dve_s.sem, dve_s.step("arg"))
            dve.wait_ge(act_s.sem, act_s.count("exps"))
            dve.tensor_scalar(sp8[2], sp8[1], 1.0, None, ALU.add).then_inc(dve_s.sem, dve_s.step("plus1"))
            dve.wait_ge(act_s.sem, act_s.count("log"))
            dve.scalar_tensor_tensor(out=sp8[0], in0=sp8[0], scalar=0.0, in1=sp8[2], op0=ALU.max, op1=ALU.add).then_inc(ch.sem, ch.up())
            dve.wait_ge(ch.sem, ch.count())
            dve.scalar_tensor_tensor(out=t8(sm.g), in0=t8(sp8[0]), scalar=-1.0,
                                                in1=sm.a_log.unsqueeze(1).broadcast_to([P, NT, 8]), op0=ALU.mult, op1=ALU.mult).then_inc(dve_s.sem, dve_s.step("g"))
            dve.wait_ge(pe_s.sem, pe_s.count("cums"))
            for d in range(2):
                dve.tensor_copy(t8(sm.gcum)[:, :, 4 * d:4 * d + 4], t8(core.wide[2][:, 64 * d:64 * d + 48])[:, :, 4 * d:4 * d + 4])
            dve.tensor_copy(sm.gtot, core.wide[2][:, 128:176]).then_inc(ch.sem, ch.up())
            dve.wait_ge(ch.sem, ch.count())
            dve.tensor_tensor(sm.e_rest, sm.gtot, sm.gcum, ALU.subtract).then_inc(dve_s.sem, dve_s.step("rest"))
            dve.wait_ge(act_s.sem, act_s.count("cums"))
    for s in (small_in, pe_s, act_s, dve_s):
        s.close()
    for s in (cv, ca, ctp, ce):
        s.close(NC)

    recurrence(core, v, "gdn")

    hi = Region(core, A_HT, A_PT)
    sq, gate = hi(NT, W), hi(NT, W)
    norm_g = hi(HD)
    ss = hi(NT * NH)
    o = v.mix[:, :, 512:512 + W]
    small_in = core.steps("gdn_norm_in", ["all"], 16)
    act_s = core.steps("scalar_steps", ["root", "gate"])
    dve_s = core.steps("vector_steps", ["mean"])
    with nc.Block() as block:
        @block.sync
        def _(sp):
            sp.dma_start(norm_g, io["gdn_norm"][i:i + 1, :].partition_broadcast(P)).then_inc(small_in.sem, 16)

        @block.scalar
        def _(act):
            act.wait_ge(dve_s.sem, dve_s.count("mean"))
            act.activation(ss, ss, ACT.Sqrt).then_inc(act_s.sem, act_s.step("root"))
            act.activation(gate, v.pt[:, :, GATE0:GATE0 + W], ACT.Silu).then_inc(act_s.sem, act_s.step("gate"))

        @block.vector
        def _(dve):
            ch = core.vchain
            dve.tensor_tensor(o, v.pt[:, :, V0:V0 + W], v.pt[:, :, V0 + W:V0 + 2 * W], ALU.add).then_inc(ch.sem, ch.up())
            dve.wait_ge(ch.sem, ch.count())
            dve.tensor_tensor(sq, o, o, ALU.mult).then_inc(ch.sem, ch.up())
            dve.wait_ge(ch.sem, ch.count())
            dve.tensor_reduce(ss, sq.rearrange("p t (h n) -> p (t h) n", n=HD), AX.X, ALU.add).then_inc(ch.sem, ch.up())
            dve.wait_ge(ch.sem, ch.count())
            dve.tensor_scalar(ss, ss, 1.0 / HD, EPS, ALU.mult, ALU.add).then_inc(dve_s.sem, dve_s.step("mean"))
            dve.wait_ge(act_s.sem, act_s.count("root"))
            dve.reciprocal(ss, ss).then_inc(ch.sem, ch.up())
            dve.wait_ge(ch.sem, ch.count())
            dve.wait_ge(act_s.sem, act_s.count("gate"))
            dve.tensor_tensor(o, o, gate, ALU.mult).then_inc(ch.sem, ch.up())
            dve.wait_ge(ch.sem, ch.count())
            dve.wait_ge(small_in.sem, small_in.count("all"))
            for t in range(NT):
                w = v.mix[:, t, 512:512 + W].rearrange("p (h n) -> p h n", h=NH)
                x = dve.tensor_tensor(w, w, ss[:, t * NH:(t + 1) * NH].unsqueeze(2).broadcast_to([P, NH, HD]), ALU.mult)
            x.then_inc(ch.sem, ch.up())
            dve.wait_ge(ch.sem, ch.count())
            for t in range(NT):
                w = v.mix[:, t, 512:512 + W].rearrange("p (h n) -> p h n", h=NH)
                x = dve.tensor_tensor(w, w, norm_g.unsqueeze(1).broadcast_to([P, NH, HD]), ALU.mult)
            x.then_inc(ch.sem, ch.up())
            dve.wait_ge(ch.sem, ch.count())
    for s in (small_in, act_s, dve_s):
        s.close()


def rwkv(core, v, io, i):
    nc = core.nc
    mv = MixerViews(core)
    lora = v.fm[:, 14 * T:15 * T]
    lo, hi = Region(core, A_WORK, A_END), Region(core, A_HT, A_PT)
    ups = lo(512)
    w0, a0, k_k, k_a = lo(512), lo(512), lo(W), lo(W)
    act_in = lo(T)
    pre = [[lo(512) for _ in range(2)] for _ in range(2)]
    inv = lo(NT * NH)
    sq = hi(NT, W)
    key = hi(NT * W)
    r_, k_, v_ = (v.pt[:, :, RKV0 + n * W:RKV0 + (n + 1) * W] for n in range(3))

    def t3(ap):
        return ap.rearrange("p (t n) -> p t n", t=NT)

    def row(name):
        return io[name][i:i + 1].rearrange("a b c -> a (b c)") if len(io[name].shape) == 3 else io[name][i:i + 1, :]

    small_in = core.steps("rwkv_small_in", ["all"], 16 * 7)
    lora_s = core.steps("scalar_steps", ["tanh", "root"])
    mm = core.steps("lora_up", [f"{a}{t}" for t in range(NT) for a in "wa"])
    add = core.steps("lora_biased", ["mean"] + [f"{a}{t}" for t in range(NT) for a in "wa"])
    sg = core.steps("lora_sigmoid", [f"{a}{t}" for t in range(NT) for a in "wa"])
    with nc.Block() as block:
        @block.sync
        def _(sp):
            for dst, src in ((ups[0:32, :].rearrange("p (d n) -> p d n", d=2), io["rwkv_w_up"][i].rearrange("d k n -> k d n")),
                             (ups[32:64, :].rearrange("p (d n) -> p d n", d=2), io["rwkv_a_up"][i].rearrange("d k n -> k d n")),
                             (ups[64:128, 0:W], io["rwkv_g_up"][i]),
                             (w0, row("rwkv_w0").partition_broadcast(P)), (a0, row("rwkv_a0").partition_broadcast(P)),
                             (k_k, row("rwkv_k_k").partition_broadcast(P)), (k_a, row("rwkv_k_a").partition_broadcast(P))):
                sp.dma_start(dst, src).then_inc(small_in.sem, 16)

        @block.tensor
        def _(pe):
            pe.wait_ge(small_in.sem, small_in.count("all"))
            pe.wait_ge(lora_s.sem, lora_s.count("tanh"))
            for t in range(NT):
                ts = slice(t * P, (t + 1) * P)
                if t >= 2:
                    pe.wait_ge(add.sem, add.count(f"w{t - 2}"))
                pe.matmul(core.bank[t % 2][:, :], act_in[0:32, ts], ups[0:32, :], start=True, stop=True).then_inc(mm.sem, mm.step(f"w{t}"))
                if t >= 2:
                    pe.wait_ge(add.sem, add.count(f"a{t - 2}"))
                pe.matmul(core.wide[t % 2][:, 0:512], act_in[32:64, ts], ups[32:64, :], start=True, stop=True).then_inc(mm.sem, mm.step(f"a{t}"))

        @block.scalar
        def _(act):
            act.activation(act_in[0:32, :], lora[0:32, :], ACT.Tanh)
            act.copy(act_in[32:64, :], lora[32:64, :]).then_inc(lora_s.sem, lora_s.step("tanh"))
            act.wait_ge(add.sem, add.count("mean"))
            act.activation(inv, inv, ACT.Sqrt).then_inc(lora_s.sem, lora_s.step("root"))
            for t in range(NT):
                for a, out, src in (("w", mv.sig_w, pre[t % 2][0]), ("a", mv.kk_a, pre[t % 2][1])):
                    act.wait_ge(add.sem, add.count(f"{a}{t}"))
                    act.activation(out[0][:, t * W:(t + 1) * W], src[:, 0:W], ACT.Sigmoid)
                    act.activation(out[1][:, t * W:(t + 1) * W], src[:, W:512], ACT.Sigmoid).then_inc(sg.sem, sg.step(f"{a}{t}"))

        @block.vector
        def _(dve):
            ch = core.vchain
            dve.wait_ge(small_in.sem, small_in.count("all"))

            def over_tiles(ap):
                return ap.unsqueeze(1).broadcast_to([P, NT, W])
            dve.tensor_tensor(t3(mv.kk), k_, over_tiles(k_k), ALU.mult).then_inc(ch.sem, ch.up())
            dve.wait_ge(ch.sem, ch.count())
            dve.tensor_tensor(sq, t3(mv.kk), t3(mv.kk), ALU.mult).then_inc(ch.sem, ch.up())
            dve.wait_ge(ch.sem, ch.count())
            dve.tensor_reduce(inv, sq.rearrange("p t (h n) -> p (t h) n", n=HD), AX.X, ALU.add).then_inc(ch.sem, ch.up())
            dve.wait_ge(ch.sem, ch.count())
            dve.tensor_scalar(inv, inv, 1e-12, None, ALU.add).then_inc(add.sem, add.step("mean"))
            for t in range(NT):
                if t >= 2:
                    dve.wait_ge(sg.sem, sg.count(f"a{t - 2}"))
                dve.wait_ge(mm.sem, mm.count(f"w{t}"))
                dve.tensor_tensor(pre[t % 2][0], core.bank[t % 2][:, :], w0, ALU.add).then_inc(add.sem, add.step(f"w{t}"))
                dve.wait_ge(mm.sem, mm.count(f"a{t}"))
                dve.tensor_tensor(pre[t % 2][1], core.wide[t % 2][:, 0:512], a0, ALU.add).then_inc(add.sem, add.step(f"a{t}"))
            dve.wait_ge(lora_s.sem, lora_s.count("root"))
            dve.reciprocal(inv, inv).then_inc(ch.sem, ch.up())
            dve.wait_ge(ch.sem, ch.count())
            kk = mv.kk.rearrange("p (g n) -> p g n", n=HD)
            dve.tensor_tensor(kk, kk, inv.unsqueeze(2).broadcast_to([P, NT * NH, HD]), ALU.mult).then_inc(ch.sem, ch.up())
            dve.wait_ge(ch.sem, ch.count())
            dve.wait_ge(sg.sem, sg.count(f"a{NT - 1}"))
            dve.tensor_tensor(t3(key), k_, over_tiles(k_a), ALU.mult).then_inc(ch.sem, ch.up())
            dve.wait_ge(ch.sem, ch.count())
            for d in range(2):
                dve.scalar_tensor_tensor(out=mv.kd[d], in0=mv.kk_a[d], scalar=-1.0, in1=key, op0=ALU.add, op1=ALU.mult).then_inc(ch.sem, ch.up())
                dve.wait_ge(ch.sem, ch.count())
                dve.tensor_tensor(t3(mv.kd[d]), t3(mv.kd[d]), k_, ALU.add)
                x = dve.tensor_tensor(mv.kk_a[d], mv.kk_a[d], mv.kk, ALU.mult)
            x.then_inc(ch.sem, ch.up())
            dve.wait_ge(ch.sem, ch.count())
    for s in (small_in, lora_s, mm, add, sg):
        s.close()

    recurrence(core, v, "rwkv")

    lo, hi = Region(core, A_WORK, A_END), Region(core, A_HT, A_PT)
    g_up, sig_g = lo(W), lo(T)
    r_k, gn_w, gn_b = lo(W), lo(W), lo(W)
    mu, ss, bon = lo(NT * NH), lo(NT * NH), lo(NT * NH)
    y, tmp, bonus = hi(NT * W), hi(NT * W), hi(NT * W)
    out = v.mix[:, :, 768:1024]
    small_in = core.steps("rwkv_norm_in", ["all"], 16 * 4)
    act_s = core.steps("scalar_steps", ["sigmoid", "root"])
    dve_s = core.steps("vector_steps", ["mean"])
    g_mm = core.steps("lora_up", [f"g{t}" for t in range(NT)])
    g_ev = core.steps("lora_biased", [f"g{t}" for t in range(NT)])

    def groups(ap):
        return ap.rearrange("p (g n) -> p g n", n=HD)

    def per_group(ap):
        return ap.unsqueeze(2).broadcast_to([P, NT * NH, HD])

    def over_tiles(ap):
        return ap.unsqueeze(1).broadcast_to([P, NT, W])

    def r_v(t):
        return v.pt[:, t, RKV0 + 2 * W:RKV0 + 3 * W].rearrange("p (h n) -> p h n", h=NH)

    with nc.Block() as block:
        @block.sync
        def _(sp):
            for dst, src in ((g_up[64:128, :], io["rwkv_g_up"][i]), (r_k, row("rwkv_r_k").partition_broadcast(P)),
                             (gn_w, row("rwkv_gn_w").partition_broadcast(P)), (gn_b, row("rwkv_gn_b").partition_broadcast(P))):
                sp.dma_start(dst, src).then_inc(small_in.sem, 16)

        @block.tensor
        def _(pe):
            pe.wait_ge(small_in.sem, small_in.count("all"))
            pe.wait_ge(act_s.sem, act_s.count("sigmoid"))
            for t in range(NT):
                if t >= 2:
                    pe.wait_ge(g_ev.sem, g_ev.count(f"g{t - 2}"))
                pe.matmul(core.bank[t % 2][:, 0:W], sig_g[64:128, t * P:(t + 1) * P], g_up[64:128, :], start=True, stop=True).then_inc(g_mm.sem, g_mm.step(f"g{t}"))

        @block.scalar
        def _(act):
            act.activation(sig_g[64:128, :], lora[64:128, :], ACT.Sigmoid).then_inc(act_s.sem, act_s.step("sigmoid"))
            act.wait_ge(dve_s.sem, dve_s.count("mean"))
            act.activation(ss, ss, ACT.Sqrt).then_inc(act_s.sem, act_s.step("root"))

        @block.vector
        def _(dve):
            ch = core.vchain
            dve.wait_ge(small_in.sem, small_in.count("all"))
            dve.tensor_tensor(t3(y), v.pt[:, :, V0:V0 + W], v.pt[:, :, V0 + W:V0 + 2 * W], ALU.add)
            dve.tensor_tensor(tmp, mv.kd[0], mv.kd[1], ALU.add).then_inc(ch.sem, ch.up())
            dve.wait_ge(ch.sem, ch.count())
            dve.tensor_reduce(mu, groups(y), AX.X, ALU.add).then_inc(ch.sem, ch.up())
            dve.wait_ge(ch.sem, ch.count())
            dve.tensor_tensor(t3(tmp), t3(tmp), r_, ALU.mult).then_inc(ch.sem, ch.up())
            dve.wait_ge(ch.sem, ch.count())
            dve.tensor_scalar(mu, mu, 1.0 / HD, None, ALU.mult)
            dve.tensor_tensor(t3(tmp), t3(tmp), over_tiles(r_k), ALU.mult).then_inc(ch.sem, ch.up())
            dve.wait_ge(ch.sem, ch.count())
            dve.tensor_reduce(bon, groups(tmp), AX.X, ALU.add).then_inc(ch.sem, ch.up())
            dve.wait_ge(ch.sem, ch.count())
            dve.tensor_tensor(groups(y), groups(y), per_group(mu), ALU.subtract).then_inc(ch.sem, ch.up())
            dve.wait_ge(ch.sem, ch.count())
            dve.tensor_tensor(tmp, y, y, ALU.mult).then_inc(ch.sem, ch.up())
            dve.wait_ge(ch.sem, ch.count())
            dve.tensor_reduce(ss, groups(tmp), AX.X, ALU.add).then_inc(ch.sem, ch.up())
            dve.wait_ge(ch.sem, ch.count())
            dve.tensor_scalar(ss, ss, 1.0 / HD, GN_EPS, ALU.mult, ALU.add).then_inc(dve_s.sem, dve_s.step("mean"))
            for t in range(NT):
                b = bonus[:, t * W:(t + 1) * W].rearrange("p (h n) -> p h n", h=NH)
                x = dve.tensor_tensor(b, r_v(t), bon[:, t * NH:(t + 1) * NH].unsqueeze(2).broadcast_to([P, NH, HD]), ALU.mult)
            x.then_inc(ch.sem, ch.up())
            dve.wait_ge(ch.sem, ch.count())
            dve.tensor_tensor(t3(bonus), t3(bonus), over_tiles(gn_b), ALU.add).then_inc(ch.sem, ch.up())
            dve.wait_ge(ch.sem, ch.count())
            dve.wait_ge(act_s.sem, act_s.count("root"))
            dve.reciprocal(ss, ss).then_inc(ch.sem, ch.up())
            dve.wait_ge(ch.sem, ch.count())
            dve.tensor_tensor(groups(y), groups(y), per_group(ss), ALU.mult).then_inc(ch.sem, ch.up())
            dve.wait_ge(ch.sem, ch.count())
            dve.tensor_tensor(t3(y), t3(y), over_tiles(gn_w), ALU.mult).then_inc(ch.sem, ch.up())
            dve.wait_ge(ch.sem, ch.count())
            dve.tensor_tensor(y, y, bonus, ALU.add).then_inc(ch.sem, ch.up())
            dve.wait_ge(ch.sem, ch.count())
            for t in range(NT):
                dve.wait_ge(g_mm.sem, g_mm.count(f"g{t}"))
                dve.tensor_tensor(v.mix[:, t, 768:1024], core.bank[t % 2][:, 0:W], y[:, t * W:(t + 1) * W], ALU.mult).then_inc(g_ev.sem, g_ev.step(f"g{t}"))
            dve.wait_ge(g_ev.sem, g_ev.count(f"g{NT - 1}"))

    for s in (small_in, act_s, dve_s, g_mm, g_ev):
        s.close()


def gate_rows(core, v, j, streams, region):
    rows = {c: region(D) for c in streams}
    col = region(KD, P)
    g_v = core.steps("gate_spread", [f"c{c}" for c in streams])
    g_mm = core.steps("gate_rows", [f"c{c}" for c in streams])
    g_ev = core.steps("gate_copied", [f"c{c}" for c in streams])

    def dve_part(dve):
        for n, c in enumerate(streams):
            if n:
                dve.wait_ge(g_mm.sem, g_mm.count(f"c{streams[n - 1]}"))
            for k in range(KD):
                x = dve.tensor_scalar(col[:, k, :], v.ones, v.gate[:, j, c, k:k + 1], None, ALU.mult)
            x.then_inc(g_v.sem, g_v.step(f"c{c}"))

    def pe_part(pe):
        for n, c in enumerate(streams):
            pe.wait_ge(g_v.sem, g_v.count(f"c{c}"))
            if n:
                pe.wait_ge(g_ev.sem, g_ev.count(f"c{streams[n - 1]}"))
            for k in range(KD):
                x = pe.matmul(core.wide[2][:, k * P:(k + 1) * P], col[:, k, :], v.ident, start=True, stop=True)
            x.then_inc(g_mm.sem, g_mm.step(f"c{c}"))

    def act_part(act):
        for c in streams:
            act.wait_ge(g_mm.sem, g_mm.count(f"c{c}"))
            act.copy(rows[c], core.wide[2][:, :]).then_inc(g_ev.sem, g_ev.step(f"c{c}"))

    def ready(eng):
        eng.wait_ge(g_ev.sem, g_ev.count(f"c{streams[-1]}"))

    def close():
        for s in (g_v, g_mm, g_ev):
            s.close()

    return rows, dve_part, pe_part, act_part, ready, close


def post_norm(core, v, tiles, rows, region):
    junk, tmp = [region(D) for _ in range(2)], [region(D) for _ in range(2)]
    n = len(tiles)
    y_mm = core.steps("y_product", [f"t{q}" for q in range(n)])
    y_a = core.steps("y_scalar", [f"{a}{q}" for q in range(n) for a in ("square", "root")])
    y_v = core.steps("y_vector", [f"{a}{q}" for q in range(n) for a in ("mean", "scaled")])
    done = core.steps("x_updated", ["all"])

    def act_part(act):
        for q, t in enumerate(tiles):
            act.wait_ge(y_mm.sem, y_mm.count(f"t{q}"))
            if q >= 2:
                act.wait_ge(y_a.sem, y_a.count(f"square{q - 2}"))
            act.activation(junk[q % 2], core.wide[q % 3][:, :], ACT.Square, accum_out=v.stat[:, t:t + 1]).then_inc(y_a.sem, y_a.step(f"square{q}"))
            act.wait_ge(y_v.sem, y_v.count(f"mean{q}"))
            act.activation(v.std[:, t:t + 1], v.stat[:, t:t + 1], ACT.Sqrt).then_inc(y_a.sem, y_a.step(f"root{q}"))

    def dve_part(dve):
        ch = core.vchain
        for q, t in enumerate(tiles):
            dve.wait_ge(y_a.sem, y_a.count(f"square{q}"))
            dve.tensor_scalar(v.stat[:, t:t + 1], v.stat[:, t:t + 1], 1.0 / D, EPS, ALU.mult, ALU.add).then_inc(y_v.sem, y_v.step(f"mean{q}"))
            dve.wait_ge(y_a.sem, y_a.count(f"root{q}"))
            dve.reciprocal(v.rstd[:, t:t + 1], v.std[:, t:t + 1]).then_inc(ch.sem, ch.up())
            dve.wait_ge(ch.sem, ch.count())
            dve.scalar_tensor_tensor(out=tmp[q % 2], in0=core.wide[q % 3][:, :], scalar=v.rstd[:, t:t + 1],
                                              in1=rows[stream(t)], op0=ALU.mult, op1=ALU.mult).then_inc(y_v.sem, y_v.step(f"scaled{q}"))
            dve.wait_ge(y_v.sem, y_v.count(f"scaled{q}"))
            x = dve.tensor_tensor(v.x[:, t, :], v.x[:, t, :], tmp[q % 2], ALU.add)
            if q < n - 1:
                x.then_inc(ch.sem, ch.up())
                dve.wait_ge(ch.sem, ch.count())
        x.then_inc(done.sem, done.step("all"))
        dve.wait_ge(done.sem, done.count("all"))

    def before_product(pe, q):
        if q >= 3:
            pe.wait_ge(y_v.sem, y_v.count(f"scaled{q - 3}"))

    def close():
        for s in (y_mm, y_a, y_v, done):
            s.close()

    return y_mm, act_part, dve_part, before_product, close


def merge(core, v, io, i, last):
    nc = core.nc
    tiles = list(range(CT, NT)) if last else list(range(NT))
    n = len(tiles)
    r = Region(core, A_PT, A_MIX)
    w = r(KD, D)
    rows, dve_g, pe_g, act_g, g_ready, g_close = gate_rows(core, v, 0, [0] if last else [0, 1], r)
    y_mm, act_y, dve_y, before_product, y_close = post_norm(core, v, tiles, rows, r)
    w_in = core.steps("slot_in0", ["w"], 16)
    tr = core.steps("norm_transposed", [f"t{q}" for q in range(n)])
    eva = core.steps("norm_evac_scalar", [f"t{q}" for q in range(n)])
    evv = core.steps("norm_evac_vector", [f"t{q}" for q in range(n)])
    H = KD // 2
    with nc.Block() as block:
        @block.sync
        def _(sp):
            sp.dma_start(w, io["w_out"][i].rearrange("(k p) n -> p k n", p=P)).then_inc(w_in.sem, w_in.step("w"))

        @block.tensor
        def _(pe):
            pe_g(pe)
            for q, t in enumerate(tiles):
                if q >= 2:
                    pe.wait_ge(eva.sem, eva.count(f"t{q - 2}"))
                    pe.wait_ge(evv.sem, evv.count(f"t{q - 2}"))
                for k in range(KD):
                    x = pe.transpose(core.wide[q % 2][:, k * P:(k + 1) * P], v.mix[:, t, k * P:(k + 1) * P], v.ident)
                x.then_inc(tr.sem, tr.step(f"t{q}"))
            pe.wait_ge(eva.sem, eva.count(f"t{n - 1}"))
            pe.wait_ge(evv.sem, evv.count(f"t{n - 1}"))
            g_ready(pe)
            pe.wait_ge(w_in.sem, w_in.count("w"))
            for q, t in enumerate(tiles):
                before_product(pe, q)
                for half in range(2):
                    for k in range(KD):
                        x = pe.matmul(core.wide[q % 3][:, half * 512:(half + 1) * 512], v.ht[:, k, t * P:(t + 1) * P],
                                      w[:, k, half * 512:(half + 1) * 512], start=(k == 0), stop=(k == KD - 1))
                x.then_inc(y_mm.sem, y_mm.step(f"t{q}"))

        def copied(eng_copy, q, odd):
            t = tiles[q]
            return eng_copy(v.ht[:, H * odd:H * odd + H, t * P:(t + 1) * P],
                            core.wide[q % 2][:, 512 * odd:512 * odd + 512].rearrange("p (k n) -> p k n", n=P))

        @block.scalar
        def _(act):
            act_g(act)
            for q in range(n):
                act.wait_ge(tr.sem, tr.count(f"t{q}"))
                copied(act.copy, q, 1).then_inc(eva.sem, eva.step(f"t{q}"))
            act_y(act)

        @block.vector
        def _(dve):
            dve_g(dve)
            for q in range(n):
                dve.wait_ge(tr.sem, tr.count(f"t{q}"))
                copied(dve.tensor_copy, q, 0).then_inc(evv.sem, evv.step(f"t{q}"))
            g_ready(dve)
            dve_y(dve)
    for s in (w_in, tr, eva, evv):
        s.close()
    g_close()
    y_close()


class MoeViews:

    def __init__(self, core, v):
        self.rank_t = v.small[:, 0:NT * NE]
        r = Region(core, A_HT, A_END)
        self.out = r(12 * D)
        both = r(T)
        self.rank = both[0:NE, :]
        self.affinity = both[32:32 + NE, :]
        self.rest = r.at


def route(core, v, io, i, last):
    nc = core.nc
    mo = MoeViews(core, v)
    tiles = list(range(CT, NT)) if last else list(range(NT))
    n, lo = len(tiles), tiles[0]
    act_n, dve_n, pe_n, ready, close = normed_transposed(core, v, 1, tiles, mo.rest, (h_t := core.view(mo.rest + 3 * D, KD, T)))
    r = Region(core, mo.rest + 3 * D + KD * T, A_END)
    router = r(KD, NE)
    aff = r(NT * NE)
    work, taken, ones = r(T), r(T), r(T)
    mx, sm = r(NT), r(NT)
    best = r(8)
    w_in = core.steps("slot_in0", ["w"], 16)
    pe_s = core.steps("tensor_steps", ["logits", "aff_t", "rank_t"])
    act_s = core.steps("scalar_steps", ["exp", "aff_t"])
    dve_s = core.steps("vector_steps", ["shifted", "aff", "rank"])
    segs = ([] if last else [(0, CT * P, SLOT_C)]) + [(CT * P, T, SLOT_L)]
    cols = slice(lo * NE, NT * NE)

    def t3(ap):
        return ap[:, cols].rearrange("p (t e) -> p t e", e=NE)

    with nc.Block() as block:
        @block.sync
        def _(sp):
            sp.dma_start(router, io["moe_router"][i].rearrange("(k p) e -> p k e", p=P)).then_inc(w_in.sem, w_in.step("w"))

        @block.tensor
        def _(pe):
            pe_n(pe)
            ready(pe)
            pe.wait_ge(w_in.sem, w_in.count("w"))
            for t in tiles:
                for k in range(KD):
                    x = pe.matmul(core.bank[0][:, t * NE:(t + 1) * NE], h_t[:, k, t * P:(t + 1) * P], router[:, k, :],
                                  start=(k == 0), stop=(k == KD - 1))
            x.then_inc(pe_s.sem, pe_s.step("logits"))
            pe.wait_ge(dve_s.sem, dve_s.count("aff"))
            for t in tiles:
                x = pe.transpose(core.wide[2][0:NE, t * P:(t + 1) * P], aff[:, t * NE:(t + 1) * NE], v.ident)
            x.then_inc(pe_s.sem, pe_s.step("aff_t"))
            pe.wait_ge(dve_s.sem, dve_s.count("rank"))
            for t in tiles:
                x = pe.transpose(core.bank[1][:, t * NE:(t + 1) * NE], mo.rank[:, t * P:(t + 1) * P], v.ident[0:NE, 0:NE])
            x.then_inc(pe_s.sem, pe_s.step("rank_t"))

        @block.scalar
        def _(act):
            act_n(act)
            act.wait_ge(dve_s.sem, dve_s.count("shifted"))
            act.activation(aff[:, cols], aff[:, cols], ACT.Exp).then_inc(act_s.sem, act_s.step("exp"))
            act.wait_ge(pe_s.sem, pe_s.count("aff_t"))
            act.copy(work[0:NE, lo * P:T], core.wide[2][0:NE, lo * P:T]).then_inc(act_s.sem, act_s.step("aff_t"))
            act.copy(mo.affinity[:, lo * P:T], core.wide[2][0:NE, lo * P:T])

        @block.vector
        def _(dve):
            ch = core.vchain
            dve_n(dve)
            dve.memset(ones[0:NE, :], 1.0)
            dve.wait_ge(pe_s.sem, pe_s.count("logits"))
            dve.tensor_reduce(mx[:, lo:], t3(core.bank[0]), AX.X, ALU.max).then_inc(ch.sem, ch.up())
            dve.wait_ge(ch.sem, ch.count())
            dve.tensor_tensor(t3(aff), t3(core.bank[0]), mx[:, lo:].unsqueeze(2).broadcast_to([P, n, NE]), ALU.subtract).then_inc(dve_s.sem, dve_s.step("shifted"))
            dve.wait_ge(act_s.sem, act_s.count("exp"))
            dve.tensor_reduce(sm[:, lo:], t3(aff), AX.X, ALU.add).then_inc(ch.sem, ch.up())
            dve.wait_ge(ch.sem, ch.count())
            dve.reciprocal(sm[:, lo:], sm[:, lo:]).then_inc(ch.sem, ch.up())
            dve.wait_ge(ch.sem, ch.count())
            dve.tensor_tensor(t3(aff), t3(aff), sm[:, lo:].unsqueeze(2).broadcast_to([P, n, NE]), ALU.mult).then_inc(dve_s.sem, dve_s.step("aff"))
            dve.wait_ge(act_s.sem, act_s.count("aff_t"))
            for a, b, cap in segs:
                for _ in range(cap // 8):
                    dve.max(best[0:NE, :], work[0:NE, a:b]).then_inc(ch.sem, ch.up())
                    dve.wait_ge(ch.sem, ch.count())
                    dve.match_replace(out=work[0:NE, a:b], in_to_replace=best[0:NE, :], in_values=work[0:NE, a:b], imm_value=-1.0).then_inc(ch.sem, ch.up())
                    dve.wait_ge(ch.sem, ch.count())
            dve.tensor_scalar(taken[0:NE, lo * P:T], work[0:NE, lo * P:T], 0.0, None, ALU.is_lt).then_inc(ch.sem, ch.up())
            dve.wait_ge(ch.sem, ch.count())
            for a, b, cap in segs:
                x = dve.tensor_tensor_scan(work[0:NE, a:b], ones[0:NE, a:b], taken[0:NE, a:b], 0.0, ALU.mult, ALU.add)
            x.then_inc(ch.sem, ch.up())
            dve.wait_ge(ch.sem, ch.count())
            dve.tensor_tensor(mo.rank[:, lo * P:T], work[0:NE, lo * P:T], taken[0:NE, lo * P:T], ALU.mult).then_inc(dve_s.sem, dve_s.step("rank"))
            dve.wait_ge(pe_s.sem, pe_s.count("rank_t"))
            dve.tensor_copy(mo.rank_t[:, cols], core.bank[1][:, cols]).then_inc(ch.sem, ch.up())
            dve.wait_ge(ch.sem, ch.count())
    close()
    for s in (w_in, pe_s, act_s, dve_s):
        s.close()


def experts(core, v, io, i, last):
    nc = core.nc
    mo = MoeViews(core, v)
    tiles = list(range(CT, NT)) if last else list(range(NT))
    r = Region(core, mo.rest, A_END)
    wg, wu, wd = (r(KD, D) for _ in range(3))
    G = 4
    NG = NE // G
    HALF, QUARTER = D // 2, D // 4

    class Part:

        def __init__(self, c, t0, t1, slots, take):
            self.c, self.t0, self.t1, self.slots, self.parts, self.take = c, t0, t1, slots, P // slots, take
            self.width = D // self.parts
            self.x, self.hid = r(self.width), r(self.width)
            self.xt = r(KD, slots)
            self.hidt = r(KD, slots) if c == 0 else self.x.rearrange("p (k s) -> p k s", s=slots)
            at = 0 if c == 0 else 512
            self.gate, self.up, self.down = (w[:, at:at + self.width] for w in core.wide)
            self.gathered = core.bank[c][:, 0:self.width]

        def turned(self, bank):
            return bank.rearrange("p (m j s) -> p j m s", j=self.parts, s=self.slots)

        def tiled(self, ap):
            return ap.rearrange("p (j m) s -> p j m s", j=self.parts)

        def spread(self, ap):
            return ap.rearrange("p (j m) -> p j m", j=self.parts).unsqueeze(3).broadcast_to([P, self.parts, KD // self.parts, self.slots])

        def product(self, pe, out, tokens, weights, first, final):
            for j in range(self.parts):
                x = pe.matmul(out[j * self.slots:(j + 1) * self.slots, :], tokens, weights[:, j * self.width:(j + 1) * self.width],
                              start=first, stop=final)
            return x

        def transposes(self, pe, out, src):
            for m in range(self.width // P):
                x = pe.transpose(out[:, m * P:(m + 1) * P], src[:, m * P:(m + 1) * P], v.ident)
            return x

    lat = Part(0, CT, NT, SLOT_L, v.small[:, NT * NE:NT * NE + LT * SLOT_L].rearrange("p (t s) -> p t s", s=SLOT_L))
    at = NT * NE + LT * SLOT_L
    streams = [lat] if last else [lat, Part(1, 0, CT, SLOT_C, v.small[:, at:at + CT * SLOT_C].rearrange("p (t s) -> p t s", s=SLOT_C))]
    gate_in, up_in, down_in = (core.steps(f"expert_{a}_in", ["w"], 16) for a in ("gate", "up", "down"))
    g_mm, u_mm, d_mm, x_mm = (core.steps(f"expert_{a}", ["e"]) for a in ("gate", "up", "down", "gathered"))
    hid_t, x_t = core.steps("expert_hidden_turned", ["e"]), core.steps("expert_tokens_turned", ["e"])
    sel, mod, silu, hd, kept = (core.steps(f"expert_{a}", ["e"]) for a in ("selected", "modulated", "silu", "hidden", "kept"))
    x_out, lat_out, ctx_out = (core.steps(f"expert_{a}", ["e"]) for a in ("tokens_copied", "latents_hidden_copied", "context_hidden_copied"))

    def w_of(name, e):
        return io[name][i].rearrange("e (k p) n -> e p k n", p=P)[ds(e, 1)].rearrange("e p k n -> p (e k) n")

    def n_done(s, e):
        return e * s.by + (s.base + s.by)

    def passes(eng, body):
        with eng.Fori(0, NG - 1) as g:
            for e in range(G):
                body(g * G + e, e, True)
        for e in range(G):
            body((NG - 1) * G + e, e, e < G - 1)

    with nc.Block() as block:
        @block.sync
        def _(sp):
            def body(e, _, more):
                sp.wait_ge(g_mm.sem, n_done(g_mm, e - 1))
                sp.dma_start(wg, w_of("moe_w_gate", e)).then_inc(gate_in.sem, 16)
                sp.wait_ge(u_mm.sem, n_done(u_mm, e - 1))
                sp.dma_start(wu, w_of("moe_w_up", e)).then_inc(up_in.sem, 16)
                sp.wait_ge(d_mm.sem, n_done(d_mm, e - 1))
                sp.dma_start(wd, w_of("moe_w_down", e)).then_inc(down_in.sem, 16)

            passes(sp, body)

        @block.tensor
        def _(pe):
            def gather(e):
                pe.wait_ge(sel.sem, n_done(sel, e))
                for s in streams:
                    for t in range(s.t0, s.t1):
                        x = s.product(pe, s.gathered, s.take[:, t - s.t0, :], v.x[:, t, :], t == s.t0, t == s.t1 - 1)
                x.then_inc(x_mm.sem, 1)

            def turn_tokens(e):
                pe.wait_ge(x_out.sem, n_done(x_out, e))
                for s in streams:
                    x = s.transposes(pe, s.gathered, s.x)
                x.then_inc(x_t.sem, 1)

            def body(e, _, more):
                pe.wait_ge(gate_in.sem, n_done(gate_in, e))
                pe.wait_ge(mod.sem, n_done(mod, e))
                for s in streams:
                    for k in range(KD):
                        x = s.product(pe, s.gate, s.xt[:, k, :], wg[:, k, :], k == 0, k == KD - 1)
                x.then_inc(g_mm.sem, 1)
                pe.wait_ge(up_in.sem, n_done(up_in, e))
                for s in streams:
                    for k in range(KD):
                        x = s.product(pe, s.up, s.xt[:, k, :], wu[:, k, :], k == 0, k == KD - 1)
                x.then_inc(u_mm.sem, 1)
                if more:
                    gather(e + 1)
                pe.wait_ge(hd.sem, n_done(hd, e))
                for s in streams:
                    x = s.transposes(pe, s.gate, s.hid)
                x.then_inc(hid_t.sem, 1)
                if more:
                    turn_tokens(e + 1)
                pe.wait_ge(down_in.sem, n_done(down_in, e))
                pe.wait_ge(kept.sem, n_done(kept, e - 1))
                pe.wait_ge(lat_out.sem, n_done(lat_out, e))
                for s in streams:
                    if s.c:
                        pe.wait_ge(ctx_out.sem, n_done(ctx_out, e))
                    for k in range(KD):
                        x = s.product(pe, s.down, s.hidt[:, k, :], wd[:, k, :], k == 0, k == KD - 1)
                x.then_inc(d_mm.sem, 1)

            gather(0)
            turn_tokens(0)
            passes(pe, body)

        @block.scalar
        def _(act):
            def copy_tokens(e):
                act.wait_ge(x_mm.sem, n_done(x_mm, e))
                for s in streams:
                    x = act.copy(s.x, s.gathered)
                x.then_inc(x_out.sem, 1)

            def body(e, place, more):
                act.wait_ge(g_mm.sem, n_done(g_mm, e))
                for s in streams:
                    x = act.activation(s.hid, s.gate, ACT.Silu)
                x.then_inc(silu.sem, 1)
                if more:
                    copy_tokens(e + 1)
                act.wait_ge(hid_t.sem, n_done(hid_t, e))
                act.copy(lat.tiled(lat.hidt), lat.turned(lat.gate)).then_inc(lat_out.sem, 1)
                act.wait_ge(d_mm.sem, n_done(d_mm, e))
                first = (e - place) * (D // G)
                for s in streams:
                    p0, c0 = (SLOT_L * (place % 2), first * 2 + place // 2 * D) if s.c == 0 else (SLOT_C * place, first + 8 * D)
                    for j in range(s.parts):
                        x = act.copy(mo.out[p0:p0 + s.slots, ds(c0 + j * s.width, s.width)], s.down[j * s.slots:(j + 1) * s.slots, :])
                x.then_inc(kept.sem, 1)

            copy_tokens(0)
            passes(act, body)

        @block.vector
        def _(dve):
            ch = core.vchain

            def select(e):
                dve.wait_ge(x_mm.sem, n_done(x_mm, e - 1))
                for s in streams:
                    for t in range(s.t0, s.t1):
                        x = dve.tensor_scalar(s.take[:, t - s.t0, :], v.const[:, IOTA:IOTA + s.slots], mo.rank_t[:, ds(e + t * NE, 1)],
                                              v.rstd[:, t:t + 1], ALU.is_equal, ALU.mult)
                x.then_inc(sel.sem, 1)

            def modulate(e):
                dve.wait_ge(x_t.sem, n_done(x_t, e))
                for s in streams:
                    x = dve.tensor_tensor(s.tiled(s.xt), s.turned(s.gathered), s.spread(v.scale[:, 1, s.c, :]), ALU.mult)
                x.then_inc(ch.sem, ch.up())
                dve.wait_ge(ch.sem, ch.count())
                for s in streams:
                    x = dve.tensor_tensor(s.xt, s.xt, v.mod[:, 24:32, s.c].unsqueeze(2).broadcast_to([P, KD, s.slots]), ALU.add)
                x.then_inc(mod.sem, 1)

            def body(e, place, more):
                if more:
                    select(e + 1)
                dve.wait_ge(silu.sem, n_done(silu, e))
                dve.wait_ge(u_mm.sem, n_done(u_mm, e))
                for s in streams:
                    x = dve.tensor_tensor(s.hid, s.hid, s.up, ALU.mult)
                x.then_inc(hd.sem, 1)
                if not last:
                    dve.wait_ge(hid_t.sem, n_done(hid_t, e))
                    if more:
                        dve.wait_ge(x_t.sem, n_done(x_t, e + 1))
                    dve.tensor_copy(streams[1].tiled(streams[1].hidt), streams[1].turned(streams[1].gate)).then_inc(ctx_out.sem, 1)
                if more:
                    modulate(e + 1)

            select(0)
            modulate(0)
            with ch.loop(dve, NG - 1, G) as g:
                for e in range(G):
                    body(g * G + e, e, True)
            for e in range(G):
                body((NG - 1) * G + e, e, e < G - 1)
    for s in (g_mm, u_mm, d_mm, x_mm, hid_t, x_t, sel, mod, silu, hd, kept, x_out, lat_out, gate_in, up_in, down_in):
        s.close(NE)
    ctx_out.close(0 if last else NE)


def combine(core, v, io, i, last):
    nc = core.nc
    mo = MoeViews(core, v)
    tiles = list(range(CT, NT)) if last else list(range(NT))
    r = Region(core, mo.rest, A_END)
    put = {q: r(LT * P if q < 8 else CT * P) for q in range(8 if last else 12)}
    rows, dve_g, pe_g, act_g, g_ready, g_close = gate_rows(core, v, 1, [0] if last else [0, 1], r)
    y_mm, act_y, dve_y, before_product, y_close = post_norm(core, v, tiles, rows, r)
    affinity, spread = r(T), [r(LT * P) for _ in range(2)]
    sp_mm = core.steps("rank_spread", [f"q{q}" for q in put])
    moved = core.steps("affinity_moved", ["all"])
    sp_out = core.steps("affinity_spread_copied", [f"q{q}" for q in put])
    eq = core.steps("slots_matched", [f"q{q}" for q in put])

    def span(q):
        return (CT * P, T) if q < 8 else (0, CT * P)

    with nc.Block() as block:
        @block.tensor
        def _(pe):
            pe_g(pe)
            pe.wait_ge(moved.sem, moved.count("all"))
            for q in put:
                a, b = span(q)
                if q >= 2:
                    pe.wait_ge(eq.sem, eq.count(f"q{q - 2}"))
                pe.matmul(core.wide[q % 2][:, 0:b - a], v.const[0:NE, SELW + q * P:SELW + (q + 1) * P], affinity[0:NE, a:b], start=True, stop=True)
                pe.matmul(core.bank[q % 2][:, 0:b - a], v.const[0:NE, SELW + q * P:SELW + (q + 1) * P], mo.rank[:, a:b],
                                     start=True, stop=True).then_inc(sp_mm.sem, sp_mm.step(f"q{q}"))
            pe.wait_ge(eq.sem, eq.count(f"q{max(put)}"))
            g_ready(pe)
            for n, t in enumerate(tiles):
                before_product(pe, n)
                qs = range(8) if t >= CT else range(8, 12)
                c = (t - CT if t >= CT else t) * P
                for half in range(2):
                    for q in qs:
                        x = pe.matmul(core.wide[n % 3][:, half * 512:(half + 1) * 512], put[q][:, c:c + P],
                                      mo.out[:, q * D + half * 512:q * D + half * 512 + 512], start=(q == qs[0]), stop=(q == qs[-1]))
                x.then_inc(y_mm.sem, y_mm.step(f"t{n}"))

        @block.scalar
        def _(act):
            lo = tiles[0] * P
            act.copy(affinity[0:NE, lo:T], mo.affinity[:, lo:T]).then_inc(moved.sem, moved.step("all"))
            act_g(act)
            for q in put:
                a, b = span(q)
                act.wait_ge(sp_mm.sem, sp_mm.count(f"q{q}"))
                if q >= 2:
                    act.wait_ge(eq.sem, eq.count(f"q{q - 2}"))
                act.copy(spread[q % 2][:, 0:b - a], core.wide[q % 2][:, 0:b - a]).then_inc(sp_out.sem, sp_out.step(f"q{q}"))
            act_y(act)

        @block.vector
        def _(dve):
            dve_g(dve)
            for q in put:
                a, b = span(q)
                col = COLS + (2 if q < 8 else 3)
                dve.wait_ge(sp_out.sem, sp_out.count(f"q{q}"))
                dve.scalar_tensor_tensor(out=put[q], in0=core.bank[q % 2][:, 0:b - a], scalar=v.const[:, col:col + 1], in1=spread[q % 2][:, 0:b - a],
                                         op0=ALU.is_equal, op1=ALU.mult).then_inc(eq.sem, eq.step(f"q{q}"))
            g_ready(dve)
            dve_y(dve)
    for s in (sp_mm, eq, moved, sp_out):
        s.close()
    g_close()
    y_close()


def store_result(core, v, out):
    stored = core.steps("stored", ["all"], 16)
    with core.nc.Block() as block:
        @block.sync
        def _(sp):
            sp.dma_start(out.rearrange("(t p) d -> p t d", p=P), v.x[:, CT:NT, :]).then_inc(stored.sem, stored.step("all"))
            sp.wait_ge(stored.sem, stored.count("all"))


def trunk(nc, io, out, stop=None):
    with ExitStack() as ctx:
        core = Core(nc, ctx)
        v = Views(core)
        load_start(core, v, io)
        for i in range(DEPTH):
            last = i == DEPTH - 1
            for name, part in PHASES:
                part(core, v, io, i, last) if part in WITH_LAST else part(core, v, io, i)
                if stop == (i, name):
                    return
        store_result(core, v, out)


PHASES = [("mod", modulation), ("proj", projections), ("att", attention), ("gdn", gdn), ("rwkv", rwkv),
          ("merge", merge), ("route", route), ("experts", experts), ("moe", combine)]
WITH_LAST = (attention, merge, route, experts, combine)


def constants():
    import numpy as np

    c = np.zeros((P, NCONST2), np.float32)
    p, f = np.arange(P)[:, None], np.arange(P)[None, :]
    c[:, IDENT:IDENT + P] = p == f
    c[:, UPS:UPS + P] = f > p
    c[:, UPI:UPI + P] = f >= p
    c[:, LOS:LOS + P] = f < p
    c[:, LOI:LOI + P] = f <= p
    first, second = (p < HD).astype(np.float32), (p >= HD).astype(np.float32)
    c[:, CUI:CUI + P] = (f >= p) - first
    c[:, CUS:CUS + P] = (f > p) - first
    c[:, CLI:CLI + P] = (f <= p) - second
    c[:, CLS:CLS + P] = (f < p) - second
    low = f % 32 < 16
    c[:, ROT:ROT + P] = np.where(low, -1.0 * (p == f + 16), 1.0 * (p == f - 16))
    c[:, ONES:ONES + P] = 1.0
    c[:, COLS:COLS + 1] = first
    c[:, COLS + 1:COLS + 2] = second
    c[:, COLS + 2:COLS + 3] = p % SLOT_L + 1
    c[:, COLS + 3:COLS + 4] = p % SLOT_C + 1
    c[:, IOTA:IOTA + 64] = np.arange(64)[None, :] + 1
    tok = np.arange(512)
    freqs = (np.float32(10000.0) ** (-np.arange(16, dtype=np.float32) / np.float32(16))).astype(np.float32)
    dim = np.arange(P) % HD
    pos = np.where((dim // 32)[:, None] == 0, (tok // 64)[None, :], (tok % 64)[None, :]).astype(np.float32)
    ang = pos * freqs[dim % 16][:, None]
    c[:, COS:COS + 512] = np.cos(ang)
    c[:, SIN:SIN + 512] = np.sin(ang)
    same = p // 32 == f // 32
    c[:, DLO:DLO + P], c[:, DUP:DUP + P] = (f < p) & same, (f > p) & same
    c[:, OLO:OLO + P], c[:, OUP:OUP + P] = (f < p) & ~same, (f > p) & ~same
    for t in range(8):
        c[:NE, SELW + t * P:SELW + (t + 1) * P] = np.arange(NE)[:, None] == 2 * t + np.arange(P)[None, :] // SLOT_L
    for t in range(4):
        c[:NE, SELW + (8 + t) * P:SELW + (9 + t) * P] = np.arange(NE)[:, None] == 4 * t + np.arange(P)[None, :] // SLOT_C
    return c


_PLAIN = ["c", "c_ctx", "w_mod", "b_mod", "norm_pre", "norm_post", "w_out", "da_lambda", "da_norm", "gdn_conv",
          "gdn_a_log", "gdn_dt_bias", "gdn_norm", "rwkv_w0", "rwkv_w_up", "rwkv_a0", "rwkv_a_up", "rwkv_g_up",
          "rwkv_k_k", "rwkv_k_a", "rwkv_r_k", "rwkv_gn_w", "rwkv_gn_b", "moe_router", "moe_w_gate", "moe_w_up",
          "moe_w_down"]


def layouts(inputs):
    import numpy as np

    a = {n: np.ascontiguousarray(inputs[n]) for n in _PLAIN}
    a["x"] = np.ascontiguousarray(inputs["x"])[0]
    a["ctx"] = np.ascontiguousarray(inputs["ctx"])[0]
    w = np.ascontiguousarray(inputs["w_in"])
    fm = np.concatenate([w[..., 0:1024], w[..., 1536:2304], w[..., 3344:3472]], -1)
    tm = np.concatenate([w[..., 1024:1536], w[..., 2304:2576], w[..., 2576:3344]], -1)

    def tiles(m, n):
        return np.ascontiguousarray(
            m.reshape(DEPTH, KD, P, m.shape[-1] // n, n).transpose(0, 2, 3, 1, 4).reshape(DEPTH, P, -1))

    a["w_fm"], a["w_tm"] = tiles(fm, P), tiles(tm, TMW)
    a["consts"] = constants()
    return a


def kernel(**inputs):
    import numpy as _np
    import concourse.bacc as _bacc
    from concourse import mybir as _mybir
    from concourse.bass_utils import run_bass_kernel_spmd as _run

    nc = _bacc.Bacc("TRN2", target_bir_lowering=False, num_devices=1)
    arrays = {f"in_{n}": a for n, a in layouts(inputs).items()}
    io = {n[3:]: nc.dram_tensor(n, a.shape, _mybir.dt.from_np(a.dtype), kind="ExternalInput").ap()
          for n, a in arrays.items()}
    out = nc.dram_tensor("out_0", (LT * P, D), _mybir.dt.float32, kind="ExternalOutput").ap()
    trunk(nc, io, out)
    r = _run(nc, [arrays], core_ids=[0])
    return _np.asarray(r.results[0]["out_0"]).reshape(1, LT * P, D)
```
